# Optimizing a Trainium2 kernel written in Bass

```python
import math
import jax, jax.numpy as jnp
from jax import lax
import numpy as np

D_MODEL = 1024
BATCH = 1
SEQ = 512
DEPTH = 1

CHUNK = 64
N_PREV_CHUNKS = 8
HEAD_DIM = 64
N_HEADS_A = 8
REL_CLIP = 128
N_HEADS_B = 8
N_KV_B = 2
N_IDX_HEADS = 8
IDX_DIM = 64
TOPK_MAX = 256
Q_BLOCK = 128
ROPE_THETA = 500000.0
ROT_DIM = HEAD_DIM // 4
D_FF = 2816
EPS = 1e-6

WIDTH_A = N_HEADS_A * HEAD_DIM
WIDTH_B = N_HEADS_B * HEAD_DIM
WIDTH_KV_B = N_KV_B * HEAD_DIM
SPLIT_SIZES = (WIDTH_A, WIDTH_A, WIDTH_A,
               WIDTH_B, WIDTH_KV_B, WIDTH_KV_B,
               N_IDX_HEADS * IDX_DIM, IDX_DIM,
               N_IDX_HEADS,
               D_MODEL, D_MODEL)
D_IN = sum(SPLIT_SIZES)


def _rmsnorm(x, g):
    xf = x.astype(jnp.float32)
    y = xf * lax.rsqrt(jnp.mean(xf * xf, axis=-1, keepdims=True) + EPS)
    return (y * g.astype(jnp.float32)).astype(x.dtype)

def _swiglu(x, w_in, w_out):
    gate, up = jnp.split(x @ w_in, 2, axis=-1)
    return (jax.nn.silu(gate) * up) @ w_out

def _rope_tables(seq):
    inv_freq = jnp.power(jnp.float32(ROPE_THETA), -jnp.arange(0, ROT_DIM, 2, dtype=jnp.float32) / ROT_DIM)
    ang = jnp.arange(seq, dtype=jnp.float32)[:, None] * inv_freq[None, :]
    return jnp.cos(ang)[:, None, :], jnp.sin(ang)[:, None, :]

def _partial_rope(t, cos, sin):
    tr = t[..., :ROT_DIM].astype(jnp.float32)
    t1, t2 = tr[..., :ROT_DIM // 2], tr[..., ROT_DIM // 2:]
    rot = jnp.concatenate([t1 * cos - t2 * sin, t2 * cos + t1 * sin], axis=-1)
    return jnp.concatenate([rot.astype(t.dtype), t[..., ROT_DIM:]], axis=-1)

def _mixer_a(q, k, v, rel_bias):
    B, S, H, Dh = q.shape
    nc = S // CHUNK
    band_len = (N_PREV_CHUNKS + 1) * CHUNK
    qc = q.reshape(B, nc, CHUNK, H, Dh)

    def band(t):
        tp = jnp.pad(t, ((0, 0), (N_PREV_CHUNKS * CHUNK, 0), (0, 0), (0, 0)))
        tp = tp.reshape(B, nc + N_PREV_CHUNKS, CHUNK, H, Dh)
        return jnp.concatenate([tp[:, j:j + nc] for j in range(N_PREV_CHUNKS + 1)], axis=2)

    kb, vb = band(k), band(v)
    s = jnp.einsum('bnqhd,bnkhd->bnhqk', qc, kb).astype(jnp.float32) * (Dh ** -0.5)
    qi = jnp.arange(CHUNK)
    kj = jnp.arange(band_len)
    dist = N_PREV_CHUNKS * CHUNK + qi[:, None] - kj[None, :]
    bias = rel_bias[:, jnp.clip(dist, -REL_CLIP, REL_CLIP) + REL_CLIP].astype(jnp.float32)
    key_pos = (jnp.arange(nc)[:, None] - N_PREV_CHUNKS) * CHUNK + kj[None, :]
    valid = (key_pos >= 0)[None, :, None, None, :]
    s = jnp.where(valid, s + bias[None, None], -jnp.inf)
    p = jax.nn.softmax(s, axis=-1).astype(vb.dtype)
    o = jnp.einsum('bnhqk,bnkhd->bnqhd', p, vb)
    return o.reshape(B, S, H * Dh)

def _to_blocks(a):
    B, S = a.shape[:2]
    return jnp.moveaxis(a.reshape((B, S // Q_BLOCK, Q_BLOCK) + a.shape[2:]), 1, 0)

def _mixer_b(q, k, v, q_idx, k_idx, w_idx):
    B, S, H, Dh = q.shape
    G = k.shape[2]
    R = H // G
    topk = min(TOPK_MAX, S // 4)
    nb = S // Q_BLOCK
    key_pos = jnp.arange(S)
    w_scaled = w_idx * (N_IDX_HEADS ** -0.5)

    def one_block(args):
        qb, qib, wb, pos_q = args
        sc = jnp.einsum('bqhd,bsd->bqhs', qib, k_idx).astype(jnp.float32) * (IDX_DIM ** -0.5)
        score = jnp.einsum('bqh,bqhs->bqs', wb.astype(jnp.float32), jax.nn.relu(sc))
        limit = (pos_q // CHUNK + 1) * CHUNK
        adm = key_pos[None, :] < limit[:, None]
        score = jnp.where(adm[None], score, -jnp.inf)
        _, idx = lax.top_k(score, topk)
        sel_ok = idx < limit[None, :, None]
        kg = jax.vmap(lambda t, i: t[i])(k, idx)
        vg = jax.vmap(lambda t, i: t[i])(v, idx)
        qg = qb.reshape(B, Q_BLOCK, G, R, Dh)
        s = jnp.einsum('bqgrd,bqkgd->bqgrk', qg, kg).astype(jnp.float32) * (Dh ** -0.5)
        s = jnp.where(sel_ok[:, :, None, None, :], s, -jnp.inf)
        p = jax.nn.softmax(s, axis=-1).astype(vg.dtype)
        o = jnp.einsum('bqgrk,bqkgd->bqgrd', p, vg)
        return o.reshape(B, Q_BLOCK, H * Dh)

    out = lax.map(one_block, (_to_blocks(q), _to_blocks(q_idx), _to_blocks(w_scaled),
                              key_pos.reshape(nb, Q_BLOCK)))
    return jnp.moveaxis(out, 0, 1).reshape(B, S, H * Dh)

def first_inputs(seed: int = 0) -> dict:
    key = jax.random.key(seed)
    ks = jax.random.split(key, 16)
    f32 = jnp.float32

    def w(k, shape, fan_in):
        return jax.random.normal(k, shape, f32) * (fan_in ** -0.5)

    def gain(k):
        return 1.0 + 0.02 * jax.random.normal(k, (DEPTH, D_MODEL), f32)

    return {
        'x': jax.random.normal(ks[0], (BATCH, SEQ, D_MODEL), f32),
        'n1_g': gain(ks[1]),
        'ffn1_w_in': w(ks[2], (DEPTH, D_MODEL, 2 * D_FF), D_MODEL),
        'ffn1_w_out': w(ks[3], (DEPTH, D_FF, D_MODEL), D_FF),
        'n2_g': gain(ks[4]),
        'w_in': w(ks[5], (DEPTH, D_MODEL, D_IN), D_MODEL),
        'rel_bias': 0.2 * jax.random.normal(ks[6], (DEPTH, N_HEADS_A, 2 * REL_CLIP + 1), f32),
        'w_branch_a': w(ks[7], (DEPTH, WIDTH_A, D_MODEL), WIDTH_A),
        'w_branch_b': w(ks[8], (DEPTH, WIDTH_B, D_MODEL), WIDTH_B),
        'w_out': w(ks[9], (DEPTH, D_MODEL, D_MODEL), D_MODEL),
        'n3_g': gain(ks[10]),
        'ffn2_w_in': w(ks[11], (DEPTH, D_MODEL, 2 * D_FF), D_MODEL),
        'ffn2_w_out': w(ks[12], (DEPTH, D_FF, D_MODEL), D_FF),
        'nf_g': 1.0 + 0.02 * jax.random.normal(ks[13], (D_MODEL,), f32),
    }

def first_block(x, n1_g, ffn1_w_in, ffn1_w_out, n2_g, w_in, rel_bias, w_branch_a, w_branch_b,
              w_out, n3_g, ffn2_w_in, ffn2_w_out, nf_g):
    B, S, _ = x.shape
    cos, sin = _rope_tables(S)
    split_points = list(np.cumsum(SPLIT_SIZES)[:-1])
    for l in range(DEPTH):
        x = x + 0.5 * _swiglu(_rmsnorm(x, n1_g[l]), ffn1_w_in[l], ffn1_w_out[l])
        h = _rmsnorm(x, n2_g[l])
        qa, ka, va, qb, kb, vb, qi, ki, wi, ga, gb = jnp.split(h @ w_in[l], split_points, axis=-1)
        qa = qa.reshape(B, S, N_HEADS_A, HEAD_DIM)
        ka = ka.reshape(B, S, N_HEADS_A, HEAD_DIM)
        va = va.reshape(B, S, N_HEADS_A, HEAD_DIM)
        qb = _partial_rope(qb.reshape(B, S, N_HEADS_B, HEAD_DIM), cos, sin)
        kb = _partial_rope(kb.reshape(B, S, N_KV_B, HEAD_DIM), cos, sin)
        vb = vb.reshape(B, S, N_KV_B, HEAD_DIM)
        qi = _partial_rope(qi.reshape(B, S, N_IDX_HEADS, IDX_DIM), cos, sin)
        ki = _partial_rope(ki.reshape(B, S, 1, IDX_DIM), cos, sin)[:, :, 0]
        o_a = _mixer_a(qa, ka, va, rel_bias[l])
        o_b = _mixer_b(qb, kb, vb, qi, ki, wi)
        merged = jax.nn.sigmoid(ga) * (o_a @ w_branch_a[l]) + jax.nn.sigmoid(gb) * (o_b @ w_branch_b[l])
        x = x + merged @ w_out[l]
        x = x + 0.5 * _swiglu(_rmsnorm(x, n3_g[l]), ffn2_w_in[l], ffn2_w_out[l])
    return _rmsnorm(x, nf_g)


N_MIXERS = 2
SB_HEADS = 16
SB_HEAD_DIM = D_MODEL // SB_HEADS
LRU_WIDTH = D_MODEL
LRU_BLOCKS = 16
LRU_BLOCK_W = LRU_WIDTH // LRU_BLOCKS
LRU_C = 8.0
CONV_W = 4
NORM_EPS = 1e-6


def rms_norm(x, gain):
    xf = x.astype(jnp.float32)
    y = xf * lax.rsqrt(jnp.mean(xf * xf, axis=-1, keepdims=True) + NORM_EPS)
    return (y * gain.astype(jnp.float32)).astype(x.dtype)

def swiglu(xn, w_in, w_out):
    gate, up = jnp.split(xn @ w_in, 2, axis=-1)
    return (jax.nn.silu(gate) * up) @ w_out

def stick_breaking_attention(xn, w_qkv, q_gain, k_gain, w_o):
    b, s, _ = xn.shape
    qkv = (xn @ w_qkv).reshape(b, s, 3, SB_HEADS, SB_HEAD_DIM)
    q = rms_norm(qkv[:, :, 0], q_gain).astype(jnp.float32).transpose(0, 2, 1, 3)
    k = rms_norm(qkv[:, :, 1], k_gain).astype(jnp.float32).transpose(0, 2, 1, 3)
    v = qkv[:, :, 2].astype(jnp.float32).transpose(0, 2, 1, 3)
    scale = 1.0 / math.sqrt(SB_HEAD_DIM)
    outs = []
    for blk in range(s // Q_BLOCK):
        lo = blk * Q_BLOCK
        hi = lo + Q_BLOCK
        z = jnp.einsum('bhqd,bhkd->bhqk', q[:, :, lo:hi], k[:, :, :hi]) * scale
        t_idx = lo + jnp.arange(Q_BLOCK)[:, None]
        s_idx = jnp.arange(hi)[None, :]
        mask = s_idx < t_idx
        log_beta = jax.nn.log_sigmoid(z)
        log_1m = jnp.where(mask, jax.nn.log_sigmoid(-z), 0.0)
        rev = lax.cumsum(log_1m, axis=3, reverse=True)
        rev_excl = jnp.concatenate([rev[..., 1:], jnp.zeros_like(rev[..., :1])], axis=-1)
        w = jnp.where(mask, jnp.exp(log_beta + rev_excl), 0.0)
        outs.append(jnp.einsum('bhqk,bhkd->bhqd', w, v[:, :, :hi]))
    o = jnp.concatenate(outs, axis=2)
    o = o.transpose(0, 2, 1, 3).reshape(b, s, SB_HEADS * SB_HEAD_DIM).astype(xn.dtype)
    return o @ w_o

def rglru_block(xn, w_in, conv_w, conv_b, w_r, b_r, w_i, b_i, lam, w_o):
    b, s, _ = xn.shape
    xb, yb = jnp.split(xn @ w_in, 2, axis=-1)
    y = jax.nn.gelu(yb, approximate=True)
    xpad = jnp.pad(xb, ((0, 0), (CONV_W - 1, 0), (0, 0)))
    xc = conv_b + sum(conv_w[j] * xpad[:, j:j + s] for j in range(CONV_W))
    xh = xc.reshape(b, s, LRU_BLOCKS, LRU_BLOCK_W)
    r = jax.nn.sigmoid(jnp.einsum('bsnc,ncd->bsnd', xh, w_r).reshape(b, s, LRU_WIDTH) + b_r)
    i = jax.nn.sigmoid(jnp.einsum('bsnc,ncd->bsnd', xh, w_i).reshape(b, s, LRU_WIDTH) + b_i)
    log_a = LRU_C * r.astype(jnp.float32) * jax.nn.log_sigmoid(lam.astype(jnp.float32))
    a = jnp.exp(log_a)
    mult = jnp.sqrt(-jnp.expm1(2.0 * log_a))
    u = mult * (i * xc).astype(jnp.float32)

    def combine(left, right):
        a_l, h_l = left
        a_r, h_r = right
        return a_l * a_r, a_r * h_l + h_r

    _, h = lax.associative_scan(combine, (a, u), axis=1)
    return (h.astype(xn.dtype) * y) @ w_o

def second_inputs(seed: int = 0) -> dict:
    key = jax.random.key(seed)
    keys = iter(jax.random.split(key, 40))

    def normal(shape, scale):
        return jax.random.normal(next(keys), shape, jnp.float32) * scale

    def gain(n):
        return 1.0 + normal((n,), 0.02)

    def lam_init(n):
        a_c = jax.random.uniform(next(keys), (n,), jnp.float32, 0.9, 0.999)
        a = a_c ** (1.0 / LRU_C)
        return jnp.log(a) - jnp.log1p(-a)

    d, f, w = D_MODEL, D_FF, LRU_WIDTH
    p = {}
    p["x"] = normal((BATCH, SEQ, d), 1.0)
    p["l0_ff1_norm"] = gain(d)
    p["l0_ff1_w_in"] = normal((d, 2 * f), d ** -0.5)
    p["l0_ff1_w_out"] = normal((f, d), f ** -0.5)
    p["l0_mix_norm"] = gain(d)
    p["l0_sb_w_qkv"] = normal((d, 3 * SB_HEADS * SB_HEAD_DIM), d ** -0.5)
    p["l0_sb_q_norm"] = gain(SB_HEAD_DIM)
    p["l0_sb_k_norm"] = gain(SB_HEAD_DIM)
    p["l0_sb_w_o"] = normal((SB_HEADS * SB_HEAD_DIM, d), d ** -0.5)
    p["l0_ff2_norm"] = gain(d)
    p["l0_ff2_w_in"] = normal((d, 2 * f), d ** -0.5)
    p["l0_ff2_w_out"] = normal((f, d), f ** -0.5)
    p["l1_ff1_norm"] = gain(d)
    p["l1_ff1_w_in"] = normal((d, 2 * f), d ** -0.5)
    p["l1_ff1_w_out"] = normal((f, d), f ** -0.5)
    p["l1_mix_norm"] = gain(d)
    p["l1_lru_w_in"] = normal((d, 2 * w), d ** -0.5)
    p["l1_lru_conv_w"] = normal((CONV_W, w), CONV_W ** -0.5)
    p["l1_lru_conv_b"] = normal((w,), 0.01)
    p["l1_lru_w_r"] = normal((LRU_BLOCKS, LRU_BLOCK_W, LRU_BLOCK_W), LRU_BLOCK_W ** -0.5)
    p["l1_lru_b_r"] = normal((w,), 0.01)
    p["l1_lru_w_i"] = normal((LRU_BLOCKS, LRU_BLOCK_W, LRU_BLOCK_W), LRU_BLOCK_W ** -0.5)
    p["l1_lru_b_i"] = normal((w,), 0.01)
    p["l1_lru_lambda"] = lam_init(w)
    p["l1_lru_w_o"] = normal((w, d), w ** -0.5)
    p["l1_ff2_norm"] = gain(d)
    p["l1_ff2_w_in"] = normal((d, 2 * f), d ** -0.5)
    p["l1_ff2_w_out"] = normal((f, d), f ** -0.5)
    return p

def second_block(x,
              l0_ff1_norm, l0_ff1_w_in, l0_ff1_w_out,
              l0_mix_norm, l0_sb_w_qkv, l0_sb_q_norm, l0_sb_k_norm, l0_sb_w_o,
              l0_ff2_norm, l0_ff2_w_in, l0_ff2_w_out,
              l1_ff1_norm, l1_ff1_w_in, l1_ff1_w_out,
              l1_mix_norm, l1_lru_w_in, l1_lru_conv_w, l1_lru_conv_b,
              l1_lru_w_r, l1_lru_b_r, l1_lru_w_i, l1_lru_b_i, l1_lru_lambda, l1_lru_w_o,
              l1_ff2_norm, l1_ff2_w_in, l1_ff2_w_out):
    ffn1 = [(l0_ff1_norm, l0_ff1_w_in, l0_ff1_w_out),
            (l1_ff1_norm, l1_ff1_w_in, l1_ff1_w_out)]
    ffn2 = [(l0_ff2_norm, l0_ff2_w_in, l0_ff2_w_out),
            (l1_ff2_norm, l1_ff2_w_in, l1_ff2_w_out)]
    mixers = [(l0_mix_norm, (l0_sb_w_qkv, l0_sb_q_norm, l0_sb_k_norm, l0_sb_w_o)),
              (l1_mix_norm, (l1_lru_w_in, l1_lru_conv_w, l1_lru_conv_b, l1_lru_w_r, l1_lru_b_r,
                             l1_lru_w_i, l1_lru_b_i, l1_lru_lambda, l1_lru_w_o))]
    for layer in range(DEPTH):
        n1, wi1, wo1 = ffn1[layer]
        x = x + 0.5 * swiglu(rms_norm(x, n1), wi1, wo1)
        mix_norm, mix_params = mixers[layer]
        xn = rms_norm(x, mix_norm)
        if layer % N_MIXERS == 0:
            x = x + stick_breaking_attention(xn, *mix_params)
        else:
            x = x + rglru_block(xn, *mix_params)
        n2, wi2, wo2 = ffn2[layer]
        x = x + 0.5 * swiglu(rms_norm(x, n2), wi2, wo2)
    return x


def setup_inputs(seed=0):
    out = dict(first_inputs(seed))
    for name, value in second_inputs(seed + 1).items():
        if name != "x":
            out[name + "_2"] = value
    return out


def reference(
    x, n1_g, ffn1_w_in, ffn1_w_out, n2_g, w_in, rel_bias, w_branch_a, w_branch_b, w_out, n3_g,
    ffn2_w_in, ffn2_w_out, nf_g, l0_ff1_norm_2, l0_ff1_w_in_2, l0_ff1_w_out_2, l0_mix_norm_2,
    l0_sb_w_qkv_2, l0_sb_q_norm_2, l0_sb_k_norm_2, l0_sb_w_o_2, l0_ff2_norm_2, l0_ff2_w_in_2,
    l0_ff2_w_out_2, l1_ff1_norm_2, l1_ff1_w_in_2, l1_ff1_w_out_2, l1_mix_norm_2, l1_lru_w_in_2,
    l1_lru_conv_w_2, l1_lru_conv_b_2, l1_lru_w_r_2, l1_lru_b_r_2, l1_lru_w_i_2, l1_lru_b_i_2,
    l1_lru_lambda_2, l1_lru_w_o_2, l1_ff2_norm_2, l1_ff2_w_in_2, l1_ff2_w_out_2,
):
    x = first_block(
        x, n1_g, ffn1_w_in, ffn1_w_out, n2_g, w_in, rel_bias, w_branch_a, w_branch_b, w_out,
        n3_g, ffn2_w_in, ffn2_w_out, nf_g,
    )
    return second_block(
        x, l0_ff1_norm_2, l0_ff1_w_in_2, l0_ff1_w_out_2, l0_mix_norm_2, l0_sb_w_qkv_2,
        l0_sb_q_norm_2, l0_sb_k_norm_2, l0_sb_w_o_2, l0_ff2_norm_2, l0_ff2_w_in_2,
        l0_ff2_w_out_2, l1_ff1_norm_2, l1_ff1_w_in_2, l1_ff1_w_out_2, l1_mix_norm_2,
        l1_lru_w_in_2, l1_lru_conv_w_2, l1_lru_conv_b_2, l1_lru_w_r_2, l1_lru_b_r_2,
        l1_lru_w_i_2, l1_lru_b_i_2, l1_lru_lambda_2, l1_lru_w_o_2, l1_ff2_norm_2, l1_ff2_w_in_2,
        l1_ff2_w_out_2,
    )


_drawn_inputs = setup_inputs


def setup_inputs(seed=0):
    import zlib

    import numpy as np

    out = dict(_drawn_inputs(seed))
    spreads = {}
    factors = {'n1_g': 4.362,
     'n2_g': 4.548,
     'rel_bias': 4.402,
     'n3_g': 6.512,
     'l0_ff1_norm_2': 6.249,
     'l0_mix_norm_2': 4.459,
     'l0_sb_q_norm_2': 8.0,
     'l0_sb_k_norm_2': 8.0,
     'l0_ff2_norm_2': 8.0}
    for name, (base, spread) in spreads.items():
        noise = np.random.default_rng([zlib.crc32(name.encode()), seed]).standard_normal(out[name].shape)
        drawn = base * np.exp(spread * noise) if base else spread * noise
        out[name] = __import__('jax').numpy.asarray(drawn.astype(out[name].dtype))
    for name, factor in factors.items():
        out[name] = (out[name] * factor).astype(out[name].dtype)
    return out
```

```python
from contextlib import ExitStack

import numpy as np
import concourse.bass as bass
from concourse import mybir

F32, F32R, BF16 = mybir.dt.float32, mybir.dt.float32r, mybir.dt.bfloat16
ACT, ALU = mybir.ActivationFunctionType, mybir.AluOpType

P = 128
TOK = 512
D = 1024
DT = D // P
FT = 2816 // P
QT = TOK // P
HD = 64
HEADS = 8
SB_HEADS = 16
CHUNK = 64
TOPK = min(256, TOK // 4)
EPS = 1e-6
NSLOT = 4
AHEAD = 2
UK = 8
DOWN = [(0, 8), (8, 16), (16, FT)]

UP_UNITS, DOWN_UNITS = 2 * FT, len(DOWN) * DT
PROJ_UNITS, GATE_UNITS, OUT_UNITS = 24, 3 * DT, DT
FFN_UNITS = UP_UNITS + DOWN_UNITS
U_FFN1 = 0
U_PROJ = U_FFN1 + FFN_UNITS
U_GATE = U_PROJ + PROJ_UNITS
U_OUT = U_GATE + GATE_UNITS
U_FFN2 = U_OUT + OUT_UNITS
U_FFN3 = U_FFN2 + FFN_UNITS
U_QKV = U_FFN3 + FFN_UNITS
U_SBO = U_QKV + PROJ_UNITS
U_FFN4 = U_SBO + OUT_UNITS
UNITS = U_FFN4 + FFN_UNITS
FFN_BASE = [U_FFN1, U_FFN2, U_FFN3, U_FFN4]

FFN_RES, MIX_RES = [0, 2, 3, 5], [1, 4]
S_START, S_FFN1, S_MIX1, S_FFN2, S_FINAL, S_FFN3, S_MIX2 = range(7)
T_START, T_FFN1, T_MIX1, T_FINAL, T_FFN3, T_MIX2 = range(6)
G_FINAL = 6
FFN_STAT = [S_START, S_MIX1, S_FINAL, S_MIX2]
FFN_INPUT = [T_START, T_MIX1, T_FINAL, T_MIX2]

KI, WI, QI, KB, VB, QB, QA, KA, VA = range(9)
PROJ = [(KI, 0), (WI, 0), (QI, 0), (QI, 1), (QI, 2), (QI, 3), (KB, 0), (VB, 0)] + [
    (what, t) for what in (QB, QA, KA, VA) for t in range(4)]
ROPE = [n for n, (what, _) in enumerate(PROJ) if what in (KI, QI, KB, QB)]
QUERY = (QI, QB, QA)
INDEX = [(i, h) for i in range(1, QT) for h in range(HEADS)]
INDEX_FROM, INDEX_EACH = 7, 3
ROUNDS = TOPK // 8
TOP_FROM, TOP_EACH = 10, 4
STEPS = [(br, i, h) for br in range(2) for i in range(QT) for h in range(HEADS)]
GROUPS = 2 * QT


FAR = -1e30
OUTSIDE = -3.0e38
TAKEN = -3.2e38
TAKEN_BELOW = -3.1e38



def program(nc, weights, consts, consts_b, ropes, rel, gain_cols, head_gains, x, out):
    with ExitStack() as ctx:
        build(nc, ctx, weights, consts, consts_b, ropes, rel, gain_cols, head_gains, x, out)


def build(nc, ctx, weights, consts, consts_b, ropes, rel, gain_cols, head_gains, x, out):
    size = {F32: 4, F32R: 4, BF16: 2}
    fixed = [(nc.sbuf_base + 63) // 64 * 64]

    def place(name, shape, dt=F32, where=fixed):
        tensor = nc.alloc_sbuf_tensor_at(name, shape, dt, offset=where[0])
        where[0] += (int(np.prod(shape[1:])) * size[dt] + 31) // 32 * 32
        assert where[0] <= nc.sbuf_usable_end
        return tensor

    X = place("x_sb", [P, DT, TOK])
    xn_hi = place("xn_hi", [P, DT, TOK], F32R)
    xn_lo = place("xn_lo", [P, DT, TOK], F32R)
    raw = [place(f"raw{s}", [P, UK, P]) for s in range(NSLOT)]
    w_hi = [place(f"w_hi{s}", [P, UK, P], F32R) for s in range(NSLOT)]
    w_lo = [place(f"w_lo{s}", [P, UK, P], F32R) for s in range(NSLOT)]
    rstd = place("rstd", [P, TOK])
    ssq = place("ssq", [P, TOK])
    const = place("const", [P, 6, P])
    ident, mean_all, mean_head, swap, minus_upto, minus_ones = (const[:, n, :] for n in range(6))
    const_b = place("const_b", [P, 2, P], BF16)
    ident_b, far_b = const_b[:, 0, :], const_b[:, 1, :]
    gains = place("gains", [P, 7, DT])
    head_gain = place("head_gain", [P, 4])
    eps_col = place("eps_col", [P, 1])
    one_col = place("one_col", [P, 1])
    small = place("small", [P, 232])
    w_tok = small[:, 0:32]
    top8 = small[:, 32:48]
    row_sum, row_neg_max, row_inv = small[:, 96:160], small[:, 160:224], small[:, 224:232]
    region = fixed[0]

    at = [region]
    h_hi = place("h_hi", [P, FT, TOK], F32R, at)
    h_lo = place("h_lo", [P, FT, TOK], F32R, at)
    scratch = place("scratch", [P, 7, TOK], F32, at)

    at = [region]
    qa = place("qa", [P, 4, TOK], F32, at)
    ka = place("ka", [P, 4, TOK], F32, at)
    qb = place("qb", [P, 4, TOK], F32, at)
    kb = place("kb", [P, TOK], F32, at)
    va = place("va", [P, QT, 512], F32, at)
    vb = place("vb", [P, QT, P], F32, at)
    bias = place("bias", [P, HEADS, TOK], F32, at)
    mask = [place(f"mask{i}", [P, P * (i + 1)], F32, at) for i in range(QT)]
    before_attention = [at[0]]
    o_hi = [place("oa_hi", [P, 4, TOK], F32R, at), place("ob_hi", [P, 4, TOK], F32R, at)]
    o_lo = [place("oa_lo", [P, 4, TOK], F32R, at), place("ob_lo", [P, 4, TOK], F32R, at)]
    assert at[0] <= region + 2 * FT * TOK * 4 + TOK * 4
    qi = place("qi", [P, 4, TOK], F32, before_attention)
    ki = place("ki", [P, TOK], F32, before_attention)
    rope = place("rope", [P, 2, TOK], F32, before_attention)
    at = [region]
    m_hi = place("m_hi", [P, DT, TOK], F32R, at)
    m_lo = place("m_lo", [P, DT, TOK], F32R, at)

    at = [region]
    sb_q = place("sb_q", [P, DT, TOK], F32, at)
    sb_k = place("sb_k", [P, DT, TOK], F32, at)
    sb_v = place("sb_v", [P, QT, D], F32, at)
    so_hi = place("so_hi", [P, DT, TOK], F32R, at)
    so_lo = place("so_lo", [P, DT, TOK], F32R, at)
    width = [TOK - P * j for j in range(QT)]
    col = [0, width[0], width[0] + width[1] + width[3], width[0] + width[1]]
    SBW = sum(width)
    sb_e = [place(f"sb_e{b}", [P, SBW], F32, at) for b in range(2)]
    sb_s = [place(f"sb_s{b}", [P, SBW], F32, at) for b in range(2)]

    PS = ctx.enter_context(nc.psum_tensor("ps", [P, 8, TOK], F32))
    ps_flat = PS[:, :, :].rearrange("p b n -> p (b n)")

    names = """hi_done lo_done unit_done consts_in gains_in rope_in bias_in cols_ready
        x_updated x_normed sq_done ssq_zeroed ssq_done ms_done rms_done rstd_ready
        xg_done xn_hi_done xn_lo_done gate_scaled silu_done up_scaled h_made h_hi_done h_lo_done
        plain_made rope_scaled swap_done rope_sined rope_added
        wi_made wt_turned wt_copied v_made v_turned v_copied
        idx_done relu_done idx_added score_ready top_found top_taken mask_ready bias_ready
        s_done s_biased p_made p_turned pt_copied pv_done inv_made o_normed o_turned o_hi_done
        o_lo_done gate_in gate_sig branch_gated merged m_hi_done m_lo_done
        qk_sq qk_ms qk_rms qk_inv qk_normed z_done abs_done e_done l_done sp_done cum_done
        w_done sb_pv so_hi_done so_lo_done stored""".split()
    S = {name: ctx.enter_context(nc.semaphore(name)) for name in names}
    raw_landed = [ctx.enter_context(nc.semaphore(f"raw_landed{s}")) for s in range(NSLOT)]
    x_landed = [ctx.enter_context(nc.semaphore(f"x_landed{k}")) for k in range(DT)]

    def evacuated_1(n):
        what, t = PROJ[n]
        if n in ROPE:
            return S["rope_scaled"], ROPE.index(n) + 1
        if what == WI:
            return S["wi_made"], 1
        if what in (VB, VA):
            return S["v_made"], 1 if what == VB else 2 + t
        return S["plain_made"], 1 + t + 4 * (what == KA)

    def evacuated_2(n):
        return (S["plain_made"], 8 + n + 1) if n < 2 * DT else (S["v_made"], 5 + n - 2 * DT + 1)

    block = ctx.enter_context(nc.Block())

    @block.sync
    def _(sp):
        def load(u, s):
            sp.dma_start(raw[s][:, :, :], weights[u]).then_inc(raw_landed[s], 16)

        for s in range(NSLOT):
            load(s, s)
        with sp.Fori(1, UNITS // NSLOT) as it:
            for s in range(NSLOT):
                sp.wait_ge(S["lo_done"], NSLOT * it + (s + 1 - NSLOT))
                load(NSLOT * it + s, s)
        for n in range(DT):
            sp.wait_ge(S["x_updated"], DT * FFN_RES[3] + n + 1)
            sp.dma_start(out[:, n, :], X[:, n, :]).then_inc(S["stored"], 16)
        sp.wait_ge(S["stored"], 16 * DT)

    @block.gpsimd
    def _(pool):
        with pool.Fori(0, UNITS // NSLOT) as it:
            for s in range(NSLOT):
                pool.wait_ge(S["hi_done"], NSLOT * it + (s + 1))
                nc.gpsimd.tensor_tensor(w_lo[s][:, :, :], raw[s][:, :, :], w_hi[s][:, :, :].bitcast(F32),
                                        ALU.subtract).then_inc(S["lo_done"], 1)

    @block.tensor
    def _(pe):
        def unit(u, s, outs, tiles, before=None, start=True, stop=True):
            pe.wait_ge(S["lo_done"], u + 1)
            for k, (hi, lo) in enumerate(tiles):
                if before:
                    before(k)
                opens = start and (k == 0 or outs[k] != outs[k - 1])
                ends = stop and (k == len(tiles) - 1 or outs[k] != outs[k + 1])
                to = PS[:, outs[k], :]
                pe.matmul(to, w_hi[s][:, k, :], hi, start=opens, stop=False)
                pe.matmul(to, w_hi[s][:, k, :], lo, start=False, stop=False)
                last = pe.matmul(to, w_lo[s][:, k, :], hi, start=False, stop=ends)
            last.then_inc(S["unit_done"], 1)

        xn = [(xn_hi[:, k, :], xn_lo[:, k, :]) for k in range(DT)]

        def mean_square(stat):
            pe.wait_ge(S["ssq_done"], DT * (stat + 1))
            pe.matmul(PS[:, 4, :], mean_all, ssq[:, :], start=True, stop=True).then_inc(S["ms_done"], 1)

        def first_unit_waits(t, stat):
            def before(k):
                if k == DT - 1:
                    mean_square(stat)
                pe.wait_ge(S["xn_lo_done"], DT * t + k + 1)
            return before

        def ffn_up(n):
            def tile(F, j, before=None):
                u = FFN_BASE[n] + 2 * F
                for g in range(2):
                    unit(u + g, 2 * j + g, [2 * j + g] * UK, xn, before if g == 0 else None)

            if n == 0:
                pe.wait_ge(S["consts_in"], 32)
            else:
                pe.wait_ge(S["x_updated"], DT * FFN_RES[n])
            for j in range(2):
                tile(j, j, first_unit_waits(FFN_INPUT[n], FFN_STAT[n]) if j == 0 else None)
            with pe.Fori(1, FT // 2) as it:
                for j in range(2):
                    pe.wait_ge(S["h_made"], 2 * it + (FT * n + j - 1))
                    tile(2 * it + j, j)

        def residual(u0, kinds, tiles, ready, freed, freed0):
            def body(it):
                for j in range(4):
                    pe.wait_ge(freed, 4 * it + (freed0 + j - 3))
                    for c, (k0, k1) in enumerate(kinds):
                        n_u = 4 * len(kinds)
                        at_unit = j * len(kinds) + c
                        unit(n_u * it + (u0 + at_unit), at_unit % NSLOT, [j] * (k1 - k0), tiles[k0:k1],
                             (lambda k, k0=k0: ready(k0 + k)) if j == 0 else None,
                             start=(c == 0), stop=(c == len(kinds) - 1))
            with pe.Fori(0, 2) as it:
                body(it)

        def ffn_down(n):
            def ready(k):
                if k == 0:
                    pe.wait_ge(S["h_lo_done"], FT * n + FT - 1)
                if k == FT - 1:
                    pe.wait_ge(S["h_lo_done"], FT * n + FT)

            pe.wait_ge(S["h_made"], FT * n + FT - 1)
            freed, freed0 = (S["x_updated"], DT * FFN_RES[n]) if n else (S["ssq_done"], DT * S_FFN1)
            residual(FFN_BASE[n] + UP_UNITS, DOWN,
                     [(h_hi[:, k, :], h_lo[:, k, :]) for k in range(FT)], ready, freed, freed0)

        def projection_1():
            pe.wait_ge(S["x_updated"], DT * (FFN_RES[0] + 1))
            for n, (what, t) in enumerate(PROJ):
                if n >= 4:
                    pe.wait_ge(*evacuated_1(n - 4))
                unit(U_PROJ + n, n % NSLOT, [n % 4] * UK, xn,
                     first_unit_waits(T_FFN1, S_FFN1) if n == 0 else None)
                turn_1(n - 1)
                if n == 2:
                    pe.wait_ge(S["wi_made"], 1)
                    for i in range(QT):
                        last = pe.transpose(PS[:, 4, 8 * i:8 * i + 8], scratch[0:8, 4, P * i:P * (i + 1)],
                                            ident[0:8, 0:8])
                    last.then_inc(S["wt_turned"], 1)
                for m in index_steps(n):
                    i, h = INDEX[m]
                    if m == 0:
                        pe.wait_ge(S["rope_added"], 5)
                    if m >= 2:
                        pe.wait_ge(S["relu_done"], m - 1)
                    r = HD * (h % 2)
                    pe.matmul(PS[:, 6 + m % 2, 0:P * (i + 1)], qi[r:r + HD, h // 2, P * i:P * (i + 1)],
                              ki[r:r + HD, 0:P * (i + 1)], start=True, stop=True).then_inc(S["idx_done"], 1)
            turn_1(len(PROJ) - 1)

        def turn_1(n):
            if n < 0:
                return
            what, t = PROJ[n]
            if n in ROPE:
                k = ROPE.index(n)
                pe.wait_ge(S["rope_scaled"], k + 1)
                if k:
                    pe.wait_ge(S["rope_sined"], k)
                pe.matmul(PS[:, 5, :], swap, scratch[:, k % 2, :], start=True, stop=True)\
                  .then_inc(S["swap_done"], 1)
            if what in (VB, VA):
                v = 0 if what == VB else 1 + t
                turn_v(v, 4, 4 + v % 2)

        def turn_v(v, bank, buf):
            pe.wait_ge(S["v_made"], v + 1)
            if v:
                pe.wait_ge(S["v_copied"], v)
            else:
                pe.wait_ge(S["wt_copied"], 1)
            for i in range(QT):
                last = pe.transpose(PS[:, bank, P * i:P * (i + 1)], scratch[:, buf, P * i:P * (i + 1)], ident)
            last.then_inc(S["v_turned"], 1)

        def attention_1():
            for m in range(len(STEPS) + 4):
                if m < len(STEPS):
                    br, i, h = STEPS[m]
                    t, r = (h // 2, HD * (h % 2)) if br == 0 else (h % 4, HD * (h // 4))
                    q = (qa, qb)[br][r:r + HD, t, P * i:P * (i + 1)]
                    k = ka[r:r + HD, t, 0:P * (i + 1)] if br == 0 else kb[r:r + HD, 0:P * (i + 1)]
                    if m == 0:
                        pe.wait_ge(S["plain_made"], 8)
                        pe.wait_ge(S["rope_added"], len(ROPE))
                        pe.wait_ge(S["v_copied"], 5)
                    if m >= 2:
                        pe.wait_ge(S["s_biased"], m - 1)
                    pe.matmul(PS[:, 4 + m % 2, 0:P * (i + 1)], q, k, start=True, stop=True)\
                      .then_inc(S["s_done"], 1)
                if 1 <= m <= len(STEPS):
                    n = m - 1
                    br, i, h = STEPS[n]
                    pe.wait_ge(S["p_made"], n + 1)
                    if n >= 2:
                        pe.wait_ge(S["pt_copied"], n - 1)
                    for j in range(i + 1):
                        last = pe.transpose(PS[:, 6 + n % 2, P * j:P * (j + 1)],
                                            scratch[:, 3 + n % 2, P * j:P * (j + 1)], ident)
                    last.then_inc(S["p_turned"], 1)
                if 2 <= m < len(STEPS) + 2:
                    n = m - 2
                    br, i, h = STEPS[n]
                    group = n // HEADS
                    pe.wait_ge(S["pt_copied"], n + 1)
                    if h == 0 and group >= 2:
                        pe.wait_ge(S["o_normed"], group - 1)
                    for j in range(i + 1):
                        v = va[:, j, HD * h:HD * (h + 1)] if br == 0 else vb[:, j, HD * (h // 4):HD * (h // 4 + 1)]
                        last = pe.matmul(PS[:, group % 2, HD * h:HD * (h + 1)],
                                         scratch[:, 5 + n % 2, P * j:P * (j + 1)], v,
                                         start=(j == 0), stop=(j == i))
                    last.then_inc(S["pv_done"], 1)
                if m % HEADS == 3 and m > HEADS:
                    g = m // HEADS - 1
                    pe.wait_ge(S["o_normed"], g + 1)
                    if g >= 2:
                        pe.wait_ge(S["o_lo_done"], g - 1)
                    for c in range(4):
                        last = pe.transpose(PS[:, 2 + g % 2, P * c:P * (c + 1)],
                                            ssq[:, P * c:P * (c + 1)], ident)
                    last.then_inc(S["o_turned"], 1)

        def merge():
            pe.wait_ge(S["o_normed"], GROUPS)
            o = [(o_hi[br][:, k, :], o_lo[br][:, k, :]) for br in range(2) for k in range(4)]
            for n in range(DT):
                b = 4 * (n % 2)
                if n >= 2:
                    pe.wait_ge(S["merged"], n - 1)
                for g in range(2):
                    unit(U_GATE + 3 * n + g, (3 * n + g) % NSLOT, [b + g] * UK, xn)
                if n == 0:
                    pe.wait_ge(S["o_lo_done"], GROUPS)
                unit(U_GATE + 3 * n + 2, (3 * n + 2) % NSLOT, [b + 2] * 4 + [b + 3] * 4, o)

        def mixer_out_1():
            pe.wait_ge(S["merged"], DT - 1)
            residual(U_OUT, [(0, DT)], [(m_hi[:, k, :], m_lo[:, k, :]) for k in range(DT)],
                     lambda k: pe.wait_ge(S["m_lo_done"], k + 1), S["x_updated"], DT * MIX_RES[0])

        def projection_2():
            pe.wait_ge(S["x_updated"], DT * (FFN_RES[2] + 1))
            for n in range(PROJ_UNITS + 1):
                if n < PROJ_UNITS:
                    if n >= 4:
                        pe.wait_ge(*evacuated_2(n - 4))
                    unit(U_QKV + n, n % NSLOT, [n % 4] * UK, xn,
                         first_unit_waits(T_FFN3, S_FFN3) if n == 0 else None)
                v = n - 1
                if 0 <= v < 2 * DT:
                    pe.wait_ge(S["qk_sq"], v + 1)
                    if v == 0:
                        pe.wait_ge(S["rms_done"], S_FFN3 + 1)
                    if v >= 2:
                        pe.wait_ge(S["qk_rms"], v - 1)
                    pe.matmul(PS[:, 4 + v % 2, :], mean_head, scratch[:, v % 2, :], start=True, stop=True)\
                      .then_inc(S["qk_ms"], 1)
                elif v >= 2 * DT:
                    turn_v(5 + v - 2 * DT, 6, 4 + v % 2)

        def stick_breaking():
            def bank(h, j):
                return TOK * 4 * (h % 2) + col[j]

            def z(h):
                r, t = HD * (h % 2), h // 2
                if h >= 2:
                    pe.wait_ge(S["w_done"], h - 1)
                for j in (0, 1, 2, 3):
                    pe.matmul(ps_flat[:, bank(h, j):bank(h, j) + width[j]],
                              sb_k[r:r + HD, t, P * j:P * (j + 1)], sb_q[r:r + HD, t, P * j:TOK],
                              start=(j < 3), stop=False, skip_group_check=True)
                for j in range(QT):
                    last = pe.matmul(ps_flat[:, bank(h, j):bank(h, j) + P], ident_b, far_b,
                                     start=False, stop=(j == 3), skip_group_check=True)
                last.then_inc(S["z_done"], 1)

            def cumulate(h):
                pe.wait_ge(S["sp_done"], h + 1)
                for j in range(QT):
                    for k in range(j, QT):
                        to = bank(h, j) + P * (k - j)
                        last = pe.matmul(ps_flat[:, to:to + width[k]], minus_upto if k == j else minus_ones,
                                         sb_s[h % 2][:, col[k]:col[k] + width[k]],
                                         start=False, stop=True, skip_group_check=True)
                last.then_inc(S["cum_done"], 1)

            def weigh(h):
                pe.wait_ge(S["w_done"], h + 1)
                if h % 2 == 0 and h >= 4:
                    pe.wait_ge(S["so_lo_done"], h // 2 - 1)
                b, r = 3 + 4 * (h // 2 % 2), HD * (h % 2)
                for j in range(QT):
                    last = pe.matmul(PS[r:r + HD, b, P * j:TOK], sb_v[:, j, HD * h:HD * (h + 1)],
                                     sb_s[h % 2][:, col[j]:col[j] + width[j]],
                                     start=(j == 0), stop=(j == 3), skip_group_check=True)
                last.then_inc(S["sb_pv"], 1)

            pe.wait_ge(S["qk_normed"], 2 * DT)
            pe.wait_ge(S["v_copied"], 5 + DT)
            z(0)
            z(1)
            for h in range(SB_HEADS + 1):
                if h < SB_HEADS:
                    cumulate(h)
                if h:
                    weigh(h - 1)
                if h + 2 < SB_HEADS:
                    z(h + 2)

        def mixer_out_2():
            pe.wait_ge(S["w_done"], SB_HEADS)
            residual(U_SBO, [(0, DT)], [(so_hi[:, k, :], so_lo[:, k, :]) for k in range(DT)],
                     lambda k: pe.wait_ge(S["so_lo_done"], k + 1), S["x_updated"], DT * MIX_RES[1])

        ffn_up(0)
        ffn_down(0)
        projection_1()
        attention_1()
        merge()
        mixer_out_1()
        ffn_up(1)
        ffn_down(1)
        mean_square(S_FFN2)
        ffn_up(2)
        ffn_down(2)
        projection_2()
        stick_breaking()
        mixer_out_2()
        ffn_up(3)
        ffn_down(3)

    @block.scalar
    def _(act):
        for k in range(DT):
            act.dma_start(X[:, k, :], x[:, k, :]).then_inc(x_landed[k], 16)
        act.dma_start(gains[:, :, :], gain_cols).then_inc(S["gains_in"], 16)
        act.dma_start(head_gain[:, 0:2], head_gains).then_inc(S["gains_in"], 16)
        act.dma_start(const[:, :, :], consts).then_inc(S["consts_in"], 16)
        act.dma_start(const_b[:, :, :], consts_b).then_inc(S["consts_in"], 16)
        act.wait_ge(S["cols_ready"], 2)

        def copy(dst, src):
            return nc.scalar.activation(dst, src, ACT.Copy)

        def round_weights(u, s, turn):
            act.wait_ge(raw_landed[s], 16 * turn + 16)
            if not (isinstance(u, int) and u < NSLOT):
                act.wait_ge(S["unit_done"], u + (1 - NSLOT))
            copy(w_hi[s][:, :, :], raw[s][:, :, :]).then_inc(S["hi_done"], 1)

        def ahead(u):
            if u + AHEAD < UNITS:
                round_weights(u + AHEAD, (u + AHEAD) % NSLOT, (u + AHEAD) // NSLOT)

        def ahead_in_loop(it, per, u0, j):
            v = u0 + j + AHEAD
            round_weights(per * it + v, v % NSLOT, (per // NSLOT) * it + v // NSLOT)

        def root_mean_square(stat):
            act.wait_ge(S["ms_done"], stat + 1)
            nc.scalar.activation(scratch[:, 6, :], PS[:, 4, :], ACT.Sqrt, bias=eps_col[:, 0:1])\
              .then_inc(S["rms_done"], 1)

        def square(k, b, stat, n_before):
            if not isinstance(n_before, int) or n_before >= 2:
                act.wait_ge(S["ssq_done"], n_before + (DT * stat - 1))
            nc.scalar.activation(scratch[:, 4 + b, :], X[:, k, :], ACT.Square).then_inc(S["sq_done"], 1)

        def round_input(k, b, t):
            act.wait_ge(S["xg_done"], k + (DT * t + 1))
            copy(xn_hi[:, k, :], scratch[:, 2 + b, :]).then_inc(S["xn_hi_done"], 1)

        def ffn_up(n):
            def tile(F, j, first=False):
                u = FFN_BASE[n] + 2 * F if isinstance(F, int) else None
                if first:
                    ahead(u)
                    root_mean_square(FFN_STAT[n])
                    ahead(u + 1)
                elif u is not None:
                    ahead(u)
                    ahead(u + 1)
                f = FT * n + F if isinstance(F, int) else F + FT * n
                act.wait_ge(S["gate_scaled"], f + 1)
                nc.scalar.activation(scratch[:, j, :], scratch[:, j, :], ACT.Silu).then_inc(S["silu_done"], 1)
                act.wait_ge(S["h_made"], f + 1)
                copy(h_hi[:, F, :], scratch[:, 2 + j, :]).then_inc(S["h_hi_done"], 1)

            tile(0, 0, first=True)
            tile(1, 1)
            with act.Fori(1, FT // 2) as it:
                for j in range(2):
                    ahead_in_loop(it, 4, FFN_BASE[n], 2 * j)
                    ahead_in_loop(it, 4, FFN_BASE[n], 2 * j + 1)
                    tile(2 * it + j, j)

        def residual(u0, per, r, t, stat):
            with act.Fori(0, 2) as it:
                for j in range(4):
                    for c in range(per):
                        ahead_in_loop(it, 4 * per, u0, j * per + c)
                    tail(4 * it + j, j % 2, r, t, stat)

        def tail(k, b, r, t, stat):
            act.wait_ge(S["x_updated"], k + (DT * r + 1))
            square(k, b, stat, k)
            if t is not None:
                round_input(k, b, t)

        def projection_1():
            act.wait_ge(S["unit_done"], U_PROJ)
            act.dma_start(rope[:, :, :], ropes).then_inc(S["rope_in"], 16)
            runs = bass.AP(rel.tensor, 1, [[1, P], [rel.shape[1], HEADS], [1, TOK]])
            act.dma_start(bias[:, :, :], runs).then_inc(S["bias_in"], 16)
            for n, (what, t) in enumerate(PROJ):
                ahead(U_PROJ + n)
                if n == 0:
                    root_mean_square(S_FFN1)
                copy_v_1(n - 1)
                for m in index_steps(n):
                    i, h = INDEX[m]
                    act.wait_ge(S["idx_done"], m + 1)
                    if m >= 2:
                        act.wait_ge(S["idx_added"], m - 1)
                    nc.scalar.activation(scratch[:, 5 + m % 2, 0:P * (i + 1)], PS[:, 6 + m % 2, 0:P * (i + 1)],
                                         ACT.Relu).then_inc(S["relu_done"], 1)
            copy_v_1(len(PROJ) - 1)

        def copy_v_1(n):
            if n >= 0 and PROJ[n][0] == VB:
                copy_v(0, 4, vb[:, :, :])
            if n >= 0 and PROJ[n][0] == VA:
                t = PROJ[n][1]
                copy_v(1 + t, 4, va[:, :, P * t:P * (t + 1)])

        def copy_v(v, bank, dst):
            act.wait_ge(S["v_turned"], v + 1)
            copy(dst, PS[:, bank, :].rearrange("p (i n) -> p i n", i=QT)).then_inc(S["v_copied"], 1)

        def attention_1():
            for m in range(len(STEPS) + 4):
                if m < len(STEPS):
                    br, i, h = STEPS[m]
                    act.wait_ge(S["s_biased"], m + 1)
                    if m >= 2:
                        act.wait_ge(S["p_turned"], m - 1)
                    nc.scalar.activation(scratch[:, 3 + m % 2, 0:P * (i + 1)], scratch[:, 1 + m % 2, 0:P * (i + 1)],
                                         ACT.Exp, bias=row_neg_max[:, m:m + 1], scale=-1.0,
                                         accum_out=row_sum[:, m:m + 1]).then_inc(S["p_made"], 1)
                if 1 <= m <= len(STEPS):
                    n = m - 1
                    br, i, h = STEPS[n]
                    act.wait_ge(S["p_turned"], n + 1)
                    if n >= 2:
                        act.wait_ge(S["pv_done"], n - 1)
                    copy(scratch[:, 5 + n % 2, 0:P * (i + 1)], PS[:, 6 + n % 2, 0:P * (i + 1)])\
                        .then_inc(S["pt_copied"], 1)
                if m % HEADS == 3 and m > HEADS:
                    g = m // HEADS - 1
                    br, i = g // QT, g % QT
                    act.wait_ge(S["o_turned"], g + 1)
                    copy(o_hi[br][:, :, P * i:P * (i + 1)], PS[:, 2 + g % 2, :].rearrange("p (c n) -> p c n", c=4))\
                        .then_inc(S["o_hi_done"], 1)

        def merge():
            for n in range(DT):
                for g in range(3):
                    ahead(U_GATE + 3 * n + g)
                    if g < 2:
                        act.wait_ge(S["gate_in"], 2 * n + g + 1)
                        nc.scalar.activation(scratch[:, 1 + g, :], scratch[:, 1 + g, :], ACT.Sigmoid)\
                            .then_inc(S["gate_sig"], 1)
                act.wait_ge(S["merged"], n + 1)
                copy(m_hi[:, n, :], scratch[:, 5 + n % 2, :]).then_inc(S["m_hi_done"], 1)

        def projection_2():
            for n in range(PROJ_UNITS + 1):
                if n < PROJ_UNITS:
                    ahead(U_QKV + n)
                if n == 0:
                    root_mean_square(S_FFN3)
                if n < 2 * DT:
                    act.wait_ge(S["plain_made"], 8 + n + 1)
                    if n >= 2:
                        act.wait_ge(S["qk_ms"], n - 1)
                    nc.scalar.activation(scratch[:, n % 2, :], (sb_q, sb_k)[n // DT][:, n % DT, :], ACT.Square)\
                        .then_inc(S["qk_sq"], 1)
                v = n - 1
                if 0 <= v < 2 * DT:
                    act.wait_ge(S["qk_ms"], v + 1)
                    if v >= 2:
                        act.wait_ge(S["qk_normed"], v - 1)
                    nc.scalar.activation(scratch[:, 2 + v % 2, :], PS[:, 4 + v % 2, :], ACT.Sqrt,
                                         bias=eps_col[:, 0:1]).then_inc(S["qk_rms"], 1)
                elif v >= 2 * DT:
                    t = v - 2 * DT
                    copy_v(5 + t, 6, sb_v[:, :, P * t:P * (t + 1)])

        def stick_breaking():
            def split_out(hp):
                act.wait_ge(S["sb_pv"], 2 * hp + 2)
                copy(so_hi[:, hp, :], PS[:, 3 + 4 * (hp % 2), :]).then_inc(S["so_hi_done"], 1)

            for h in range(SB_HEADS + 1):
                if h >= 4 and h % 2 == 0:
                    split_out(h // 2 - 2)
                if h < SB_HEADS:
                    e = sb_e[h % 2][:, :]
                    act.wait_ge(S["z_done"], h + 1)
                    if h >= 2:
                        act.wait_ge(S["sp_done"], h - 1)
                    zs = ps_flat[:, TOK * 4 * (h % 2):TOK * 4 * (h % 2) + SBW]
                    nc.scalar.activation(e, zs, ACT.Abs).then_inc(S["abs_done"], 1)
                    act.wait_ge(S["abs_done"], h + 1)
                    nc.scalar.activation(e, e, ACT.Exp, scale=-1.0).then_inc(S["e_done"], 1)
                    act.wait_ge(S["e_done"], h + 1)
                    nc.scalar.activation(e, e, ACT.Ln, bias=one_col[:, 0:1]).then_inc(S["l_done"], 1)
                if h:
                    act.wait_ge(S["cum_done"], h)
                    b = TOK * 4 * ((h - 1) % 2)
                    nc.scalar.activation(sb_s[(h - 1) % 2][:, :], ps_flat[:, b:b + SBW], ACT.Exp)\
                        .then_inc(S["w_done"], 1)
            split_out(SB_HEADS // 2 - 1)

        for u in range(AHEAD):
            round_weights(u, u, 0)
        for k in range(DT):
            act.wait_ge(x_landed[k], 16)
            square(k, k % 2, S_START, k)
            round_input(k, k % 2, T_START)
        ffn_up(0)
        residual(FFN_BASE[0] + UP_UNITS, len(DOWN), FFN_RES[0], T_FFN1, S_FFN1)
        projection_1()
        attention_1()
        merge()
        residual(U_OUT, 1, MIX_RES[0], T_MIX1, S_MIX1)
        ffn_up(1)
        residual(FFN_BASE[1] + UP_UNITS, len(DOWN), FFN_RES[1], None, S_FFN2)
        root_mean_square(S_FFN2)
        for k in range(DT):
            act.wait_ge(S["x_normed"], k + 1)
            square(k, k % 2, S_FINAL, k)
            round_input(k, k % 2, T_FINAL)
        ffn_up(2)
        residual(FFN_BASE[2] + UP_UNITS, len(DOWN), FFN_RES[2], T_FFN3, S_FFN3)
        projection_2()
        stick_breaking()
        residual(U_SBO, 1, MIX_RES[1], T_MIX2, S_MIX2)
        ffn_up(3)
        for u in range(FFN_BASE[3] + UP_UNITS, UNITS):
            ahead(u)

    @block.vector
    def _(dve):
        def multiply(dst, p, q):
            return nc.vector.tensor_tensor(dst, p, q, ALU.mult)

        def scale_two(dst, p, scalar, q):
            return nc.vector.scalar_tensor_tensor(dst, p, scalar, q, ALU.mult, ALU.mult)

        def reciprocal_rms(stat):
            dve.wait_ge(S["rms_done"], stat + 1)
            nc.vector.reciprocal(rstd[:, :], scratch[:, 6, :]).then_inc(S["rstd_ready"], 1)
            dve.wait_ge(S["rstd_ready"], stat + 1)

        def zero_ssq(stat):
            nc.vector.memset(ssq[:, :], 0.0).then_inc(S["ssq_zeroed"], 1)
            dve.wait_ge(S["ssq_zeroed"], stat + 1)

        def tail(k, b, t, stat):
            if t is not None:
                nc.vector.tensor_scalar(scratch[:, 2 + b, :], X[:, k, :], gains[:, t, bass.ds(k, 1)], None,
                                        ALU.mult).then_inc(S["xg_done"], 1)
            dve.wait_ge(S["sq_done"], k + (DT * stat + 1))
            if not (isinstance(k, int) and k + stat == 0):
                dve.wait_ge(S["ssq_done"], k + DT * stat)
            nc.vector.tensor_tensor(ssq[:, :], ssq[:, :], scratch[:, 4 + b, :], ALU.add).then_inc(S["ssq_done"], 1)
            if t is not None:
                dve.wait_ge(S["xn_hi_done"], k + (DT * t + 1))
                nc.vector.tensor_tensor(xn_lo[:, k, :], scratch[:, 2 + b, :], xn_hi[:, k, :].bitcast(F32),
                                        ALU.subtract).then_inc(S["xn_lo_done"], 1)

        def ffn_up(n):
            def tile(F, j):
                u, f = 2 * F + FFN_BASE[n], F + FT * n
                dve.wait_ge(S["unit_done"], u + 1)
                multiply(scratch[:, j, :], PS[:, 2 * j, :], rstd[:, :]).then_inc(S["gate_scaled"], 1)
                dve.wait_ge(S["unit_done"], u + 2)
                multiply(scratch[:, 2 + j, :], PS[:, 2 * j + 1, :], rstd[:, :]).then_inc(S["up_scaled"], 1)
                dve.wait_ge(S["silu_done"], f + 1)
                dve.wait_ge(S["up_scaled"], f + 1)
                multiply(scratch[:, 2 + j, :], scratch[:, 2 + j, :], scratch[:, j, :]).then_inc(S["h_made"], 1)
                dve.wait_ge(S["h_hi_done"], f + 1)
                nc.vector.tensor_tensor(h_lo[:, F, :], scratch[:, 2 + j, :], h_hi[:, F, :].bitcast(F32),
                                        ALU.subtract).then_inc(S["h_lo_done"], 1)

            reciprocal_rms(FFN_STAT[n])
            with dve.Fori(0, FT // 2) as it:
                for j in range(2):
                    tile(2 * it + j, j)

        def residual(u0, per, factor, r, t, stat):
            if stat is not None:
                zero_ssq(stat)
            with dve.Fori(0, 2) as it:
                for j in range(4):
                    k = 4 * it + j
                    dve.wait_ge(S["unit_done"], 4 * per * it + (u0 + per * (j + 1)))
                    nc.vector.scalar_tensor_tensor(X[:, k, :], PS[:, j, :], factor, X[:, k, :],
                                                   ALU.mult, ALU.add).then_inc(S["x_updated"], 1)
                    if stat is not None:
                        dve.wait_ge(S["x_updated"], k + (DT * r + 1))
                        tail(k, j % 2, t, stat)

        def evacuate(dst, bank, factor):
            if factor == 1.0:
                return multiply(dst, PS[:, bank, :], rstd[:, :])
            return scale_two(dst, PS[:, bank, :], factor, rstd[:, :])

        def projection_1():
            reciprocal_rms(S_FFN1)
            nc.vector.memset(mask[0][:, :], 0.0).then_inc(S["mask_ready"], 1)
            dve.wait_ge(S["bias_in"], 16)
            nc.vector.memset(bias[0:CHUNK, :, 0:CHUNK], FAR).then_inc(S["bias_ready"], 1)
            dve.wait_ge(S["mask_ready"], 1)
            nc.vector.memset(mask[0][0:CHUNK, CHUNK:P], FAR).then_inc(S["mask_ready"], 1)
            dve.wait_ge(S["rope_in"], 16)
            rounds = 0
            for n, (what, t) in enumerate(PROJ):
                bank = n % 4
                factor = HD ** -0.5 if what in QUERY else 1.0
                dve.wait_ge(S["unit_done"], U_PROJ + n + 1)
                if n in ROPE:
                    k = ROPE.index(n)
                    evacuate(scratch[:, k % 2, :], bank, factor).then_inc(S["rope_scaled"], 1)
                    dve.wait_ge(S["rope_scaled"], k + 1)
                    dst = {KI: ki[:, :], QI: qi[:, t, :], KB: kb[:, :], QB: qb[:, t, :]}[what]
                    multiply(dst, scratch[:, k % 2, :], rope[:, 0, :])
                elif what == WI:
                    scale_two(scratch[0:8, 4, :], PS[0:8, bank, :], HEADS ** -0.5, rstd[0:8, :])\
                        .then_inc(S["wi_made"], 1)
                elif what in (VB, VA):
                    v = 0 if what == VB else 1 + t
                    if v >= 2:
                        dve.wait_ge(S["v_turned"], v - 1)
                    if v == 0:
                        dve.wait_ge(S["wt_turned"], 1)
                    evacuate(scratch[:, 4 + v % 2, :], bank, factor).then_inc(S["v_made"], 1)
                else:
                    evacuate((qa if what == QA else ka)[:, t, :], bank, factor).then_inc(S["plain_made"], 1)
                if n - 1 in ROPE:
                    finish_rope(n - 1)
                if n == 2:
                    dve.wait_ge(S["wt_turned"], 1)
                    nc.vector.tensor_copy(w_tok, PS[:, 4, 0:32]).then_inc(S["wt_copied"], 1)
                for m in index_steps(n):
                    add_index(m)
                if n >= TOP_FROM:
                    for _ in range(TOP_EACH):
                        if rounds < ROUNDS * (QT - 1):
                            select(rounds)
                            rounds += 1
            for k in range(rounds, ROUNDS * (QT - 1)):
                select(k)

        def finish_rope(n):
            k = ROPE.index(n)
            what, t = PROJ[n]
            dst = {KI: ki[:, :], QI: qi[:, t, :], KB: kb[:, :], QB: qb[:, t, :]}[what]
            dve.wait_ge(S["swap_done"], k + 1)
            multiply(scratch[:, 2 + k % 2, :], PS[:, 5, :], rope[:, 1, :]).then_inc(S["rope_sined"], 1)
            dve.wait_ge(S["rope_sined"], k + 1)
            nc.vector.tensor_tensor(dst, dst, scratch[:, 2 + k % 2, :], ALU.add).then_inc(S["rope_added"], 1)

        def add_index(m):
            i, h = INDEX[m]
            W = P * (i + 1)
            relu = scratch[:, 5 + m % 2, 0:W]
            weight = w_tok[:, 8 * i + h:8 * i + h + 1]
            dve.wait_ge(S["relu_done"], m + 1)
            if m == 0:
                dve.wait_ge(S["wt_copied"], 1)
            if h == 0:
                nc.vector.tensor_scalar(mask[i][:, :], relu, weight, None, ALU.mult).then_inc(S["idx_added"], 1)
            else:
                dve.wait_ge(S["idx_added"], m)
                nc.vector.scalar_tensor_tensor(mask[i][:, :], relu, weight, mask[i][:, :],
                                               ALU.mult, ALU.add).then_inc(S["idx_added"], 1)
            if h == HEADS - 1:
                dve.wait_ge(S["idx_added"], m + 1)
                nc.vector.memset(mask[i][0:CHUNK, W - CHUNK:W], OUTSIDE).then_inc(S["score_ready"], 1)

        def select(k):
            i, eight = 1 + k // ROUNDS, top8[:, 8 * (k % 2):8 * (k % 2) + 8]
            if k % ROUNDS == 0:
                dve.wait_ge(S["score_ready"], i)
            if k:
                dve.wait_ge(S["top_taken"], k)
            nc.vector.max(eight, mask[i][:, :]).then_inc(S["top_found"], 1)
            dve.wait_ge(S["top_found"], k + 1)
            nc.vector.match_replace(mask[i][:, :], eight, mask[i][:, :], TAKEN).then_inc(S["top_taken"], 1)
            if k % ROUNDS == ROUNDS - 1:
                dve.wait_ge(S["top_taken"], k + 1)
                nc.vector.tensor_scalar(mask[i][:, :], mask[i][:, :], TAKEN_BELOW, FAR, ALU.is_gt, ALU.mult)\
                    .then_inc(S["mask_ready"], 1)

        def attention_1():
            for m in range(len(STEPS) + 5):
                if m < len(STEPS):
                    br, i, h = STEPS[m]
                    W = P * (i + 1)
                    dve.wait_ge(S["s_done"], m + 1)
                    if m == 0:
                        dve.wait_ge(S["bias_ready"], 1)
                    if br == 1 and h == 0:
                        dve.wait_ge(S["mask_ready"], 2 + i)
                    if m >= 2:
                        dve.wait_ge(S["p_made"], m - 1)
                    add = bias[:, h, W - 1::-1] if br == 0 else mask[i][:, :]
                    nc.vector.tensor_tensor_reduce(scratch[:, 1 + m % 2, 0:W], PS[:, 4 + m % 2, 0:W], add,
                                                   -1.0, -FAR, ALU.add, ALU.min,
                                                   row_neg_max[:, m:m + 1]).then_inc(S["s_biased"], 1)
                if m % HEADS == 1 and m > HEADS:
                    g = m // HEADS - 1
                    dve.wait_ge(S["p_made"], HEADS * (g + 1))
                    nc.vector.reciprocal(row_inv, row_sum[:, HEADS * g:HEADS * (g + 1)]).then_inc(S["inv_made"], 1)
                    dve.wait_ge(S["inv_made"], g + 1)
                    dve.wait_ge(S["pv_done"], HEADS * (g + 1))
                    if g:
                        dve.wait_ge(S["o_turned"], g)
                    multiply(ssq[:, :].rearrange("p (h d) -> p h d", h=HEADS),
                             PS[:, g % 2, :].rearrange("p (h d) -> p h d", h=HEADS),
                             row_inv.unsqueeze(2).broadcast_to([P, HEADS, HD])).then_inc(S["o_normed"], 1)
                if m % HEADS == 4 and m > HEADS:
                    g = m // HEADS - 1
                    br, i = g // QT, g % QT
                    dve.wait_ge(S["o_hi_done"], g + 1)
                    nc.vector.tensor_tensor(o_lo[br][:, :, P * i:P * (i + 1)],
                                            PS[:, 2 + g % 2, :].rearrange("p (c n) -> p c n", c=4),
                                            o_hi[br][:, :, P * i:P * (i + 1)].bitcast(F32), ALU.subtract)\
                        .then_inc(S["o_lo_done"], 1)

        def merge():
            for n in range(DT):
                b = 4 * (n % 2)
                for g in range(2):
                    dve.wait_ge(S["unit_done"], U_GATE + 3 * n + g + 1)
                    multiply(scratch[:, 1 + g, :], PS[:, b + g, :], rstd[:, :]).then_inc(S["gate_in"], 1)
                dve.wait_ge(S["unit_done"], U_GATE + 3 * n + 3)
                for g in range(2):
                    dve.wait_ge(S["gate_sig"], 2 * n + g + 1)
                    multiply(scratch[:, 3 + g, :], PS[:, b + 2 + g, :], scratch[:, 1 + g, :])\
                        .then_inc(S["branch_gated"], 1)
                dve.wait_ge(S["branch_gated"], 2 * n + 2)
                nc.vector.tensor_tensor(scratch[:, 5 + n % 2, :], scratch[:, 3, :], scratch[:, 4, :], ALU.add)\
                    .then_inc(S["merged"], 1)
                dve.wait_ge(S["m_hi_done"], n + 1)
                nc.vector.tensor_tensor(m_lo[:, n, :], scratch[:, 5 + n % 2, :], m_hi[:, n, :].bitcast(F32),
                                        ALU.subtract).then_inc(S["m_lo_done"], 1)

        def projection_2():
            reciprocal_rms(S_FFN3)
            for n in range(PROJ_UNITS + 1):
                if n < 2 * DT:
                    dve.wait_ge(S["unit_done"], U_QKV + n + 1)
                    evacuate((sb_q, sb_k)[n // DT][:, n % DT, :], n % 4, 1.0).then_inc(S["plain_made"], 1)
                elif n < PROJ_UNITS:
                    v = 5 + n - 2 * DT
                    dve.wait_ge(S["unit_done"], U_QKV + n + 1)
                    dve.wait_ge(S["v_turned"], v - 1)
                    evacuate(scratch[:, 4 + n % 2, :], n % 4, 1.0).then_inc(S["v_made"], 1)
                v = n - 1
                if 0 <= v < 2 * DT:
                    which, t = v // DT, v % DT
                    inv = scratch[:, 2 + v % 2, :]
                    dve.wait_ge(S["qk_rms"], v + 1)
                    nc.vector.reciprocal(inv, inv).then_inc(S["qk_inv"], 1)
                    dve.wait_ge(S["qk_inv"], v + 1)
                    dst = (sb_q, sb_k)[which][:, t, :]
                    if v == 0:
                        dve.wait_ge(S["cols_ready"], 3)
                    scale_two(dst, dst, head_gain[:, 2 + which:3 + which], inv).then_inc(S["qk_normed"], 1)

        def stick_breaking():
            def split_out(hp):
                dve.wait_ge(S["so_hi_done"], hp + 1)
                nc.vector.tensor_tensor(so_lo[:, hp, :], PS[:, 3 + 4 * (hp % 2), :], so_hi[:, hp, :].bitcast(F32),
                                        ALU.subtract).then_inc(S["so_lo_done"], 1)

            for h in range(SB_HEADS):
                b = TOK * 4 * (h % 2)
                zs = ps_flat[:, b:b + SBW]
                if h >= 4 and h % 2 == 0:
                    split_out(h // 2 - 2)
                dve.wait_ge(S["l_done"], h + 1)
                if h >= 2:
                    dve.wait_ge(S["sb_pv"], h - 1)
                nc.vector.scalar_tensor_tensor(sb_s[h % 2][:, :], zs, 0.0, sb_e[h % 2][:, :], ALU.max, ALU.add)\
                    .then_inc(S["sp_done"], 1)
            split_out(SB_HEADS // 2 - 2)
            split_out(SB_HEADS // 2 - 1)

        nc.vector.memset(eps_col[:, :], EPS).then_inc(S["cols_ready"], 1)
        nc.vector.memset(one_col[:, :], 1.0).then_inc(S["cols_ready"], 1)
        zero_ssq(S_START)
        dve.wait_ge(S["gains_in"], 32)
        nc.vector.tensor_scalar(head_gain[:, 2:3], head_gain[:, 0:1], HD ** -0.5, None, ALU.mult)
        nc.vector.tensor_copy(head_gain[:, 3:4], head_gain[:, 1:2]).then_inc(S["cols_ready"], 1)
        for k in range(DT):
            dve.wait_ge(x_landed[k], 16)
            tail(k, k % 2, T_START, S_START)
        ffn_up(0)
        residual(FFN_BASE[0] + UP_UNITS, len(DOWN), 0.5, FFN_RES[0], T_FFN1, S_FFN1)
        projection_1()
        attention_1()
        merge()
        residual(U_OUT, 1, 1.0, MIX_RES[0], T_MIX1, S_MIX1)
        ffn_up(1)
        residual(FFN_BASE[1] + UP_UNITS, len(DOWN), 0.5, FFN_RES[1], None, S_FFN2)
        reciprocal_rms(S_FFN2)
        zero_ssq(S_FINAL)
        for k in range(DT):
            scale_two(X[:, k, :], X[:, k, :], gains[:, G_FINAL, k:k + 1], rstd[:, :]).then_inc(S["x_normed"], 1)
            dve.wait_ge(S["x_normed"], k + 1)
            tail(k, k % 2, T_FINAL, S_FINAL)
        ffn_up(2)
        residual(FFN_BASE[2] + UP_UNITS, len(DOWN), 0.5, FFN_RES[2], T_FFN3, S_FFN3)
        projection_2()
        stick_breaking()
        residual(U_SBO, 1, 1.0, MIX_RES[1], T_MIX2, S_MIX2)
        ffn_up(3)
        residual(FFN_BASE[3] + UP_UNITS, len(DOWN), 0.5, FFN_RES[3], None, None)


def index_steps(n):
    first = INDEX_EACH * (n - INDEX_FROM)
    return range(max(first, 0), max(min(first + INDEX_EACH, len(INDEX)), 0))


def _units(w, width=P):
    k, n = w.shape
    return w.reshape(k // P, P, n // P, P).transpose(2, 1, 0, 3)


def _ffn_units(w_in, w_out):
    up = _units(w_in).reshape(2, FT, P, UK, P).transpose(1, 0, 2, 3, 4).reshape(UP_UNITS, P, UK, P)
    down = np.pad(_units(w_out), ((0, 0), (0, 0), (0, len(DOWN) * UK - FT), (0, 0)))
    down = down.reshape(DT, P, len(DOWN), UK, P).transpose(0, 2, 1, 3, 4).reshape(DOWN_UNITS, P, UK, P)
    return [up, down]


def _mixer_units(w_in, w_a, w_b, w_out):
    width = HEADS * HD
    cut = np.cumsum([width, width, width, width, 2 * HD, 2 * HD, width, HD, HEADS, D])
    qa, ka, va, qb, kb, vb, qi, ki, wi, ga, gb = np.split(w_in, cut, axis=1)
    qb = qb.reshape(D, 2, 4, HD).transpose(0, 2, 1, 3).reshape(D, width)
    ki = np.concatenate([ki, ki], axis=1)
    wi = np.pad(wi, ((0, 0), (0, P - HEADS)))
    proj = [_units(np.ascontiguousarray(w)) for w in (ki, wi, qi, kb, vb, qb, qa, ka, va)]
    both = np.concatenate([_units(w_a), _units(w_b)], axis=2)
    gate = np.stack([_units(np.ascontiguousarray(ga)), _units(np.ascontiguousarray(gb)), both], axis=1)
    return proj + [gate.reshape(GATE_UNITS, P, UK, P), _units(w_out)]


def _constants():
    rows, cols = np.arange(P)[:, None], np.arange(P)[None, :]
    head = (rows // HD == cols // HD)
    rot = HD // 4
    d = np.arange(P) % HD
    partner = np.where(d < rot // 2, np.arange(P) + rot // 2, np.arange(P) - rot // 2)
    swap = (rows == partner[None, :]) & (d < rot)[None, :]
    upto = rows >= cols
    consts = np.stack([rows == cols, np.full((P, P), 1.0 / D), head / HD, swap, -1.0 * upto,
                       np.full((P, P), -1.0)], axis=1).astype(np.float32)
    freq = np.power(np.float32(500000.0), -np.arange(0, rot, 2, dtype=np.float32) / np.float32(rot))
    ang = np.arange(TOK, dtype=np.float32)[None, :] * freq.astype(np.float32)[:, None]
    cos, sin = np.ones((P, TOK), np.float32), np.zeros((P, TOK), np.float32)
    for p in range(P):
        if d[p] < rot:
            cos[p] = np.cos(ang[d[p] % (rot // 2)])
            sin[p] = np.sin(ang[d[p] % (rot // 2)]) * (-1.0 if d[p] < rot // 2 else 1.0)
    return consts, np.stack([rows == cols, FAR * upto], axis=1), np.stack([cos, sin], axis=1)


def kernel(**inputs):
    import ml_dtypes
    import concourse.bacc as bacc
    from concourse.bass_utils import run_bass_kernel_spmd

    i = {name: np.asarray(value) for name, value in inputs.items()}
    streams = _ffn_units(i["ffn1_w_in"][0], i["ffn1_w_out"][0])
    streams += _mixer_units(i["w_in"][0], i["w_branch_a"][0], i["w_branch_b"][0], i["w_out"][0])
    streams += _ffn_units(i["ffn2_w_in"][0], i["ffn2_w_out"][0])
    streams += _ffn_units(i["l0_ff1_w_in_2"], i["l0_ff1_w_out_2"])
    streams += [_units(i["l0_sb_w_qkv_2"]), _units(i["l0_sb_w_o_2"])]
    streams += _ffn_units(i["l0_ff2_w_in_2"], i["l0_ff2_w_out_2"])
    gain = np.stack([i["n1_g"][0], i["n2_g"][0], i["n3_g"][0], i["l0_ff1_norm_2"], i["l0_mix_norm_2"],
                     i["l0_ff2_norm_2"], i["nf_g"]])
    rel = i["rel_bias"][0]
    rel = np.pad(rel, ((0, 0), (0, TOK + P - rel.shape[1])), mode="edge")
    consts, consts_b, ropes = _constants()
    q_gain, k_gain = i["l0_sb_q_norm_2"], i["l0_sb_k_norm_2"]
    arrays = {
        "weights": np.concatenate(streams, axis=0),
        "consts": consts,
        "consts_b": consts_b.astype(ml_dtypes.bfloat16),
        "ropes": ropes,
        "rel": np.ascontiguousarray(rel),
        "gain_cols": np.ascontiguousarray(gain.reshape(7, DT, P).transpose(2, 0, 1)),
        "head_gains": np.stack([np.concatenate([q_gain, q_gain]), np.concatenate([k_gain, k_gain])], axis=1),
        "x_t": np.ascontiguousarray(i["x"][0].T.reshape(DT, P, TOK).transpose(1, 0, 2)),
    }
    nc = bacc.Bacc("TRN2", target_bir_lowering=False, num_devices=1)
    args = [nc.dram_tensor(name, v.shape, mybir.dt.from_np(v.dtype), kind="ExternalInput").ap()
            for name, v in arrays.items()]
    args.append(nc.dram_tensor("out_t", (P, DT, TOK), F32, kind="ExternalOutput").ap())
    program(nc, *args)
    r = run_bass_kernel_spmd(nc, [arrays], core_ids=[0])
    got = np.asarray(r.results[0]["out_t"])
    return np.ascontiguousarray(got.transpose(2, 1, 0).reshape(1, TOK, D))
```

```python
from contextlib import ExitStack

import numpy as np
import concourse.bass as bass
from concourse import mybir

F32, F32R, BF16 = mybir.dt.float32, mybir.dt.float32r, mybir.dt.bfloat16
ACT, ALU = mybir.ActivationFunctionType, mybir.AluOpType

P = 128
TOK = 512
D = 1024
DT = D // P
FT = 2816 // P
QT = TOK // P
HD = 64
HEADS = 8
SB_HEADS = 16
CHUNK = 64
TOPK = min(256, TOK // 4)
EPS = 1e-6
NSLOT = 4
AHEAD = 2
UK = 8
DOWN = [(0, 8), (8, 16), (16, FT)]

UP_UNITS, DOWN_UNITS = 2 * FT, len(DOWN) * DT
PROJ_UNITS, GATE_UNITS, OUT_UNITS = 24, 3 * DT, DT
FFN_UNITS = UP_UNITS + DOWN_UNITS
U_FFN1 = 0
U_PROJ = U_FFN1 + FFN_UNITS
U_GATE = U_PROJ + PROJ_UNITS
U_OUT = U_GATE + GATE_UNITS
U_FFN2 = U_OUT + OUT_UNITS
U_FFN3 = U_FFN2 + FFN_UNITS
U_QKV = U_FFN3 + FFN_UNITS
U_SBO = U_QKV + PROJ_UNITS
U_FFN4 = U_SBO + OUT_UNITS
UNITS = U_FFN4 + FFN_UNITS
FFN_BASE = [U_FFN1, U_FFN2, U_FFN3, U_FFN4]

FFN_RES, MIX_RES = [0, 2, 3, 5], [1, 4]
S_START, S_FFN1, S_MIX1, S_FINAL, S_FFN3, S_MIX2 = range(6)
T_START, T_FFN1, T_MIX1, T_FINAL, T_FFN3, T_MIX2 = range(6)
G_FINAL = 6
FFN_STAT = [S_START, S_MIX1, S_FINAL, S_MIX2]
FFN_INPUT = [T_START, T_MIX1, T_FINAL, T_MIX2]

KI, WI, QI, KB, VB, QB, QA, KA, VA = range(9)
PROJ = [(KI, 0), (WI, 0)] + [(what, t) for what in (QI, QA, KA, VA) for t in range(4)] + [
    (KB, 0), (VB, 0), (QB, 0), (QB, 1), (QB, 2), (QB, 3)]
PROJ_ALONE = 18
ROPE = [n for n, (what, _) in enumerate(PROJ) if what in (KI, QI, KB, QB)]
VALUES = [n for n, (what, _) in enumerate(PROJ) if what in (VA, VB)]
QUERY = (QI, QB, QA)
INDEX = [(i, h) for i in range(1, QT) for h in range(HEADS)]
INDEX_FROM, INDEX_EACH = 7, 3
ROUNDS = TOPK // 8
TOP_FROM, TOP_EACH = 10, 4
STEPS = [(br, i, h) for br in range(2) for i in range(QT) for h in range(HEADS)]
HALF = len(STEPS) // 2
GROUPS = 2 * QT
VALUE_BUFFER = (0, 2, 0, 2, 0)
LAST_STEP = len(STEPS) + 3
BETWEEN = len(PROJ) - PROJ_ALONE + 2 * DT
PROJ_STEPS = HALF - 2


def filled(m):
    if m < 0:
        return 0
    first = (len(PROJ) - PROJ_ALONE) * UK
    if m < PROJ_STEPS:
        return first * (m + 1) // PROJ_STEPS
    return first + 2 * DT * UK * (m + 1 - PROJ_STEPS) // (LAST_STEP + 1 - PROJ_STEPS)


STARTS = [next(m for m in range(LAST_STEP + 1) if filled(m) > UK * n) for n in range(BETWEEN)]
ENDS = [next(m for m in range(LAST_STEP + 1) if filled(m) >= UK * (n + 1)) for n in range(BETWEEN)]

FILL = [(9, 3), (9, 3)]

FAR = -1e30
OUTSIDE = -3.0e38
TAKEN = -3.2e38
TAKEN_BELOW = -3.1e38


def program(nc, weights, consts, consts_b, ropes, rel, gain_cols, head_gains, x, out):
    with ExitStack() as ctx:
        build(nc, ctx, weights, consts, consts_b, ropes, rel, gain_cols, head_gains, x, out)


def build(nc, ctx, weights, consts, consts_b, ropes, rel, gain_cols, head_gains, x, out):
    size = {F32: 4, F32R: 4, BF16: 2}
    fixed = [(nc.sbuf_base + 63) // 64 * 64]

    def place(name, shape, dt=F32, where=fixed):
        tensor = nc.alloc_sbuf_tensor_at(name, shape, dt, offset=where[0])
        where[0] += (int(np.prod(shape[1:])) * size[dt] + 31) // 32 * 32
        assert where[0] <= nc.sbuf_usable_end
        return tensor

    X = place("x_sb", [P, DT, TOK])
    xn_hi = place("xn_hi", [P, DT, TOK], F32R)
    xn_lo = place("xn_lo", [P, DT, TOK], F32R)
    raw = [place(f"raw{s}", [P, UK, P]) for s in range(NSLOT)]
    w_hi = [place(f"w_hi{s}", [P, UK, P], F32R) for s in range(NSLOT)]
    w_lo = [place(f"w_lo{s}", [P, UK, P], F32R) for s in range(NSLOT)]
    rstd = place("rstd", [P, TOK])
    ssq = place("ssq", [P, TOK])
    const = place("const", [P, 6, P])
    ident, mean_all, mean_head, swap = (const[:, n, :] for n in range(4))
    const_r = place("const_r", [P, 2, P], F32R)
    minus_upto_r, minus_ones_r = const_r[:, 0, :], const_r[:, 1, :]
    const_b = place("const_b", [P, 2, P], BF16)
    ident_b, far_b = const_b[:, 0, :], const_b[:, 1, :]
    gains = place("gains", [P, 7, DT])
    head_gain = place("head_gain", [P, 4])
    eps_col = place("eps_col", [P, 1])
    one_col = place("one_col", [P, 1])
    small = place("small", [P, 232])
    w_tok = small[:, 0:32]
    top8 = small[:, 32:48]
    row_sum, row_neg_max, row_inv = small[:, 96:160], small[:, 160:224], small[:, 224:232]
    region = fixed[0]

    at = [region]
    h_hi = place("h_hi", [P, FT, TOK], F32R, at)
    h_lo = place("h_lo", [P, FT, TOK], F32R, at)
    scratch = place("scratch", [P, 7, TOK], F32, at)

    at = [region]
    qa = place("qa", [P, 4, TOK], F32, at)
    ka = place("ka", [P, 4, TOK], F32, at)
    bias = place("bias", [P, HEADS, TOK], F32, at)
    qb = place("qb", [P, 4, TOK], F32, at)
    kb = place("kb", [P, TOK], F32, at)
    va = place("va", [P, QT, 512], F32, at)
    vb = place("vb", [P, QT, P], F32, at)
    mask = [place(f"mask{i}", [P, P * (i + 1)], F32, at) for i in range(QT)]
    over_oa = [at[0]]
    o_hi = [place("oa_hi", [P, 4, TOK], F32R, at)]
    o_lo = [place("oa_lo", [P, 4, TOK], F32R, at)]
    over_ob = [at[0]]
    o_hi += [place("ob_hi", [P, 4, TOK], F32R, at)]
    o_lo += [place("ob_lo", [P, 4, TOK], F32R, at)]
    assert at[0] <= region + 2 * FT * TOK * 4 + TOK * 4
    qi = place("qi", [P, 4, TOK], F32, over_oa)
    ki = place("ki", [P, TOK], F32, over_oa)
    rope = place("rope", [P, 2, TOK], F32, over_ob)
    at = [region]
    gates = place("gates", [P, 2 * DT, TOK], F32, at)
    at = [region + 12 * TOK * 4]
    m_hi = place("m_hi", [P, DT, TOK], F32R, at)
    m_lo = place("m_lo", [P, DT, TOK], F32R, at)

    def gate(j):
        return gates[:, (j + 12) % 16, :]

    width = [TOK - P * j for j in range(QT)]
    col = [0, width[0], width[0] + width[1] + width[3], width[0] + width[1]]
    SBW = sum(width)
    at = [region]
    sb_q = [place(f"sb_q_{part}", [P, 2, TOK], F32R, at) for part in ("hi", "lo")]
    sb_k = [place(f"sb_k_{part}", [P, 2, TOK], F32R, at) for part in ("hi", "lo")]
    sb_v = [place(f"sb_v_{part}", [P, 2, QT, P], F32R, at) for part in ("hi", "lo")]
    so_hi = place("so_hi", [P, DT, TOK], F32R, at)
    so_lo = place("so_lo", [P, DT, TOK], F32R, at)
    sb_e = place("sb_e", [P, SBW], F32, at)
    sp = [place(f"sp_{part}", [P, SBW], F32R, at) for part in ("hi", "lo")]
    sb_w = [place(f"sb_w_{part}", [P, SBW], F32R, at) for part in ("hi", "lo")]
    assert at[0] <= region + 2 * FT * TOK * 4

    PS = ctx.enter_context(nc.psum_tensor("ps", [P, 8, TOK], F32))
    ps_flat = PS[:, :, :].rearrange("p b n -> p (b n)")

    names = """hi_done lo_done unit_done consts_in gains_in rope_in bias_in cols_ready
        x_updated x_normed sq_done ssq_zeroed ssq_done ms_done rms_done rstd_ready
        sq2_done ssq2_zeroed ssq2_done ms2_done r1_made m2_scaled rms2_done r2_made
        xg_done xn_hi_done xn_lo_done gate_scaled silu_done up_scaled h_made h_hi_done h_lo_done
        plain_made rope_scaled swap_done rope_sined rope_added
        wi_made wt_turned wt_copied v_made v_turned v_copied
        idx_done relu_done idx_added score_ready top_found top_taken mask_ready bias_ready
        s_done s_biased p_made p_turned pt_copied pv_done inv_made o_normed o_turned o_hi_done
        o_lo_done gate_in gate_sig branch_gated merged m_hi_done m_lo_done
        qk_made qk_sq qk_ms qk_ln qk_inv qk_normed qk_hi qk_split sv_made sv_turned sv_hi sv_split
        z_done abs_done e_done l_done sp_done sp_hi_done sp_split cum_done
        w_done w_hi_done w_split sb_pv so_hi_done so_lo_done stored""".split()
    S = {name: ctx.enter_context(nc.semaphore(name)) for name in names}
    raw_landed = [ctx.enter_context(nc.semaphore(f"raw_landed{s}")) for s in range(NSLOT)]
    x_landed = [ctx.enter_context(nc.semaphore(f"x_landed{k}")) for k in range(DT)]

    def evacuated_1(n):
        what, t = PROJ[n]
        if n in ROPE:
            return S["rope_scaled"], ROPE.index(n) + 1
        if what == WI:
            return S["wi_made"], 1
        if n in VALUES:
            return S["v_made"], VALUES.index(n) + 1
        return S["plain_made"], 1 + t + 4 * (what == KA)

    def evacuated_between(n):
        if n < len(PROJ) - PROJ_ALONE:
            return evacuated_1(PROJ_ALONE + n)
        return S["gate_in"], n + PROJ_ALONE - len(PROJ) + 1

    def unit_between(n):
        return U_PROJ + PROJ_ALONE + n

    def evacuated_2(n):
        t, c = divmod(n, 3)
        return (S["sv_made"], t + 1) if c == 2 else (S["qk_made"], 2 * t + c + 1)

    block = ctx.enter_context(nc.Block())

    @block.sync
    def _(sp):
        def load(u, s):
            sp.dma_start(raw[s][:, :, :], weights[u]).then_inc(raw_landed[s], 16)

        for s in range(NSLOT):
            load(s, s)
        with sp.Fori(1, UNITS // NSLOT) as it:
            for s in range(NSLOT):
                sp.wait_ge(S["lo_done"], NSLOT * it + (s + 1 - NSLOT))
                load(NSLOT * it + s, s)
        for n in range(DT):
            sp.wait_ge(S["x_updated"], DT * FFN_RES[3] + n + 1)
            sp.dma_start(out[:, n, :], X[:, n, :]).then_inc(S["stored"], 16)
        sp.wait_ge(S["stored"], 16 * DT)

    @block.gpsimd
    def _(pool):
        with pool.Fori(0, UNITS // NSLOT) as it:
            for s in range(NSLOT):
                pool.wait_ge(S["hi_done"], NSLOT * it + (s + 1))
                nc.gpsimd.tensor_tensor(w_lo[s][:, :, :], raw[s][:, :, :], w_hi[s][:, :, :].bitcast(F32),
                                        ALU.subtract).then_inc(S["lo_done"], 1)

    @block.tensor
    def _(pe):
        def unit(u, s, outs, tiles, before=None, start=True, stop=True, part=None):
            k0, k1 = part or (0, len(tiles))
            if k0 == 0:
                pe.wait_ge(S["lo_done"], u + 1)
            for k in range(k0, k1):
                hi, lo = tiles[k]
                if before:
                    before(k)
                opens = start and (k == 0 or outs[k] != outs[k - 1])
                ends = stop and (k == len(tiles) - 1 or outs[k] != outs[k + 1])
                to = PS[:, outs[k], :]
                pe.matmul(to, w_hi[s][:, k, :], hi, start=opens, stop=False)
                pe.matmul(to, w_hi[s][:, k, :], lo, start=False, stop=False)
                last = pe.matmul(to, w_lo[s][:, k, :], hi, start=False, stop=ends)
            if k1 == len(tiles):
                last.then_inc(S["unit_done"], 1)

        xn = [(xn_hi[:, k, :], xn_lo[:, k, :]) for k in range(DT)]

        def mean_square(stat):
            pe.wait_ge(S["ssq_done"], DT * (stat + 1))
            pe.matmul(PS[:, mean_bank(stat), :], mean_all, ssq[:, :], start=True, stop=True)\
              .then_inc(S["ms_done"], 1)

        def first_unit_waits(t, stat):
            def before(k):
                if k == DT - 1:
                    mean_square(stat)
                    if stat == S_FINAL:
                        pe.wait_ge(S["ssq2_done"], DT)
                        pe.matmul(PS[:, 5, :], mean_all, scratch[:, 0, :], start=True, stop=True)\
                          .then_inc(S["ms2_done"], 1)
                pe.wait_ge(S["xn_lo_done"], DT * t + k + 1)
            return before

        def ffn_up(n):
            def tile(F, j, before=None):
                u = FFN_BASE[n] + 2 * F
                for g in range(2):
                    unit(u + g, 2 * j + g, [2 * j + g] * UK, xn, before if g == 0 else None)

            if n == 0:
                pe.wait_ge(S["consts_in"], 32)
            else:
                pe.wait_ge(S["x_updated"], DT * FFN_RES[n])
            for j in range(2):
                tile(j, j, first_unit_waits(FFN_INPUT[n], FFN_STAT[n]) if j == 0 else None)
            with pe.Fori(1, FT // 2) as it:
                for j in range(2):
                    pe.wait_ge(S["h_made"], 2 * it + (FT * n + j - 1))
                    tile(2 * it + j, j)

        def residual(u0, kinds, tiles, ready, freed, freed0):
            def body(it):
                for j in range(4):
                    pe.wait_ge(freed, 4 * it + (freed0 + j - 3))
                    for c, (k0, k1) in enumerate(kinds):
                        n_u = 4 * len(kinds)
                        at_unit = j * len(kinds) + c
                        unit(n_u * it + (u0 + at_unit), at_unit % NSLOT, [j] * (k1 - k0), tiles[k0:k1],
                             (lambda k, k0=k0: ready(k0 + k)) if j == 0 else None,
                             start=(c == 0), stop=(c == len(kinds) - 1))
            with pe.Fori(0, 2) as it:
                body(it)

        def ffn_down(n):
            def ready(k):
                if k == 0:
                    pe.wait_ge(S["h_lo_done"], FT * n + FT - 1)
                if k == FT - 1:
                    pe.wait_ge(S["h_lo_done"], FT * n + FT)

            pe.wait_ge(S["h_made"], FT * n + FT - 1)
            freed, freed0 = (S["x_updated"], DT * FFN_RES[n]) if n else (S["ssq_done"], DT * S_FFN1)
            residual(FFN_BASE[n] + UP_UNITS, DOWN,
                     [(h_hi[:, k, :], h_lo[:, k, :]) for k in range(FT)], ready, freed, freed0)

        def projection_1():
            pe.wait_ge(S["x_updated"], DT * (FFN_RES[0] + 1))
            for n in range(PROJ_ALONE):
                if n >= 4:
                    pe.wait_ge(*evacuated_1(n - 4))
                unit(U_PROJ + n, n % NSLOT, [n % 4] * UK, xn,
                     first_unit_waits(T_FFN1, S_FFN1) if n == 0 else None)
                turn_1(n - 1)
                if n == 2:
                    pe.wait_ge(S["wi_made"], 1)
                    for i in range(QT):
                        last = pe.transpose(PS[:, 4, 8 * i:8 * i + 8], scratch[0:8, 2, P * i:P * (i + 1)],
                                            ident[0:8, 0:8])
                    last.then_inc(S["wt_turned"], 1)
                for m in index_steps(n):
                    i, h = INDEX[m]
                    if m == 0:
                        pe.wait_ge(S["rope_added"], 5)
                    if m == 1:
                        pe.wait_ge(S["rope_sined"], 5)
                    if m >= 2:
                        pe.wait_ge(S["relu_done"], m - 1)
                    r = HD * (h % 2)
                    pe.matmul(PS[:, 5 + m % 2, 0:P * (i + 1)], qi[r:r + HD, h // 2, P * i:P * (i + 1)],
                              ki[r:r + HD, 0:P * (i + 1)], start=True, stop=True).then_inc(S["idx_done"], 1)
            turn_1(PROJ_ALONE - 1)

        def turn_1(n):
            if n < 0:
                return
            if n in ROPE:
                k = ROPE.index(n)
                pe.wait_ge(S["rope_scaled"], k + 1)
                if k == 5:
                    pe.wait_ge(S["v_copied"], 4)
                elif k:
                    pe.wait_ge(S["rope_sined"], k)
                if k == 6:
                    pe.wait_ge(S["v_copied"], 5)
                pe.matmul(PS[:, 7, :], swap, scratch[:, 5, :], start=True, stop=True)\
                  .then_inc(S["swap_done"], 1)
            if n in VALUES:
                v = VALUES.index(n)
                pe.wait_ge(S["v_made"], v + 1)
                if v == 4:
                    pe.wait_ge(S["rope_sined"], 6)
                elif v:
                    pe.wait_ge(S["v_copied"], v)
                for i in range(QT):
                    last = pe.transpose(PS[:, 7, P * i:P * (i + 1)],
                                        scratch[:, VALUE_BUFFER[v], P * i:P * (i + 1)], ident)
                last.then_inc(S["v_turned"], 1)

        def between(m):
            for g in range(filled(m - 1), filled(m)):
                n, k = divmod(g, UK)
                u = unit_between(n)
                if k == 0 and n >= 2:
                    pe.wait_ge(*evacuated_between(n - 2))
                unit(u, u % NSLOT, [2 + n % 2] * UK, xn, part=(k, k + 1))

        def attention_1():
            pe.wait_ge(S["plain_made"], 8)
            pe.wait_ge(S["v_copied"], 4)
            pe.wait_ge(S["relu_done"], len(INDEX))
            for m in range(LAST_STEP + 1):
                if m < len(STEPS):
                    br, i, h = STEPS[m]
                    t, r = (h // 2, HD * (h % 2)) if br == 0 else (h % 4, HD * (h // 4))
                    q = (qa, qb)[br][r:r + HD, t, P * i:P * (i + 1)]
                    k = ka[r:r + HD, t, 0:P * (i + 1)] if br == 0 else kb[r:r + HD, 0:P * (i + 1)]
                    if br == 1 and i == 0 and h < 4:
                        pe.wait_ge(S["rope_added"], 7 + h)
                    if m >= 2:
                        pe.wait_ge(S["s_biased"], m - 1)
                    pe.matmul(PS[:, 4 + m % 2, 0:P * (i + 1)], q, k, start=True, stop=True)\
                      .then_inc(S["s_done"], 1)
                between(m)
                if 1 <= m <= len(STEPS):
                    n = m - 1
                    br, i, h = STEPS[n]
                    pe.wait_ge(S["p_made"], n + 1)
                    if n >= 1:
                        pe.wait_ge(S["pt_copied"], n)
                    for j in range(i + 1):
                        last = pe.transpose(PS[:, 6, P * j:P * (j + 1)],
                                            scratch[:, 2 + n % 2, P * j:P * (j + 1)], ident)
                    last.then_inc(S["p_turned"], 1)
                if 2 <= m < len(STEPS) + 2:
                    n = m - 2
                    br, i, h = STEPS[n]
                    group = n // HEADS
                    pe.wait_ge(S["pt_copied"], n + 1)
                    if h == 0 and group >= 2:
                        pe.wait_ge(S["o_lo_done"], group - 1)
                    if n == HALF:
                        pe.wait_ge(S["v_copied"], 5)
                    for j in range(i + 1):
                        v = va[:, j, HD * h:HD * (h + 1)] if br == 0 else vb[:, j, HD * (h // 4):HD * (h // 4 + 1)]
                        last = pe.matmul(PS[:, group % 2, HD * h:HD * (h + 1)],
                                         scratch[:, 4, P * j:P * (j + 1)], v,
                                         start=(j == 0), stop=(j == i))
                    last.then_inc(S["pv_done"], 1)
                if m % HEADS == 3 and m > HEADS:
                    g = m // HEADS - 1
                    pe.wait_ge(S["o_normed"], g + 1)
                    for c in range(4):
                        last = pe.transpose(PS[:, g % 2, P * c:P * (c + 1)],
                                            ssq[:, P * c:P * (c + 1)], ident)
                    last.then_inc(S["o_turned"], 1)
                if m - 2 in ENDS and ENDS.index(m - 2) < len(PROJ) - PROJ_ALONE:
                    turn_1(PROJ_ALONE + ENDS.index(m - 2))

        def merge():
            pe.wait_ge(S["o_lo_done"], GROUPS)
            o = [(o_hi[br][:, k, :], o_lo[br][:, k, :]) for br in range(2) for k in range(4)]
            for n in range(DT):
                b, u = 4 * (n % 2), U_GATE + 2 * DT + n
                if n >= 2:
                    pe.wait_ge(S["merged"], n - 1)
                unit(u, u % NSLOT, [b] * 4 + [b + 1] * 4, o)

        def mixer_out_1():
            pe.wait_ge(S["gate_in"], 2 * DT)
            pe.wait_ge(S["merged"], DT - 1)
            residual(U_OUT, [(0, DT)], [(m_hi[:, k, :], m_lo[:, k, :]) for k in range(DT)],
                     lambda k: pe.wait_ge(S["m_lo_done"], k + 1), S["x_updated"], DT * MIX_RES[0])

        def project(k0, k1):
            for g in range(k0, k1):
                n, k = divmod(g, UK)
                if k == 0 and n >= 2:
                    pe.wait_ge(*evacuated_2(n - 2))
                unit(U_QKV + n, n % NSLOT, [4 + n % 2] * UK, xn,
                     first_unit_waits(T_FFN3, S_FFN3) if n == 0 else None, part=(k, k + 1))

        def head_mean_square(t, c):
            pe.wait_ge(S["qk_sq"], 2 * t + c + 1)
            if t == 0 and c == 0:
                pe.wait_ge(S["rms_done"], S_FFN3 + 1)
            if t and c == 0:
                pe.wait_ge(S["sv_split"], t)
            if t and c == 1:
                pe.wait_ge(S["qk_ln"], 2 * t)
            pe.matmul(PS[:, 6 + c, :], mean_head, scratch[:, 2 + c, :], start=True, stop=True)\
              .then_inc(S["qk_ms"], 1)

        def turn_values(t):
            pe.wait_ge(S["sv_made"], t + 1)
            pe.wait_ge(S["qk_ln"], 2 * t + 1)
            for i in range(QT):
                last = pe.transpose(PS[:, 6, P * i:P * (i + 1)], scratch[:, 6, P * i:P * (i + 1)], ident)
            last.then_inc(S["sv_turned"], 1)

        def three(out, a, b, start):
            pe.matmul(out, a[0], b[0], start=start, stop=False, skip_group_check=True)
            pe.matmul(out, a[0], b[1], start=False, stop=False, skip_group_check=True)
            return pe.matmul(out, a[1], b[0], start=False, stop=True, skip_group_check=True)

        def stick_scores(h):
            r, b = HD * (h % 2), h // 2 % 2
            pe.wait_ge(S["qk_split"], 2 * (h // 2) + 2)
            if h:
                pe.wait_ge(S["w_done"], h)
            for j in range(QT):
                three(ps_flat[:, col[j]:col[j] + width[j]],
                      [k[r:r + HD, b, P * j:P * (j + 1)] for k in sb_k],
                      [q[r:r + HD, b, P * j:TOK] for q in sb_q], j < 3)
            for j in range(QT):
                last = pe.matmul(ps_flat[:, col[j]:col[j] + P], ident_b, far_b,
                                 start=False, stop=True, skip_group_check=True)
            last.then_inc(S["z_done"], 1)

        def cumulate(h):
            pe.wait_ge(S["sp_split"], h + 1)
            for j in range(QT):
                for k in range(j, QT):
                    to = col[j] + P * (k - j)
                    for part in sp:
                        last = pe.matmul(ps_flat[:, to:to + width[k]], (minus_upto_r if k == j else minus_ones_r),
                                         part[:, col[k]:col[k] + width[k]],
                                         start=False, stop=True, skip_group_check=True)
            last.then_inc(S["cum_done"], 1)

        def weigh(h):
            pe.wait_ge(S["w_split"], h + 1)
            pe.wait_ge(S["sv_split"], h // 2 + 1)
            if h:
                pe.wait_ge(S["so_lo_done"], h)
            for j in range(QT):
                last = three(PS[:, 3, P * j:TOK], [v[:, h // 2 % 2, j, :] for v in sb_v],
                             [w[:, col[j]:col[j] + width[j]] for w in sb_w], j == 0)
            last.then_inc(S["sb_pv"], 1)

        so = [(so_hi[:, k, :], so_lo[:, k, :]) for k in range(DT)]

        def out_part(n, k0, k1):
            unit(U_SBO + n, n % NSLOT, [(n + 4) % 8] * DT, so,
                 lambda k: pe.wait_ge(S["so_lo_done"], 2 * k + 2), part=(k0, k1))

        def mixer_2():
            pairs = SB_HEADS // 2
            pe.wait_ge(S["x_updated"], DT * (FFN_RES[2] + 1))
            project(0, 2 * UK)
            head_mean_square(0, 0)
            project(2 * UK, 3 * UK)
            head_mean_square(0, 1)
            for h in range(SB_HEADS):
                t, odd = divmod(h, 2)
                at = (3 * (t + 1)) * UK + 12 * odd
                before, behind = FILL[odd]
                stick_scores(h)
                if not odd:
                    turn_values(t)
                if t + 1 < pairs:
                    if odd:
                        project(at, at + 8)
                        head_mean_square(t + 1, 1)
                        project(at + 8, at + before)
                    else:
                        project(at, at + before)
                else:
                    if h == SB_HEADS - 2:
                        pe.wait_ge(*evacuated_2(3 * pairs - 1))
                        pe.wait_ge(S["sv_split"], pairs)
                    for n in (0, 1) if not odd else (2, 3):
                        out_part(n, 0, pairs - 2)
                if h:
                    weigh(h - 1)
                cumulate(h)
                if t + 1 < pairs:
                    project(at + before, at + before + behind)
                    if not odd:
                        head_mean_square(t + 1, 0)
            for n in range(4):
                out_part(n, pairs - 2, pairs - 1)
            weigh(SB_HEADS - 1)
            for n in range(4):
                out_part(n, pairs - 1, pairs)
            for n in range(4, DT):
                out_part(n, 0, DT)

        ffn_up(0)
        ffn_down(0)
        projection_1()
        attention_1()
        merge()
        mixer_out_1()
        ffn_up(1)
        ffn_down(1)
        ffn_up(2)
        ffn_down(2)
        mixer_2()
        ffn_up(3)
        ffn_down(3)

    @block.scalar
    def _(act):
        for k in range(DT):
            act.dma_start(X[:, k, :], x[:, k, :]).then_inc(x_landed[k], 16)
        act.dma_start(gains[:, :, :], gain_cols).then_inc(S["gains_in"], 16)
        act.dma_start(head_gain[:, 0:2], head_gains).then_inc(S["gains_in"], 16)
        act.dma_start(const[:, :, :], consts).then_inc(S["consts_in"], 16)
        act.dma_start(const_b[:, :, :], consts_b).then_inc(S["consts_in"], 16)
        act.wait_ge(S["cols_ready"], 2)

        def copy(dst, src):
            return nc.scalar.activation(dst, src, ACT.Copy)

        def round_weights(u, s, turn):
            act.wait_ge(raw_landed[s], 16 * turn + 16)
            if not (isinstance(u, int) and u < NSLOT):
                act.wait_ge(S["unit_done"], u + (1 - NSLOT))
            copy(w_hi[s][:, :, :], raw[s][:, :, :]).then_inc(S["hi_done"], 1)

        def ahead(u):
            if u + AHEAD < UNITS:
                round_weights(u + AHEAD, (u + AHEAD) % NSLOT, (u + AHEAD) // NSLOT)

        def ahead_in_loop(it, per, u0, j):
            v = u0 + j + AHEAD
            round_weights(per * it + v, v % NSLOT, (per // NSLOT) * it + v // NSLOT)

        def root_mean_square(stat):
            act.wait_ge(S["ms_done"], stat + 1)
            nc.scalar.activation(scratch[:, 6, :], PS[:, mean_bank(stat), :], ACT.Sqrt, bias=eps_col[:, 0:1])\
              .then_inc(S["rms_done"], 1)
            if stat == S_FINAL:
                act.wait_ge(S["m2_scaled"], 1)
                nc.scalar.activation(scratch[:, 5, :], scratch[:, 4, :], ACT.Sqrt, bias=eps_col[:, 0:1])\
                  .then_inc(S["rms2_done"], 1)

        def square(k, b, stat, n_before):
            if not isinstance(n_before, int) or n_before >= 2:
                act.wait_ge(S["ssq_done"], n_before + (DT * stat - 1))
            nc.scalar.activation(scratch[:, 4 + b, :], X[:, k, :], ACT.Square).then_inc(S["sq_done"], 1)
            if stat == S_FINAL:
                act.wait_ge(S["ssq2_done"], n_before)
                nc.scalar.activation(scratch[:, 1, :], X[:, k, :], ACT.Square,
                                     scale=gains[:, G_FINAL, bass.ds(k, 1)]).then_inc(S["sq2_done"], 1)

        def round_input(k, b, t):
            act.wait_ge(S["xg_done"], k + (DT * t + 1))
            copy(xn_hi[:, k, :], scratch[:, 2 + b, :]).then_inc(S["xn_hi_done"], 1)

        def ffn_up(n):
            def tile(F, j, first=False):
                u = FFN_BASE[n] + 2 * F if isinstance(F, int) else None
                if first:
                    ahead(u)
                    root_mean_square(FFN_STAT[n])
                    ahead(u + 1)
                elif u is not None:
                    ahead(u)
                    ahead(u + 1)
                f = FT * n + F if isinstance(F, int) else F + FT * n
                act.wait_ge(S["gate_scaled"], f + 1)
                nc.scalar.activation(scratch[:, j, :], scratch[:, j, :], ACT.Silu).then_inc(S["silu_done"], 1)
                act.wait_ge(S["h_made"], f + 1)
                copy(h_hi[:, F, :], scratch[:, 2 + j, :]).then_inc(S["h_hi_done"], 1)

            tile(0, 0, first=True)
            tile(1, 1)
            with act.Fori(1, FT // 2) as it:
                for j in range(2):
                    ahead_in_loop(it, 4, FFN_BASE[n], 2 * j)
                    ahead_in_loop(it, 4, FFN_BASE[n], 2 * j + 1)
                    tile(2 * it + j, j)

        def residual(u0, per, r, t, stat):
            with act.Fori(0, 2) as it:
                for j in range(4):
                    for c in range(per):
                        ahead_in_loop(it, 4 * per, u0, j * per + c)
                    tail(4 * it + j, j % 2, r, t, stat)

        def tail(k, b, r, t, stat):
            act.wait_ge(S["x_updated"], k + (DT * r + 1))
            square(k, b, stat, k)
            round_input(k, b, t)

        def projection_1():
            act.wait_ge(S["unit_done"], U_PROJ)
            act.dma_start(rope[:, :, :], ropes).then_inc(S["rope_in"], 16)
            runs = bass.AP(rel.tensor, 1, [[1, P], [rel.shape[1], HEADS], [1, TOK]])
            act.dma_start(bias[:, :, :], runs).then_inc(S["bias_in"], 16)
            for n in range(PROJ_ALONE):
                ahead(U_PROJ + n)
                if n == 0:
                    root_mean_square(S_FFN1)
                copy_values(n - 1)
                for m in index_steps(n):
                    i, h = INDEX[m]
                    act.wait_ge(S["idx_done"], m + 1)
                    if m >= 2:
                        act.wait_ge(S["idx_added"], m - 1)
                    nc.scalar.activation(scratch[:, (1, 4)[m % 2], 0:P * (i + 1)],
                                         PS[:, 5 + m % 2, 0:P * (i + 1)], ACT.Relu).then_inc(S["relu_done"], 1)
            copy_values(PROJ_ALONE - 1)

        def copy_values(n):
            if n not in VALUES:
                return
            v = VALUES.index(n)
            act.wait_ge(S["v_turned"], v + 1)
            dst = vb[:, :, :] if v == 4 else va[:, :, P * v:P * (v + 1)]
            copy(dst, PS[:, 7, :].rearrange("p (i n) -> p i n", i=QT)).then_inc(S["v_copied"], 1)

        def attention_1():
            for m in range(LAST_STEP + 1):
                if m in STARTS:
                    ahead(unit_between(STARTS.index(m)))
                if m < len(STEPS):
                    br, i, h = STEPS[m]
                    act.wait_ge(S["s_biased"], m + 1)
                    if m >= 2:
                        act.wait_ge(S["p_turned"], m - 1)
                    nc.scalar.activation(scratch[:, 2 + m % 2, 0:P * (i + 1)], scratch[:, 1, 0:P * (i + 1)],
                                         ACT.Exp, bias=row_neg_max[:, m:m + 1], scale=-1.0,
                                         accum_out=row_sum[:, m:m + 1]).then_inc(S["p_made"], 1)
                if 1 <= m <= len(STEPS):
                    n = m - 1
                    br, i, h = STEPS[n]
                    act.wait_ge(S["p_turned"], n + 1)
                    if n >= 1:
                        act.wait_ge(S["pv_done"], n)
                    copy(scratch[:, 4, 0:P * (i + 1)], PS[:, 6, 0:P * (i + 1)])\
                        .then_inc(S["pt_copied"], 1)
                if m % HEADS == 3 and m > HEADS:
                    g = m // HEADS - 1
                    br, i = g // QT, g % QT
                    act.wait_ge(S["o_turned"], g + 1)
                    copy(o_hi[br][:, :, P * i:P * (i + 1)], PS[:, g % 2, :].rearrange("p (c n) -> p c n", c=4))\
                        .then_inc(S["o_hi_done"], 1)
                if m - 3 in ENDS and ENDS.index(m - 3) < len(PROJ) - PROJ_ALONE:
                    copy_values(PROJ_ALONE + ENDS.index(m - 3))

        def merge():
            def sigmoids(n):
                for j in (2 * n, 2 * n + 1):
                    act.wait_ge(S["gate_in"], j + 1)
                    nc.scalar.activation(gate(j), gate(j), ACT.Sigmoid).then_inc(S["gate_sig"], 1)

            sigmoids(0)
            for n in range(DT):
                ahead(U_GATE + 2 * DT + n)
                if n + 1 < DT:
                    sigmoids(n + 1)
                act.wait_ge(S["merged"], n + 1)
                copy(m_hi[:, n, :], scratch[:, 5 + n % 2, :]).then_inc(S["m_hi_done"], 1)

        def mixer_2():
            pairs = SB_HEADS // 2

            def head_square(t, c):
                act.wait_ge(S["qk_made"], 2 * t + c + 1)
                nc.scalar.activation(scratch[:, 2 + c, :], scratch[:, c, :], ACT.Square).then_inc(S["qk_sq"], 1)

            def head_rms(t, c):
                act.wait_ge(S["qk_ms"], 2 * t + c + 1)
                nc.scalar.activation(scratch[:, 4 + c, :], PS[:, 6 + c, :], ACT.Ln, bias=eps_col[:, 0:1])\
                  .then_inc(S["qk_ln"], 1)
                act.wait_ge(S["qk_ln"], 2 * t + c + 1)
                nc.scalar.activation(scratch[:, 4 + c, :], scratch[:, 4 + c, :], ACT.Exp, scale=-0.5)\
                  .then_inc(S["qk_inv"], 1)

            def round_values(t):
                act.wait_ge(S["sv_turned"], t + 1)
                copy(sb_v[0][:, t % 2, :, :], PS[:, 6, :].rearrange("p (i n) -> p i n", i=QT))\
                    .then_inc(S["sv_hi"], 1)

            def round_out(h):
                r = HD * (h % 2)
                act.wait_ge(S["sb_pv"], h + 1)
                copy(so_hi[r:r + HD, h // 2, :], PS[r:r + HD, 3, :]).then_inc(S["so_hi_done"], 1)

            ahead(U_QKV)
            root_mean_square(S_FFN3)
            ahead(U_QKV + 1)
            head_square(0, 0)
            ahead(U_QKV + 2)
            act.preload_act_table_set("natural_log_exp_and_others")
            head_rms(0, 0)
            head_square(0, 1)
            head_rms(0, 1)
            for h in range(SB_HEADS):
                t, odd = divmod(h, 2)
                act.wait_ge(S["z_done"], h + 1)
                if h:
                    act.wait_ge(S["w_split"], h)
                nc.scalar.activation(sb_e[:, :], ps_flat[:, 0:SBW], ACT.Abs).then_inc(S["abs_done"], 1)
                act.wait_ge(S["abs_done"], h + 1)
                nc.scalar.activation(sb_e[:, :], sb_e[:, :], ACT.Exp, scale=-1.0).then_inc(S["e_done"], 1)
                act.wait_ge(S["e_done"], h + 1)
                nc.scalar.activation(sb_e[:, :], sb_e[:, :], ACT.Ln, bias=one_col[:, 0:1]).then_inc(S["l_done"], 1)
                if not odd:
                    round_values(t)
                    if t + 1 < pairs:
                        ahead(U_QKV + 3 * (t + 1))
                        ahead(U_QKV + 3 * (t + 1) + 1)
                        head_square(t + 1, 0)
                    else:
                        ahead(U_SBO)
                        ahead(U_SBO + 1)
                elif t + 1 < pairs:
                    ahead(U_QKV + 3 * (t + 1) + 2)
                    head_square(t + 1, 1)
                    head_rms(t + 1, 1)
                if h:
                    round_out(h - 1)
                act.wait_ge(S["cum_done"], h + 1)
                nc.scalar.activation(sb_e[:, :], ps_flat[:, 0:SBW], ACT.Exp).then_inc(S["w_done"], 1)
                if not odd and t + 1 < pairs:
                    head_rms(t + 1, 0)
            round_out(SB_HEADS - 1)
            for k in range(DT):
                if k + 2 < DT:
                    ahead(U_SBO + k + 2)
                tail(k, k % 2, MIX_RES[1], T_MIX2, S_MIX2)

        for u in range(AHEAD):
            round_weights(u, u, 0)
        for k in range(DT):
            act.wait_ge(x_landed[k], 16)
            square(k, k % 2, S_START, k)
            round_input(k, k % 2, T_START)
        ffn_up(0)
        residual(FFN_BASE[0] + UP_UNITS, len(DOWN), FFN_RES[0], T_FFN1, S_FFN1)
        projection_1()
        attention_1()
        merge()
        residual(U_OUT, 1, MIX_RES[0], T_MIX1, S_MIX1)
        ffn_up(1)
        residual(FFN_BASE[1] + UP_UNITS, len(DOWN), FFN_RES[1], T_FINAL, S_FINAL)
        ffn_up(2)
        residual(FFN_BASE[2] + UP_UNITS, len(DOWN), FFN_RES[2], T_FFN3, S_FFN3)
        mixer_2()
        ffn_up(3)
        for u in range(FFN_BASE[3] + UP_UNITS, UNITS):
            ahead(u)

    @block.vector
    def _(dve):
        def multiply(dst, p, q):
            return nc.vector.tensor_tensor(dst, p, q, ALU.mult)

        def scale_two(dst, p, scalar, q):
            return nc.vector.scalar_tensor_tensor(dst, p, scalar, q, ALU.mult, ALU.mult)

        def reciprocal_rms(stat):
            dve.wait_ge(S["rms_done"], stat + 1)
            nc.vector.reciprocal(rstd[:, :], scratch[:, 6, :]).then_inc(S["rstd_ready"], 1)
            dve.wait_ge(S["rstd_ready"], stat + 1)

        def zero_ssq(stat):
            nc.vector.memset(ssq[:, :], 0.0).then_inc(S["ssq_zeroed"], 1)
            dve.wait_ge(S["ssq_zeroed"], stat + 1)

        def tail(k, b, t, stat):
            nc.vector.tensor_scalar(scratch[:, 2 + b, :], X[:, k, :], gains[:, t, bass.ds(k, 1)], None,
                                    ALU.mult).then_inc(S["xg_done"], 1)
            dve.wait_ge(S["sq_done"], k + (DT * stat + 1))
            if not (isinstance(k, int) and k + stat == 0):
                dve.wait_ge(S["ssq_done"], k + DT * stat)
            nc.vector.tensor_tensor(ssq[:, :], ssq[:, :], scratch[:, 4 + b, :], ALU.add).then_inc(S["ssq_done"], 1)
            if stat == S_FINAL:
                dve.wait_ge(S["sq2_done"], k + 1)
                nc.vector.tensor_tensor(scratch[:, 0, :], scratch[:, 0, :], scratch[:, 1, :], ALU.add)\
                    .then_inc(S["ssq2_done"], 1)
            dve.wait_ge(S["xn_hi_done"], k + (DT * t + 1))
            nc.vector.tensor_tensor(xn_lo[:, k, :], scratch[:, 2 + b, :], xn_hi[:, k, :].bitcast(F32),
                                    ALU.subtract).then_inc(S["xn_lo_done"], 1)

        def ffn_up(n):
            def tile(F, j):
                u, f = 2 * F + FFN_BASE[n], F + FT * n
                dve.wait_ge(S["unit_done"], u + 1)
                multiply(scratch[:, j, :], PS[:, 2 * j, :], rstd[:, :]).then_inc(S["gate_scaled"], 1)
                dve.wait_ge(S["unit_done"], u + 2)
                multiply(scratch[:, 2 + j, :], PS[:, 2 * j + 1, :], rstd[:, :]).then_inc(S["up_scaled"], 1)
                dve.wait_ge(S["silu_done"], f + 1)
                dve.wait_ge(S["up_scaled"], f + 1)
                multiply(scratch[:, 2 + j, :], scratch[:, 2 + j, :], scratch[:, j, :]).then_inc(S["h_made"], 1)
                dve.wait_ge(S["h_hi_done"], f + 1)
                nc.vector.tensor_tensor(h_lo[:, F, :], scratch[:, 2 + j, :], h_hi[:, F, :].bitcast(F32),
                                        ALU.subtract).then_inc(S["h_lo_done"], 1)

            if n == 2:
                final_norms()
            else:
                reciprocal_rms(FFN_STAT[n])
            for j in range(2):
                tile(j, j)
            if n == 2:
                for k in range(DT):
                    scale_two(X[:, k, :], X[:, k, :], gains[:, G_FINAL, k:k + 1], scratch[:, 6, :])\
                        .then_inc(S["x_normed"], 1)
                dve.wait_ge(S["x_normed"], DT)
            with dve.Fori(1, FT // 2) as it:
                for j in range(2):
                    tile(2 * it + j, j)

        def final_norms():
            dve.wait_ge(S["rms_done"], S_FINAL + 1)
            nc.vector.reciprocal(scratch[:, 6, :], scratch[:, 6, :]).then_inc(S["r1_made"], 1)
            dve.wait_ge(S["r1_made"], 1)
            dve.wait_ge(S["ms2_done"], 1)
            multiply(scratch[:, 4, :], PS[:, 5, :], scratch[:, 6, :]).then_inc(S["r1_made"], 1)
            dve.wait_ge(S["r1_made"], 2)
            multiply(scratch[:, 4, :], scratch[:, 4, :], scratch[:, 6, :]).then_inc(S["m2_scaled"], 1)
            dve.wait_ge(S["rms2_done"], 1)
            nc.vector.reciprocal(scratch[:, 5, :], scratch[:, 5, :]).then_inc(S["r2_made"], 1)
            dve.wait_ge(S["r2_made"], 1)
            multiply(rstd[:, :], scratch[:, 5, :], scratch[:, 6, :]).then_inc(S["rstd_ready"], 1)
            dve.wait_ge(S["rstd_ready"], S_FINAL + 1)

        def residual(u0, per, factor, r, t, stat):
            if stat is not None:
                zero_ssq(stat)
            if stat == S_FINAL:
                nc.vector.memset(scratch[:, 0, :], 0.0).then_inc(S["ssq2_zeroed"], 1)
                dve.wait_ge(S["ssq2_zeroed"], 1)
            with dve.Fori(0, 2) as it:
                for j in range(4):
                    update(4 * it + j, j, 4 * per * it + (u0 + per * (j + 1)), factor, r, t, stat, j % 2)

        def update(k, bank, units, factor, r, t, stat, b):
            dve.wait_ge(S["unit_done"], units)
            nc.vector.scalar_tensor_tensor(X[:, k, :], PS[:, bank, :], factor, X[:, k, :],
                                           ALU.mult, ALU.add).then_inc(S["x_updated"], 1)
            if stat is not None:
                dve.wait_ge(S["x_updated"], k + (DT * r + 1))
                tail(k, b, t, stat)

        def evacuate(dst, bank, factor):
            if factor == 1.0:
                return multiply(dst, PS[:, bank, :], rstd[:, :])
            return scale_two(dst, PS[:, bank, :], factor, rstd[:, :])

        def evacuate_1(n):
            what, t = PROJ[n]
            bank = n % 4 if n < PROJ_ALONE else 2 + (n - PROJ_ALONE) % 2
            factor = HD ** -0.5 if what in QUERY else 1.0
            dve.wait_ge(S["unit_done"], U_PROJ + n + 1)
            if n in ROPE:
                k = ROPE.index(n)
                evacuate(scratch[:, 5, :], bank, factor).then_inc(S["rope_scaled"], 1)
                dve.wait_ge(S["rope_scaled"], k + 1)
                multiply(rope_out(n), scratch[:, 5, :], rope[:, 0, :])
            elif what == WI:
                scale_two(scratch[0:8, 2, :], PS[0:8, bank, :], HEADS ** -0.5, rstd[0:8, :])\
                    .then_inc(S["wi_made"], 1)
            elif n in VALUES:
                v = VALUES.index(n)
                if v >= 2:
                    dve.wait_ge(S["v_turned"], v - 1)
                evacuate(scratch[:, VALUE_BUFFER[v], :], bank, factor).then_inc(S["v_made"], 1)
            else:
                evacuate((qa if what == QA else ka)[:, t, :], bank, factor).then_inc(S["plain_made"], 1)

        def rope_out(n):
            what, t = PROJ[n]
            return {KI: ki[:, :], QI: qi[:, t, :], KB: kb[:, :], QB: qb[:, t, :]}[what]

        def finish_rope(n):
            if n not in ROPE:
                return
            k = ROPE.index(n)
            dve.wait_ge(S["swap_done"], k + 1)
            multiply(scratch[:, 6, :], PS[:, 7, :], rope[:, 1, :]).then_inc(S["rope_sined"], 1)
            dve.wait_ge(S["rope_sined"], k + 1)
            nc.vector.tensor_tensor(rope_out(n), rope_out(n), scratch[:, 6, :], ALU.add)\
                .then_inc(S["rope_added"], 1)

        def projection_1():
            reciprocal_rms(S_FFN1)
            nc.vector.memset(mask[0][:, :], 0.0).then_inc(S["mask_ready"], 1)
            dve.wait_ge(S["bias_in"], 16)
            nc.vector.memset(bias[0:CHUNK, :, 0:CHUNK], FAR).then_inc(S["bias_ready"], 1)
            dve.wait_ge(S["mask_ready"], 1)
            nc.vector.memset(mask[0][0:CHUNK, CHUNK:P], FAR).then_inc(S["mask_ready"], 1)
            dve.wait_ge(S["rope_in"], 16)
            for n in range(PROJ_ALONE):
                if n - 1 in ROPE and n in ROPE:
                    finish_rope(n - 1)
                    evacuate_1(n)
                else:
                    evacuate_1(n)
                    finish_rope(n - 1)
                if n == 2:
                    dve.wait_ge(S["wt_turned"], 1)
                    nc.vector.tensor_copy(w_tok, PS[:, 4, 0:32]).then_inc(S["wt_copied"], 1)
                for m in index_steps(n):
                    add_index(m)
                for k in range(TOP_EACH * (n - TOP_FROM), TOP_EACH * (n - TOP_FROM + 1)):
                    if k >= 0:
                        select(k)

        def add_index(m):
            i, h = INDEX[m]
            W = P * (i + 1)
            relu = scratch[:, (1, 4)[m % 2], 0:W]
            weight = w_tok[:, 8 * i + h:8 * i + h + 1]
            dve.wait_ge(S["relu_done"], m + 1)
            if m == 0:
                dve.wait_ge(S["wt_copied"], 1)
            if h == 0:
                nc.vector.tensor_scalar(mask[i][:, :], relu, weight, None, ALU.mult).then_inc(S["idx_added"], 1)
            else:
                dve.wait_ge(S["idx_added"], m)
                nc.vector.scalar_tensor_tensor(mask[i][:, :], relu, weight, mask[i][:, :],
                                               ALU.mult, ALU.add).then_inc(S["idx_added"], 1)
            if h == HEADS - 1:
                dve.wait_ge(S["idx_added"], m + 1)
                nc.vector.memset(mask[i][0:CHUNK, W - CHUNK:W], OUTSIDE).then_inc(S["score_ready"], 1)

        def select(k):
            i, eight = 1 + k // ROUNDS, top8[:, 8 * (k % 2):8 * (k % 2) + 8]
            if k % ROUNDS == 0:
                dve.wait_ge(S["score_ready"], i)
            if k:
                dve.wait_ge(S["top_taken"], k)
            nc.vector.max(eight, mask[i][:, :]).then_inc(S["top_found"], 1)
            dve.wait_ge(S["top_found"], k + 1)
            nc.vector.match_replace(mask[i][:, :], eight, mask[i][:, :], TAKEN).then_inc(S["top_taken"], 1)
            if k % ROUNDS == ROUNDS - 1:
                dve.wait_ge(S["top_taken"], k + 1)
                nc.vector.tensor_scalar(mask[i][:, :], mask[i][:, :], TAKEN_BELOW, FAR, ALU.is_gt, ALU.mult)\
                    .then_inc(S["mask_ready"], 1)

        def attention_1():
            taken = TOP_EACH * (PROJ_ALONE - TOP_FROM)
            for m in range(LAST_STEP + 2):
                if m < len(STEPS):
                    br, i, h = STEPS[m]
                    W = P * (i + 1)
                    dve.wait_ge(S["s_done"], m + 1)
                    if m == 0:
                        dve.wait_ge(S["bias_ready"], 1)
                    if br == 1 and h == 0:
                        dve.wait_ge(S["mask_ready"], 2 + i)
                    if m >= 1:
                        dve.wait_ge(S["p_made"], m)
                    add = bias[:, h, W - 1::-1] if br == 0 else mask[i][:, :]
                    nc.vector.tensor_tensor_reduce(scratch[:, 1, 0:W], PS[:, 4 + m % 2, 0:W], add,
                                                   -1.0, -FAR, ALU.add, ALU.min,
                                                   row_neg_max[:, m:m + 1]).then_inc(S["s_biased"], 1)
                if m - 1 in ENDS:
                    n = ENDS.index(m - 1)
                    if n < len(PROJ) - PROJ_ALONE:
                        evacuate_1(PROJ_ALONE + n)
                    else:
                        j = n + PROJ_ALONE - len(PROJ)
                        dve.wait_ge(S["unit_done"], unit_between(n) + 1)
                        evacuate(gate(j), 2 + n % 2, 1.0).then_inc(S["gate_in"], 1)
                if m - 3 in ENDS and ENDS.index(m - 3) < len(PROJ) - PROJ_ALONE:
                    finish_rope(PROJ_ALONE + ENDS.index(m - 3))
                if m % HEADS == 1 and m > HEADS:
                    g = m // HEADS - 1
                    dve.wait_ge(S["p_made"], HEADS * (g + 1))
                    nc.vector.reciprocal(row_inv, row_sum[:, HEADS * g:HEADS * (g + 1)]).then_inc(S["inv_made"], 1)
                    dve.wait_ge(S["inv_made"], g + 1)
                    dve.wait_ge(S["pv_done"], HEADS * (g + 1))
                    if g:
                        dve.wait_ge(S["o_turned"], g)
                    multiply(ssq[:, :].rearrange("p (h d) -> p h d", h=HEADS),
                             PS[:, g % 2, :].rearrange("p (h d) -> p h d", h=HEADS),
                             row_inv.unsqueeze(2).broadcast_to([P, HEADS, HD])).then_inc(S["o_normed"], 1)
                if m % HEADS == 4 and m > HEADS:
                    g = m // HEADS - 1
                    br, i = g // QT, g % QT
                    dve.wait_ge(S["o_hi_done"], g + 1)
                    nc.vector.tensor_tensor(o_lo[br][:, :, P * i:P * (i + 1)],
                                            PS[:, g % 2, :].rearrange("p (c n) -> p c n", c=4),
                                            o_hi[br][:, :, P * i:P * (i + 1)].bitcast(F32), ALU.subtract)\
                        .then_inc(S["o_lo_done"], 1)
                if taken < ROUNDS * (QT - 1):
                    select(taken)
                    taken += 1

        def merge():
            for n in range(DT):
                b = 4 * (n % 2)
                dve.wait_ge(S["unit_done"], U_GATE + 2 * DT + n + 1)
                for g in range(2):
                    dve.wait_ge(S["gate_sig"], 2 * n + g + 1)
                    multiply(scratch[:, 3 + g, :], PS[:, b + g, :], gate(2 * n + g)).then_inc(S["branch_gated"], 1)
                dve.wait_ge(S["branch_gated"], 2 * n + 2)
                nc.vector.tensor_tensor(scratch[:, 5 + n % 2, :], scratch[:, 3, :], scratch[:, 4, :], ALU.add)\
                    .then_inc(S["merged"], 1)
                dve.wait_ge(S["m_hi_done"], n + 1)
                nc.vector.tensor_tensor(m_lo[:, n, :], scratch[:, 5 + n % 2, :], m_hi[:, n, :].bitcast(F32),
                                        ALU.subtract).then_inc(S["m_lo_done"], 1)

        def mixer_2():
            pairs = SB_HEADS // 2

            def make(t, c):
                n = 3 * t + c
                dve.wait_ge(S["unit_done"], U_QKV + n + 1)
                if c == 2:
                    if t:
                        dve.wait_ge(S["sv_turned"], t)
                    evacuate(scratch[:, 6, :], 4 + n % 2, 1.0).then_inc(S["sv_made"], 1)
                else:
                    evacuate(scratch[:, c, :], 4 + n % 2, 1.0).then_inc(S["qk_made"], 1)

            def head_norm(t, c):
                dve.wait_ge(S["qk_inv"], 2 * t + c + 1)
                hi, lo = (part[:, t % 2, :] for part in (sb_q, sb_k)[c])
                full = scratch[:, c, :]
                scale_two(full, full, head_gain[:, 2 + c:3 + c], scratch[:, 4 + c, :])\
                    .then_inc(S["qk_normed"], 1)
                dve.wait_ge(S["qk_normed"], 2 * t + c + 1)
                nc.vector.tensor_copy(hi, full).then_inc(S["qk_hi"], 1)
                dve.wait_ge(S["qk_hi"], 2 * t + c + 1)
                nc.vector.tensor_tensor(lo, full, hi.bitcast(F32), ALU.subtract).then_inc(S["qk_split"], 1)

            def split_values(t):
                dve.wait_ge(S["sv_hi"], t + 1)
                hi, lo = (part[:, t % 2, :, :] for part in sb_v)
                nc.vector.tensor_tensor(lo, PS[:, 6, :].rearrange("p (i n) -> p i n", i=QT), hi.bitcast(F32),
                                        ALU.subtract).then_inc(S["sv_split"], 1)

            def split_out(h):
                r = HD * (h % 2)
                dve.wait_ge(S["so_hi_done"], h + 1)
                nc.vector.tensor_tensor(so_lo[r:r + HD, h // 2, :], PS[r:r + HD, 3, :],
                                        so_hi[r:r + HD, h // 2, :].bitcast(F32), ALU.subtract)\
                    .then_inc(S["so_lo_done"], 1)

            reciprocal_rms(S_FFN3)
            zero_ssq(S_MIX2)
            dve.wait_ge(S["cols_ready"], 3)
            make(0, 0)
            make(0, 1)
            head_norm(0, 0)
            head_norm(0, 1)
            make(0, 2)
            for h in range(SB_HEADS):
                t, odd = divmod(h, 2)
                if odd and t + 1 < pairs:
                    make(t + 1, 1)
                dve.wait_ge(S["l_done"], h + 1)
                nc.vector.scalar_tensor_tensor(sb_e[:, :], ps_flat[:, 0:SBW], 0.0, sb_e[:, :], ALU.max, ALU.add)\
                    .then_inc(S["sp_done"], 1)
                dve.wait_ge(S["sp_done"], h + 1)
                if h:
                    dve.wait_ge(S["cum_done"], h)
                nc.vector.tensor_copy(sp[0][:, :], sb_e[:, :]).then_inc(S["sp_hi_done"], 1)
                dve.wait_ge(S["sp_hi_done"], h + 1)
                nc.vector.tensor_tensor(sp[1][:, :], sb_e[:, :], sp[0][:, :].bitcast(F32), ALU.subtract)\
                    .then_inc(S["sp_split"], 1)
                if not odd:
                    split_values(t)
                if t + 1 < pairs:
                    if odd:
                        head_norm(t + 1, 1)
                    else:
                        make(t + 1, 0)
                if h:
                    split_out(h - 1)
                dve.wait_ge(S["w_done"], h + 1)
                if h:
                    dve.wait_ge(S["sb_pv"], h)
                nc.vector.tensor_copy(sb_w[0][:, :], sb_e[:, :]).then_inc(S["w_hi_done"], 1)
                dve.wait_ge(S["w_hi_done"], h + 1)
                nc.vector.tensor_tensor(sb_w[1][:, :], sb_e[:, :], sb_w[0][:, :].bitcast(F32), ALU.subtract)\
                    .then_inc(S["w_split"], 1)
                if t + 1 < pairs:
                    if odd:
                        make(t + 1, 2)
                    else:
                        head_norm(t + 1, 0)
            split_out(SB_HEADS - 1)
            for k in range(DT):
                update(k, (k + 4) % 8, U_SBO + k + 1, 1.0, MIX_RES[1], T_MIX2, S_MIX2, k % 2)

        nc.vector.memset(eps_col[:, :], EPS).then_inc(S["cols_ready"], 1)
        nc.vector.memset(one_col[:, :], 1.0).then_inc(S["cols_ready"], 1)
        dve.wait_ge(S["consts_in"], 32)
        nc.vector.tensor_copy(const_r[:, :, :], const[:, 4:6, :])
        zero_ssq(S_START)
        dve.wait_ge(S["gains_in"], 32)
        nc.vector.tensor_scalar(head_gain[:, 2:3], head_gain[:, 0:1], HD ** -0.5, None, ALU.mult)
        multiply(gains[:, T_FINAL, :], gains[:, T_FINAL, :], gains[:, G_FINAL, :])
        nc.vector.tensor_copy(head_gain[:, 3:4], head_gain[:, 1:2]).then_inc(S["cols_ready"], 1)
        for k in range(DT):
            dve.wait_ge(x_landed[k], 16)
            tail(k, k % 2, T_START, S_START)
        ffn_up(0)
        residual(FFN_BASE[0] + UP_UNITS, len(DOWN), 0.5, FFN_RES[0], T_FFN1, S_FFN1)
        projection_1()
        attention_1()
        merge()
        residual(U_OUT, 1, 1.0, MIX_RES[0], T_MIX1, S_MIX1)
        ffn_up(1)
        residual(FFN_BASE[1] + UP_UNITS, len(DOWN), 0.5, FFN_RES[1], T_FINAL, S_FINAL)
        ffn_up(2)
        residual(FFN_BASE[2] + UP_UNITS, len(DOWN), 0.5, FFN_RES[2], T_FFN3, S_FFN3)
        mixer_2()
        ffn_up(3)
        residual(FFN_BASE[3] + UP_UNITS, len(DOWN), 0.5, FFN_RES[3], None, None)


def mean_bank(stat):
    return 7 if stat == S_FFN3 else 4


def index_steps(n):
    first = INDEX_EACH * (n - INDEX_FROM)
    return range(max(first, 0), max(min(first + INDEX_EACH, len(INDEX)), 0))


def _units(w, width=P):
    k, n = w.shape
    return w.reshape(k // P, P, n // P, P).transpose(2, 1, 0, 3)


def _ffn_units(w_in, w_out):
    up = _units(w_in).reshape(2, FT, P, UK, P).transpose(1, 0, 2, 3, 4).reshape(UP_UNITS, P, UK, P)
    down = np.pad(_units(w_out), ((0, 0), (0, 0), (0, len(DOWN) * UK - FT), (0, 0)))
    down = down.reshape(DT, P, len(DOWN), UK, P).transpose(0, 2, 1, 3, 4).reshape(DOWN_UNITS, P, UK, P)
    return [up, down]


def _mixer_units(w_in, w_a, w_b, w_out):
    width = HEADS * HD
    cut = np.cumsum([width, width, width, width, 2 * HD, 2 * HD, width, HD, HEADS, D])
    qa, ka, va, qb, kb, vb, qi, ki, wi, ga, gb = np.split(w_in, cut, axis=1)
    qb = qb.reshape(D, 2, 4, HD).transpose(0, 2, 1, 3).reshape(D, width)
    ki = np.concatenate([ki, ki], axis=1)
    wi = np.pad(wi, ((0, 0), (0, P - HEADS)))
    proj = [_units(np.ascontiguousarray(w)) for w in (ki, wi, qi, qa, ka, va, kb, vb, qb)]
    both = np.concatenate([_units(w_a), _units(w_b)], axis=2)
    gate = np.stack([_units(np.ascontiguousarray(ga)), _units(np.ascontiguousarray(gb))], axis=1)
    return proj + [gate.reshape(2 * DT, P, UK, P), both, _units(w_out)]


def _constants():
    rows, cols = np.arange(P)[:, None], np.arange(P)[None, :]
    head = (rows // HD == cols // HD)
    rot = HD // 4
    d = np.arange(P) % HD
    partner = np.where(d < rot // 2, np.arange(P) + rot // 2, np.arange(P) - rot // 2)
    swap = (rows == partner[None, :]) & (d < rot)[None, :]
    upto = rows >= cols
    consts = np.stack([rows == cols, np.full((P, P), 1.0 / D), head / HD, swap, -1.0 * upto,
                       np.full((P, P), -1.0)], axis=1).astype(np.float32)
    freq = np.power(np.float32(500000.0), -np.arange(0, rot, 2, dtype=np.float32) / np.float32(rot))
    ang = np.arange(TOK, dtype=np.float32)[None, :] * freq.astype(np.float32)[:, None]
    cos, sin = np.ones((P, TOK), np.float32), np.zeros((P, TOK), np.float32)
    for p in range(P):
        if d[p] < rot:
            cos[p] = np.cos(ang[d[p] % (rot // 2)])
            sin[p] = np.sin(ang[d[p] % (rot // 2)]) * (-1.0 if d[p] < rot // 2 else 1.0)
    return consts, np.stack([rows == cols, FAR * upto], axis=1), np.stack([cos, sin], axis=1)


def kernel(**inputs):
    import ml_dtypes
    import concourse.bacc as bacc
    from concourse.bass_utils import run_bass_kernel_spmd

    i = {name: np.asarray(value) for name, value in inputs.items()}
    streams = _ffn_units(i["ffn1_w_in"][0], i["ffn1_w_out"][0])
    streams += _mixer_units(i["w_in"][0], i["w_branch_a"][0], i["w_branch_b"][0], i["w_out"][0])
    streams += _ffn_units(i["ffn2_w_in"][0], i["ffn2_w_out"][0])
    streams += _ffn_units(i["l0_ff1_w_in_2"], i["l0_ff1_w_out_2"])
    qkv = _units(i["l0_sb_w_qkv_2"]).reshape(3, DT, P, UK, P).transpose(1, 0, 2, 3, 4)
    streams += [qkv.reshape(PROJ_UNITS, P, UK, P), _units(i["l0_sb_w_o_2"])]
    streams += _ffn_units(i["l0_ff2_w_in_2"], i["l0_ff2_w_out_2"])
    gain = np.stack([i["n1_g"][0], i["n2_g"][0], i["n3_g"][0], i["l0_ff1_norm_2"], i["l0_mix_norm_2"],
                     i["l0_ff2_norm_2"], i["nf_g"]])
    rel = i["rel_bias"][0]
    rel = np.pad(rel, ((0, 0), (0, TOK + P - rel.shape[1])), mode="edge")
    consts, consts_b, ropes = _constants()
    q_gain, k_gain = i["l0_sb_q_norm_2"], i["l0_sb_k_norm_2"]
    arrays = {
        "weights": np.concatenate(streams, axis=0),
        "consts": consts,
        "consts_b": consts_b.astype(ml_dtypes.bfloat16),
        "ropes": ropes,
        "rel": np.ascontiguousarray(rel),
        "gain_cols": np.ascontiguousarray(gain.reshape(7, DT, P).transpose(2, 0, 1)),
        "head_gains": np.stack([np.concatenate([q_gain, q_gain]), np.concatenate([k_gain, k_gain])], axis=1),
        "x_t": np.ascontiguousarray(i["x"][0].T.reshape(DT, P, TOK).transpose(1, 0, 2)),
    }
    nc = bacc.Bacc("TRN2", target_bir_lowering=False, num_devices=1)
    args = [nc.dram_tensor(name, v.shape, mybir.dt.from_np(v.dtype), kind="ExternalInput").ap()
            for name, v in arrays.items()]
    args.append(nc.dram_tensor("out_t", (P, DT, TOK), F32, kind="ExternalOutput").ap())
    program(nc, *args)
    r = run_bass_kernel_spmd(nc, [arrays], core_ids=[0])
    got = np.asarray(r.results[0]["out_t"])
    return np.ascontiguousarray(got.transpose(2, 1, 0).reshape(1, TOK, D))
```

```python
from contextlib import ExitStack

import numpy as np
import concourse.bass as bass
from concourse import mybir

F32, F32R, BF16 = mybir.dt.float32, mybir.dt.float32r, mybir.dt.bfloat16
ACT, ALU = mybir.ActivationFunctionType, mybir.AluOpType

P = 128
TOK = 512
D = 1024
DT = D // P
FT = 2816 // P
QT = TOK // P
HD = 64
HEADS = 8
SB_HEADS = 16
CHUNK = 64
TOPK = min(256, TOK // 4)
EPS = 1e-6
NSLOT = 4
AHEAD = 2
UK = 8
DOWN = [(0, 8), (8, 16), (16, FT)]

UP_UNITS, DOWN_UNITS = 2 * FT, len(DOWN) * DT
PROJ_UNITS, GATE_UNITS, QKV_UNITS, OUT_UNITS = 23, 3 * DT, 3 * DT, DT
FFN_UNITS = UP_UNITS + DOWN_UNITS
U_FFN1 = 0
U_PROJ = U_FFN1 + FFN_UNITS
U_GATE = U_PROJ + PROJ_UNITS
U_OUT = U_GATE + GATE_UNITS
U_FFN2 = U_OUT + OUT_UNITS
U_FFN3 = U_FFN2 + FFN_UNITS
U_QKV = U_FFN3 + FFN_UNITS
U_SBO = U_QKV + QKV_UNITS
U_FFN4 = U_SBO + OUT_UNITS
UNITS = U_FFN4 + FFN_UNITS
FFN_BASE = [U_FFN1, U_FFN2, U_FFN3, U_FFN4]

FFN_RES, MIX_RES = [0, 2, 3, 5], [1, 4]
S_START, S_FFN1, S_MIX1, S_FINAL, S_FFN3, S_MIX2 = range(6)
T_START, T_FFN1, T_MIX1, T_FINAL, T_FFN3, T_MIX2 = range(6)
G_FINAL = 6
FFN_STAT = [S_START, S_MIX1, S_FINAL, S_MIX2]
FFN_INPUT = [T_START, T_MIX1, T_FINAL, T_MIX2]

KI, QI, KB, VB, QB, QA, KA, VA = range(8)
PROJ = [(KI, 0)] + [(what, t) for what in (QI, QA, KA, VA) for t in range(4)] + [
    (KB, 0), (VB, 0), (QB, 0), (QB, 1), (QB, 2), (QB, 3)]
PROJ_ALONE = 17
ROPE = [n for n, (what, _) in enumerate(PROJ) if what in (KI, QI, KB, QB)]
VALUES = [n for n, (what, _) in enumerate(PROJ) if what in (VA, VB)]
QUERY = (QI, QB, QA)
INDEX = [(i, h) for i in range(1, QT) for h in range(HEADS)]
INDEX_FROM, INDEX_EACH = 6, 3
ROUNDS = TOPK // 8
TOP_FROM, TOP_EACH = 8, 4
STEPS = [(br, i, h) for br in range(2) for i in range(QT) for h in range(HEADS)]
HALF = len(STEPS) // 2
GROUPS = 2 * QT
VALUE_BUFFER = (2, 0, 2, 0, 0)
LAST_STEP = len(STEPS) + 3
BETWEEN = len(PROJ) - PROJ_ALONE + 2 * DT
PROJ_STEPS = HALF - 2


def filled(m):
    if m < 0:
        return 0
    first = (len(PROJ) - PROJ_ALONE) * UK
    if m < PROJ_STEPS:
        return first * (m + 1) // PROJ_STEPS
    return first + 2 * DT * UK * (m + 1 - PROJ_STEPS) // (LAST_STEP + 1 - PROJ_STEPS)


STARTS = [next(m for m in range(LAST_STEP + 1) if filled(m) > UK * n) for n in range(BETWEEN)]
ENDS = [next(m for m in range(LAST_STEP + 1) if filled(m) >= UK * (n + 1)) for n in range(BETWEEN)]

FILL_BEFORE, FILL_BEHIND = 10, 2

FAR = -1e30
OUTSIDE = -3.0e38
TAKEN = -3.2e38
TAKEN_BELOW = -3.1e38


def program(nc, weights, consts, consts_b, ropes, rel, gain_cols, head_gains, x, out):
    with ExitStack() as ctx:
        build(nc, ctx, weights, consts, consts_b, ropes, rel, gain_cols, head_gains, x, out)


def build(nc, ctx, weights, consts, consts_b, ropes, rel, gain_cols, head_gains, x, out):
    size = {F32: 4, F32R: 4, BF16: 2}
    fixed = [(nc.sbuf_base + 63) // 64 * 64]

    def place(name, shape, dt=F32, where=fixed):
        tensor = nc.alloc_sbuf_tensor_at(name, shape, dt, offset=where[0])
        where[0] += (int(np.prod(shape[1:])) * size[dt] + 31) // 32 * 32
        assert where[0] <= nc.sbuf_usable_end
        return tensor

    X = place("x_sb", [P, DT, TOK])
    xn_hi = place("xn_hi", [P, DT, TOK], F32R)
    xn_lo = place("xn_lo", [P, DT, TOK], F32R)
    raw = [place(f"raw{s}", [P, UK, P]) for s in range(NSLOT)]
    w_hi = [place(f"w_hi{s}", [P, UK, P], F32R) for s in range(NSLOT)]
    w_lo = [place(f"w_lo{s}", [P, UK, P], F32R) for s in range(NSLOT)]
    rstd = place("rstd", [P, TOK])
    ssq = place("ssq", [P, TOK])
    const = place("const", [P, 3, P])
    ident, mean_all, swap = (const[:, n, :] for n in range(3))
    const_r = place("const_r", [P, 3, P], F32R)
    mean_head_r, minus_upto_r, minus_ones_r = (const_r[:, n, :] for n in range(3))
    const_b = place("const_b", [P, 2, P], BF16)
    ident_b, far_b = const_b[:, 0, :], const_b[:, 1, :]
    gains = place("gains", [P, 7, DT])
    head_gain = place("head_gain", [P, 4])
    eps_col = place("eps_col", [P, 1])
    one_col = place("one_col", [P, 1])
    small = place("small", [P, 232])
    w_tok = small[:, 0:32]
    top8 = small[:, 32:48]
    row_sum, row_neg_max, row_inv = small[:, 96:160], small[:, 160:224], small[:, 224:232]
    region = fixed[0]

    at = [region]
    h_hi = place("h_hi", [P, FT, TOK], F32R, at)
    h_lo = place("h_lo", [P, FT, TOK], F32R, at)
    scratch = place("scratch", [P, 7, TOK], F32, at)
    at = [region]
    first_squares = place("first_squares", [P, DT, TOK], F32, at)
    to_round = place("to_round", [P, 3, P], F32, at)

    at = [region]
    qa = place("qa", [P, 4, TOK], F32, at)
    ka = place("ka", [P, 4, TOK], F32, at)
    bias = place("bias", [P, HEADS, TOK], F32, at)
    qb = place("qb", [P, 4, TOK], F32, at)
    kb = place("kb", [P, TOK], F32, at)
    va = place("va", [P, QT, 512], F32, at)
    vb = place("vb", [P, QT, P], F32, at)
    mask = [place(f"mask{i}", [P, P * (i + 1)], F32, at) for i in range(QT)]
    over_oa = [at[0]]
    o_hi = [place("oa_hi", [P, 4, TOK], F32R, at)]
    o_lo = [place("oa_lo", [P, 4, TOK], F32R, at)]
    over_ob = [at[0]]
    o_hi += [place("ob_hi", [P, 4, TOK], F32R, at)]
    o_lo += [place("ob_lo", [P, 4, TOK], F32R, at)]
    assert at[0] <= region + 2 * FT * TOK * 4 + TOK * 4
    qi = place("qi", [P, 4, TOK], F32, over_oa)
    ki = place("ki", [P, TOK], F32, over_oa)
    rope = place("rope", [P, 2, TOK], F32, over_ob)
    at = [region]
    gates = place("gates", [P, 2 * DT, TOK], F32, at)
    at = [region + 12 * TOK * 4]
    m_hi = place("m_hi", [P, DT, TOK], F32R, at)
    m_lo = place("m_lo", [P, DT, TOK], F32R, at)

    def gate(j):
        return gates[:, (j + 12) % 16, :]

    width = [TOK - P * j for j in range(QT)]
    col = [0, width[0], width[0] + width[1] + width[3], width[0] + width[1]]
    SBW = sum(width)
    at = [region]
    sb_q = [place(f"sb_q_{part}", [P, 2, TOK], F32R, at) for part in ("hi", "lo")]
    sb_k = [place(f"sb_k_{part}", [P, 2, TOK], F32R, at) for part in ("hi", "lo")]
    sb_v = [place(f"sb_v_{part}", [P, 2, QT, P], F32R, at) for part in ("hi", "lo")]
    so_hi = place("so_hi", [P, DT, TOK], F32R, at)
    so_lo = place("so_lo", [P, DT, TOK], F32R, at)
    sb_e = place("sb_e", [P, SBW], F32, at)
    sp = [place(f"sp_{part}", [P, SBW], F32R, at) for part in ("hi", "lo")]
    sb_w = [place(f"sb_w_{part}", [P, SBW], F32R, at) for part in ("hi", "lo")]
    qk_sq = [[place(f"q_sq_{part}", [P, TOK], F32R, at) for part in ("hi", "lo")]]
    assert at[0] <= region + 2 * FT * TOK * 4
    at = [region + 2 * FT * TOK * 4 + 2 * TOK * 4]
    qk_sq += [[place(f"k_sq_{part}", [P, TOK], F32R, at) for part in ("hi", "lo")]]

    PS = ctx.enter_context(nc.psum_tensor("ps", [P, 8, TOK], F32))
    ps_flat = PS[:, :, :].rearrange("p b n -> p (b n)")

    names = """hi_done lo_done unit_done consts_in to_round_in gains_in head_gains_in rope_in bias_in cols_ready
        x_updated x_normed sq_done ssq_zeroed ssq_done ms_done rms_done rstd_ready
        sq2_done ssq2_zeroed ssq2_done ms2_done r1_made m2_scaled rms2_done r2_made
        xn_hi_done xn_lo_done gate_scaled silu_done up_scaled h_made h_hi_done h_lo_done
        plain_made rope_scaled swap_done rope_sined rope_added
        wi_made ki_twice wt_turned wt_copied v_made v_turned v_copied
        idx_done relu_done idx_added score_ready top_found top_taken mask_ready bias_ready
        s_done s_biased p_made p_turned pt_copied pv_done inv_made o_normed o_turned o_hi_done
        o_lo_done gate_in gate_sig branch_gated merged m_hi_done m_lo_done
        qk_made qk_sq_done qk_sq_hi qk_sq_split qk_ms qk_ln qk_inv qk_normed qk_hi qk_split sv_made sv_turned sv_hi sv_split
        z_done abs_done e_done l_done sp_done sp_hi_done sp_split cum_done
        w_done w_hi_done w_split sb_pv so_hi_done so_lo_done stored""".split()
    S = {name: ctx.enter_context(nc.semaphore(name)) for name in names}
    raw_landed = [ctx.enter_context(nc.semaphore(f"raw_landed{s}")) for s in range(NSLOT)]
    x_landed = [ctx.enter_context(nc.semaphore(f"x_landed{k}")) for k in range(DT)]

    def evacuated_1(n):
        what, t = PROJ[n]
        if n in ROPE:
            return S["rope_scaled"], ROPE.index(n) + 1
        if n in VALUES:
            return S["v_made"], VALUES.index(n) + 1
        return S["plain_made"], 1 + t + 4 * (what == KA)

    def evacuated_between(n):
        if n < len(PROJ) - PROJ_ALONE:
            return evacuated_1(PROJ_ALONE + n)
        return S["gate_in"], n + PROJ_ALONE - len(PROJ) + 1

    def unit_between(n):
        return U_PROJ + PROJ_ALONE + n

    def evacuated_2(n):
        t, c = divmod(n, 3)
        return (S["sv_made"], t + 1) if c == 2 else (S["qk_made"], 2 * t + c + 1)

    block = ctx.enter_context(nc.Block())

    @block.sync
    def _(sp):
        def load(u, s):
            sp.dma_start(raw[s][:, :, :], weights[u]).then_inc(raw_landed[s], 16)

        def load_next(turn, s):
            sp.wait_ge(S["lo_done"], NSLOT * turn + (s + 1 - NSLOT))
            load(NSLOT * turn + s, s)

        load(0, 0)
        sp.dma_start(gains[:, :, :], gain_cols).then_inc(S["gains_in"], 16)
        for k in range(DT):
            sp.dma_start(X[:, k, :], x[:, k, :]).then_inc(x_landed[k], 16)
            if k == 5:
                load(1, 1)
        load(2, 2)
        sp.dma_start(const[:, :, :], consts[:, 0:3]).then_inc(S["consts_in"], 16)
        sp.dma_start(to_round[:, :, :], consts[:, 3:6]).then_inc(S["to_round_in"], 16)
        sp.dma_start(const_b[:, :, :], consts_b).then_inc(S["consts_in"], 16)
        load(3, 3)
        sp.dma_start(head_gain[:, 0:2], head_gains).then_inc(S["head_gains_in"], 16)
        with sp.Fori(1, UNITS // NSLOT) as it:
            for s in range(NSLOT):
                load_next(it, s)
        for s in range(UNITS % NSLOT):
            load_next(UNITS // NSLOT, s)
        for n in range(DT):
            sp.wait_ge(S["x_updated"], DT * FFN_RES[3] + n + 1)
            sp.dma_start(out[:, n, :], X[:, n, :]).then_inc(S["stored"], 16)
        sp.wait_ge(S["stored"], 16 * DT)

    @block.gpsimd
    def _(pool):
        def rest(turn, s):
            pool.wait_ge(S["hi_done"], NSLOT * turn + (s + 1))
            nc.gpsimd.tensor_tensor(w_lo[s][:, :, :], raw[s][:, :, :], w_hi[s][:, :, :].bitcast(F32),
                                    ALU.subtract).then_inc(S["lo_done"], 1)

        with pool.Fori(0, UNITS // NSLOT) as it:
            for s in range(NSLOT):
                rest(it, s)
        for s in range(UNITS % NSLOT):
            rest(UNITS // NSLOT, s)

    @block.tensor
    def _(pe):
        def unit(u, s, outs, tiles, before=None, start=True, stop=True, part=None):
            k0, k1 = part or (0, len(tiles))
            if k0 == 0:
                pe.wait_ge(S["lo_done"], u + 1)
            for k in range(k0, k1):
                hi, lo = tiles[k]
                if before:
                    before(k)
                opens = start and (k == 0 or outs[k] != outs[k - 1])
                ends = stop and (k == len(tiles) - 1 or outs[k] != outs[k + 1])
                to = PS[:, outs[k], :]
                pe.matmul(to, w_hi[s][:, k, :], hi, start=opens, stop=False)
                pe.matmul(to, w_hi[s][:, k, :], lo, start=False, stop=False)
                last = pe.matmul(to, w_lo[s][:, k, :], hi, start=False, stop=ends)
            if k1 == len(tiles):
                last.then_inc(S["unit_done"], 1)

        xn = [(xn_hi[:, k, :], xn_lo[:, k, :]) for k in range(DT)]

        def mean_square(stat):
            pe.wait_ge(S["ssq_done"], DT * (stat + 1))
            pe.matmul(PS[:, mean_bank(stat), :], mean_all, ssq[:, :], start=True, stop=True)\
              .then_inc(S["ms_done"], 1)

        def first_unit_waits(t, stat):
            def before(k):
                if k == DT - 1 and stat != S_START:
                    mean_square(stat)
                    if stat == S_FINAL:
                        pe.wait_ge(S["ssq2_done"], DT)
                        pe.matmul(PS[:, 5, :], mean_all, scratch[:, 0, :], start=True, stop=True)\
                          .then_inc(S["ms2_done"], 1)
                pe.wait_ge(S["xn_lo_done"], DT * t + k + 1)
            return before

        def ffn_up(n):
            def tile(F, j, before=None):
                u = FFN_BASE[n] + 2 * F
                for g in range(2):
                    unit(u + g, (FFN_BASE[n] + 2 * j + g) % NSLOT, [2 * j + g] * UK, xn, before if g == 0 else None)

            if n:
                pe.wait_ge(S["x_updated"], DT * FFN_RES[n])
            def first_mean(k):
                if k == 1:
                    pe.wait_ge(S["consts_in"], 32)
                    mean_square(S_START)

            tile(0, 0, first_unit_waits(FFN_INPUT[n], FFN_STAT[n]))
            tile(1, 1, first_mean if n == 0 else None)
            with pe.Fori(1, FT // 2) as it:
                for j in range(2):
                    pe.wait_ge(S["h_made"], 2 * it + (FT * n + j - 1))
                    tile(2 * it + j, j)

        def residual(u0, kinds, tiles, ready, freed, freed0):
            def body(it):
                for j in range(4):
                    pe.wait_ge(freed, 4 * it + (freed0 + j - 3))
                    for c, (k0, k1) in enumerate(kinds):
                        n_u = 4 * len(kinds)
                        at_unit = j * len(kinds) + c
                        unit(n_u * it + (u0 + at_unit), (u0 + at_unit) % NSLOT, [j] * (k1 - k0), tiles[k0:k1],
                             (lambda k, k0=k0: ready(k0 + k)) if j == 0 else None,
                             start=(c == 0), stop=(c == len(kinds) - 1))
            with pe.Fori(0, 2) as it:
                body(it)

        def ffn_down(n):
            def ready(k):
                if k == 0:
                    pe.wait_ge(S["h_lo_done"], FT * n + FT - 1)
                if k == FT - 1:
                    pe.wait_ge(S["h_lo_done"], FT * n + FT)

            pe.wait_ge(S["h_made"], FT * n + FT - 1)
            freed, freed0 = (S["x_updated"], DT * FFN_RES[n]) if n else (S["ssq_done"], DT * S_FFN1)
            residual(FFN_BASE[n] + UP_UNITS, DOWN,
                     [(h_hi[:, k, :], h_lo[:, k, :]) for k in range(FT)], ready, freed, freed0)

        def projection_1():
            pe.wait_ge(S["x_updated"], DT * (FFN_RES[0] + 1))
            for n in range(PROJ_ALONE):
                if n >= 4:
                    pe.wait_ge(*evacuated_1(n - 4))
                unit(U_PROJ + n, (U_PROJ + n) % NSLOT, [n % 4] * UK, xn,
                     first_unit_waits(T_FFN1, S_FFN1) if n == 0 else None)
                turn_1(n - 1)
                if n == 2:
                    pe.wait_ge(S["wi_made"], 1)
                    for i in range(QT):
                        last = pe.transpose(PS[:, 4, 8 * i:8 * i + 8],
                                            scratch[HD:HD + HEADS, 2, P * i:P * (i + 1)],
                                            ident[HD:HD + HEADS, HD:HD + HEADS])
                    last.then_inc(S["wt_turned"], 1)
                for m in index_steps(n):
                    i, h = INDEX[m]
                    if m == 0:
                        pe.wait_ge(S["rope_added"], 5)
                        pe.wait_ge(S["ki_twice"], 16)
                    if m == 1:
                        pe.wait_ge(S["rope_sined"], 5)
                    if m >= 2:
                        pe.wait_ge(S["relu_done"], m - 1)
                    r = HD * (h % 2)
                    pe.matmul(PS[:, 5 + m % 2, 0:P * (i + 1)], qi[r:r + HD, h // 2, P * i:P * (i + 1)],
                              ki[r:r + HD, 0:P * (i + 1)], start=True, stop=True).then_inc(S["idx_done"], 1)

        def turn_1(n):
            if n < 0:
                return
            if n in ROPE:
                k = ROPE.index(n)
                pe.wait_ge(S["rope_scaled"], k + 1)
                if k == 5:
                    pe.wait_ge(S["v_copied"], 4)
                elif k:
                    pe.wait_ge(S["rope_sined"], k)
                if k == 6:
                    pe.wait_ge(S["v_copied"], 5)
                pe.matmul(PS[:, 7, :], swap, scratch[:, 5, :], start=True, stop=True)\
                  .then_inc(S["swap_done"], 1)
            if n in VALUES:
                v = VALUES.index(n)
                pe.wait_ge(S["v_made"], v + 1)
                if v == 4:
                    pe.wait_ge(S["rope_sined"], 6)
                elif v:
                    pe.wait_ge(S["v_copied"], v)
                for i in range(QT):
                    last = pe.transpose(PS[:, 7, P * i:P * (i + 1)],
                                        scratch[:, VALUE_BUFFER[v], P * i:P * (i + 1)], ident)
                last.then_inc(S["v_turned"], 1)

        def between(m):
            for g in range(filled(m - 1), filled(m)):
                n, k = divmod(g, UK)
                u = unit_between(n)
                if k == 0 and n >= 2:
                    pe.wait_ge(*evacuated_between(n - 2))
                unit(u, u % NSLOT, [2 + n % 2] * UK, xn, part=(k, k + 1))

        def attention_1():
            pe.wait_ge(S["plain_made"], 8)
            pe.wait_ge(S["relu_done"], len(INDEX))
            for m in range(LAST_STEP + 1):
                if m < len(STEPS):
                    br, i, h = STEPS[m]
                    t, r = (h // 2, HD * (h % 2)) if br == 0 else (h % 4, HD * (h // 4))
                    q = (qa, qb)[br][r:r + HD, t, P * i:P * (i + 1)]
                    k = ka[r:r + HD, t, 0:P * (i + 1)] if br == 0 else kb[r:r + HD, 0:P * (i + 1)]
                    if br == 1 and i == 0 and h < 4:
                        pe.wait_ge(S["rope_added"], 7 + h)
                    if m >= 2:
                        pe.wait_ge(S["s_biased"], m - 1)
                    pe.matmul(PS[:, 4 + m % 2, 0:P * (i + 1)], q, k, start=True, stop=True)\
                      .then_inc(S["s_done"], 1)
                between(m)
                if m == 0:
                    turn_1(PROJ_ALONE - 1)
                if 1 <= m <= len(STEPS):
                    n = m - 1
                    br, i, h = STEPS[n]
                    pe.wait_ge(S["p_made"], n + 1)
                    if n >= 1:
                        pe.wait_ge(S["pt_copied"], n)
                    for j in range(i + 1):
                        last = pe.transpose(PS[:, 6, P * j:P * (j + 1)],
                                            scratch[:, 2 + n % 2, P * j:P * (j + 1)], ident)
                    last.then_inc(S["p_turned"], 1)
                if 2 <= m < len(STEPS) + 2:
                    n = m - 2
                    br, i, h = STEPS[n]
                    group = n // HEADS
                    pe.wait_ge(S["pt_copied"], n + 1)
                    if h == 0 and group >= 2:
                        pe.wait_ge(S["o_lo_done"], group - 1)
                    if n in (0, HALF):
                        pe.wait_ge(S["v_copied"], 5 if n else 4)
                    for j in range(i + 1):
                        v = va[:, j, HD * h:HD * (h + 1)] if br == 0 else vb[:, j, HD * (h // 4):HD * (h // 4 + 1)]
                        last = pe.matmul(PS[:, group % 2, HD * h:HD * (h + 1)],
                                         scratch[:, 4, P * j:P * (j + 1)], v,
                                         start=(j == 0), stop=(j == i))
                    last.then_inc(S["pv_done"], 1)
                if m % HEADS == 3 and m > HEADS:
                    g = m // HEADS - 1
                    pe.wait_ge(S["o_normed"], g + 1)
                    for c in range(4):
                        last = pe.transpose(PS[:, g % 2, P * c:P * (c + 1)],
                                            ssq[:, P * c:P * (c + 1)], ident)
                    last.then_inc(S["o_turned"], 1)
                if m - 2 in ENDS and ENDS.index(m - 2) < len(PROJ) - PROJ_ALONE:
                    turn_1(PROJ_ALONE + ENDS.index(m - 2))

        def merge():
            pe.wait_ge(S["o_lo_done"], GROUPS - 1)

            def last_group(k):
                if k == 4:
                    pe.wait_ge(S["o_lo_done"], GROUPS)

            o = [(o_hi[br][:, k, :], o_lo[br][:, k, :]) for br in range(2) for k in range(4)]
            for n in range(DT):
                b, u = 4 * (n % 2), U_GATE + 2 * DT + n
                if n >= 2:
                    pe.wait_ge(S["merged"], n - 1)
                unit(u, u % NSLOT, [b] * 4 + [b + 1] * 4, o, last_group if n == 0 else None)

        def mixer_out_1():
            pe.wait_ge(S["gate_in"], 2 * DT)
            pe.wait_ge(S["merged"], DT - 1)
            residual(U_OUT, [(0, DT)], [(m_hi[:, k, :], m_lo[:, k, :]) for k in range(DT)],
                     lambda k: pe.wait_ge(S["m_lo_done"], k + 1), S["x_updated"], DT * MIX_RES[0])

        def project(k0, k1):
            for g in range(k0, k1):
                n, k = divmod(g, UK)
                if k == 0 and n >= 2:
                    pe.wait_ge(*evacuated_2(n - 2))
                unit(U_QKV + n, (U_QKV + n) % NSLOT, [4 + n % 2] * UK, xn,
                     first_unit_waits(T_FFN3, S_FFN3) if n == 0 else None, part=(k, k + 1))

        def head_mean_square(t, c):
            pe.wait_ge(S["qk_sq_split"], 2 * t + c + 1)
            if t == 0 and c == 0:
                pe.wait_ge(S["rms_done"], S_FFN3 + 1)
            if t and c == 0:
                pe.wait_ge(S["sv_split"], t)
            if t and c == 1:
                pe.wait_ge(S["qk_ln"], 2 * t)
            pe.matmul(PS[:, 6 + c, :], mean_head_r, qk_sq[c][0][:, :], start=True, stop=False)
            pe.matmul(PS[:, 6 + c, :], mean_head_r, qk_sq[c][1][:, :], start=False, stop=True)\
              .then_inc(S["qk_ms"], 1)

        def turn_values(t):
            pe.wait_ge(S["sv_made"], t + 1)
            pe.wait_ge(S["qk_ln"], 2 * t + 1)
            for i in range(QT):
                last = pe.transpose(PS[:, 6, P * i:P * (i + 1)], scratch[:, 6, P * i:P * (i + 1)], ident)
            last.then_inc(S["sv_turned"], 1)

        def three(out, a, b, start):
            pe.matmul(out, a[0], b[0], start=start, stop=False, skip_group_check=True)
            pe.matmul(out, a[0], b[1], start=False, stop=False, skip_group_check=True)
            return pe.matmul(out, a[1], b[0], start=False, stop=True, skip_group_check=True)

        def stick_scores(h):
            r, b = HD * (h % 2), h // 2 % 2
            pe.wait_ge(S["qk_split"], 2 * (h // 2) + 2)
            if h:
                pe.wait_ge(S["w_done"], h)
            for j in range(QT):
                three(ps_flat[:, col[j]:col[j] + width[j]],
                      [k[r:r + HD, b, P * j:P * (j + 1)] for k in sb_k],
                      [q[r:r + HD, b, P * j:TOK] for q in sb_q], j < 3)
            for j in (0, 2):
                pe.matmul(ps_flat[:, col[j]:col[j] + P], ident_b, far_b,
                          start=False, stop=True, skip_group_check=True)
            apart = col[3] - col[1]
            two = ps_flat[:, col[1]:col[1] + 2 * apart].rearrange("p (b n) -> p b n", n=apart)[:, :, 0:P]
            pe.matmul(two, ident_b, far_b.unsqueeze(1).broadcast_to([P, 2, P]),
                      start=False, stop=True, skip_group_check=True).then_inc(S["z_done"], 1)

        def cumulate(h):
            pe.wait_ge(S["sp_split"], h + 1)
            for j in range(QT):
                for k in range(j, QT):
                    to = col[j] + P * (k - j)
                    for part in sp:
                        last = pe.matmul(ps_flat[:, to:to + width[k]], (minus_upto_r if k == j else minus_ones_r),
                                         part[:, col[k]:col[k] + width[k]],
                                         start=False, stop=True, skip_group_check=True)
            last.then_inc(S["cum_done"], 1)

        def weigh(h):
            pe.wait_ge(S["w_split"], h + 1)
            pe.wait_ge(S["sv_split"], h // 2 + 1)
            if h:
                pe.wait_ge(S["so_lo_done"], h)
            for j in range(QT):
                last = three(PS[:, 3, P * j:TOK], [v[:, h // 2 % 2, j, :] for v in sb_v],
                             [w[:, col[j]:col[j] + width[j]] for w in sb_w], j == 0)
            last.then_inc(S["sb_pv"], 1)

        so = [(so_hi[:, k, :], so_lo[:, k, :]) for k in range(DT)]

        def out_part(n, k0, k1):
            unit(U_SBO + n, (U_SBO + n) % NSLOT, [(n + 4) % 8] * DT, so,
                 lambda k: pe.wait_ge(S["so_lo_done"], 2 * k + 2), part=(k0, k1))

        def mixer_2():
            pairs = SB_HEADS // 2
            pe.wait_ge(S["x_updated"], DT * (FFN_RES[2] + 1))
            project(0, 2 * UK + 3)
            head_mean_square(0, 0)
            project(2 * UK + 3, 2 * UK + 5)
            head_mean_square(0, 1)
            project(2 * UK + 5, 3 * UK)
            for h in range(SB_HEADS):
                t, odd = divmod(h, 2)
                at = (3 * (t + 1)) * UK + 12 * odd
                stick_scores(h)
                if t + 1 < pairs:
                    if odd:
                        project(at, at + FILL_BEFORE)
                    else:
                        project(at, at + 2)
                        turn_values(t)
                        project(at + 2, at + FILL_BEFORE)
                else:
                    if not odd:
                        turn_values(t)
                    if h == SB_HEADS - 2:
                        pe.wait_ge(*evacuated_2(3 * pairs - 1))
                    if h == SB_HEADS - 1:
                        pe.wait_ge(S["sv_split"], pairs)
                    out_part(2 * odd, 0, pairs - 2)
                    out_part(2 * odd + 1, 0, 3)
                if h:
                    weigh(h - 1)
                if odd and t + 1 < pairs:
                    head_mean_square(t + 1, 1)
                cumulate(h)
                if t + 1 < pairs:
                    project(at + FILL_BEFORE, at + FILL_BEFORE + FILL_BEHIND)
                    if not odd:
                        head_mean_square(t + 1, 0)
                else:
                    out_part(2 * odd + 1, 3, pairs - 2)
            for n in range(2):
                out_part(n, pairs - 2, pairs - 1)
            weigh(SB_HEADS - 1)
            for n in range(2, 4):
                out_part(n, pairs - 2, pairs - 1)
            for n in range(4):
                out_part(n, pairs - 1, pairs)
            for n in range(4, DT):
                out_part(n, 0, DT)

        ffn_up(0)
        ffn_down(0)
        projection_1()
        attention_1()
        merge()
        mixer_out_1()
        ffn_up(1)
        ffn_down(1)
        ffn_up(2)
        ffn_down(2)
        mixer_2()
        ffn_up(3)
        ffn_down(3)

    @block.scalar
    def _(act):
        def copy(dst, src):
            return nc.scalar.activation(dst, src, ACT.Copy)

        def round_weights(u, s, turn):
            act.wait_ge(raw_landed[s], 16 * turn + 16)
            if not (isinstance(u, int) and u < NSLOT):
                act.wait_ge(S["unit_done"], u + (1 - NSLOT))
            copy(w_hi[s][:, :, :], raw[s][:, :, :]).then_inc(S["hi_done"], 1)

        def ahead(u):
            if u + AHEAD < UNITS:
                round_weights(u + AHEAD, (u + AHEAD) % NSLOT, (u + AHEAD) // NSLOT)

        def ahead_in_loop(it, per, u0, j):
            v = u0 + j + AHEAD
            round_weights(per * it + v, v % NSLOT, (per // NSLOT) * it + v // NSLOT)

        def root_mean_square(stat):
            act.wait_ge(S["ms_done"], stat + 1)
            nc.scalar.activation(scratch[:, 6, :], PS[:, mean_bank(stat), :], ACT.Sqrt, bias=eps_col[:, 0:1])\
              .then_inc(S["rms_done"], 1)
            if stat == S_FINAL:
                act.wait_ge(S["m2_scaled"], 1)
                nc.scalar.activation(scratch[:, 5, :], scratch[:, 4, :], ACT.Sqrt, bias=eps_col[:, 0:1])\
                  .then_inc(S["rms2_done"], 1)

        def first_square(k):
            nc.scalar.activation(first_squares[:, k, :], X[:, k, :], ACT.Square).then_inc(S["sq_done"], 1)

        def square(k, b, stat, n_before):
            if not isinstance(n_before, int) or n_before >= 2:
                act.wait_ge(S["ssq_done"], n_before + (DT * stat - 1))
            nc.scalar.activation(scratch[:, 4 + b, :], X[:, k, :], ACT.Square).then_inc(S["sq_done"], 1)
            if stat == S_FINAL:
                act.wait_ge(S["ssq2_done"], n_before)
                nc.scalar.activation(scratch[:, 1, :], X[:, k, :], ACT.Square,
                                     scale=gains[:, G_FINAL, bass.ds(k, 1)]).then_inc(S["sq2_done"], 1)

        def round_input(k, t):
            nc.scalar.activation(xn_hi[:, k, :], X[:, k, :], ACT.Copy, scale=gains[:, t, bass.ds(k, 1)])\
              .then_inc(S["xn_hi_done"], 1)

        def ffn_up(n):
            def tile(F, j, first=False):
                u = FFN_BASE[n] + 2 * F if isinstance(F, int) else None
                if first:
                    ahead(u)
                    if n == 0:
                        ahead(u + 1)
                    root_mean_square(FFN_STAT[n])
                    if n:
                        ahead(u + 1)
                elif u is not None:
                    ahead(u)
                    ahead(u + 1)
                f = FT * n + F if isinstance(F, int) else F + FT * n
                act.wait_ge(S["gate_scaled"], f + 1)
                nc.scalar.activation(scratch[:, j, :], scratch[:, j, :], ACT.Silu).then_inc(S["silu_done"], 1)
                act.wait_ge(S["h_made"], f + 1)
                copy(h_hi[:, F, :], scratch[:, 2 + j, :]).then_inc(S["h_hi_done"], 1)

            tile(0, 0, first=True)
            tile(1, 1)
            with act.Fori(1, FT // 2) as it:
                for j in range(2):
                    ahead_in_loop(it, 4, FFN_BASE[n], 2 * j)
                    ahead_in_loop(it, 4, FFN_BASE[n], 2 * j + 1)
                    tile(2 * it + j, j)

        def residual(u0, per, r, t, stat):
            with act.Fori(0, 2) as it:
                for j in range(4):
                    for c in range(per):
                        ahead_in_loop(it, 4 * per, u0, j * per + c)
                    tail(4 * it + j, j % 2, r, t, stat)

        def tail(k, b, r, t, stat):
            act.wait_ge(S["x_updated"], k + (DT * r + 1))
            square(k, b, stat, k)
            round_input(k, t)

        def projection_1():
            act.wait_ge(S["unit_done"], U_PROJ)
            act.dma_start(rope[:, :, :], ropes).then_inc(S["rope_in"], 16)
            runs = bass.AP(rel.tensor, 1, [[1, P], [rel.shape[1], HEADS], [1, TOK]])
            act.dma_start(bias[:, :, :], runs).then_inc(S["bias_in"], 16)
            for n in range(PROJ_ALONE):
                ahead(U_PROJ + n)
                if n == 0:
                    root_mean_square(S_FFN1)
                if n == 1:
                    act.wait_ge(S["rope_added"], 1)
                    act.dma_start(ki[HD:P, :], ki[0:HD, :]).then_inc(S["ki_twice"], 16)
                copy_values(n - 1)
                for m in index_steps(n):
                    i, h = INDEX[m]
                    act.wait_ge(S["idx_done"], m + 1)
                    if m >= 2:
                        act.wait_ge(S["idx_added"], m - 1)
                    nc.scalar.activation(scratch[:, (1, 4)[m % 2], 0:P * (i + 1)],
                                         PS[:, 5 + m % 2, 0:P * (i + 1)], ACT.Relu).then_inc(S["relu_done"], 1)

        def copy_values(n):
            if n not in VALUES:
                return
            v = VALUES.index(n)
            act.wait_ge(S["v_turned"], v + 1)
            dst = vb[:, :, :] if v == 4 else va[:, :, P * v:P * (v + 1)]
            copy(dst, PS[:, 7, :].rearrange("p (i n) -> p i n", i=QT)).then_inc(S["v_copied"], 1)

        def attention_1():
            for m in range(LAST_STEP + 1):
                if m in STARTS:
                    ahead(unit_between(STARTS.index(m)))
                if m < len(STEPS):
                    br, i, h = STEPS[m]
                    act.wait_ge(S["s_biased"], m + 1)
                    if m >= 2:
                        act.wait_ge(S["p_turned"], m - 1)
                    nc.scalar.activation(scratch[:, 2 + m % 2, 0:P * (i + 1)], scratch[:, 1, 0:P * (i + 1)],
                                         ACT.Exp, bias=row_neg_max[:, m:m + 1], scale=-1.0,
                                         accum_out=row_sum[:, m:m + 1]).then_inc(S["p_made"], 1)
                if m == 0:
                    copy_values(PROJ_ALONE - 1)
                if 1 <= m <= len(STEPS):
                    n = m - 1
                    br, i, h = STEPS[n]
                    act.wait_ge(S["p_turned"], n + 1)
                    if n >= 1:
                        act.wait_ge(S["pv_done"], n)
                    copy(scratch[:, 4, 0:P * (i + 1)], PS[:, 6, 0:P * (i + 1)])\
                        .then_inc(S["pt_copied"], 1)
                if m % HEADS == 3 and m > HEADS:
                    g = m // HEADS - 1
                    br, i = g // QT, g % QT
                    act.wait_ge(S["o_turned"], g + 1)
                    copy(o_hi[br][:, :, P * i:P * (i + 1)], PS[:, g % 2, :].rearrange("p (c n) -> p c n", c=4))\
                        .then_inc(S["o_hi_done"], 1)
                if m - 3 in ENDS and ENDS.index(m - 3) < len(PROJ) - PROJ_ALONE:
                    copy_values(PROJ_ALONE + ENDS.index(m - 3))

        def merge():
            def sigmoids(n):
                for j in (2 * n, 2 * n + 1):
                    act.wait_ge(S["gate_in"], j + 1)
                    nc.scalar.activation(gate(j), gate(j), ACT.Sigmoid).then_inc(S["gate_sig"], 1)

            sigmoids(0)
            for n in range(DT):
                ahead(U_GATE + 2 * DT + n)
                if n + 1 < DT:
                    sigmoids(n + 1)
                act.wait_ge(S["merged"], n + 1)
                copy(m_hi[:, n, :], scratch[:, 5 + n % 2, :]).then_inc(S["m_hi_done"], 1)

        def mixer_2():
            pairs = SB_HEADS // 2

            def head_square(t, c):
                act.wait_ge(S["qk_made"], 2 * t + c + 1)
                nc.scalar.activation(scratch[:, 4 + c, :], scratch[:, c, :], ACT.Square)\
                  .then_inc(S["qk_sq_done"], 1)
                if t:
                    act.wait_ge(S["qk_ms"], 2 * t + c - 1)
                act.wait_ge(S["qk_sq_done"], 2 * t + c + 1)
                copy(qk_sq[c][0][:, :], scratch[:, 4 + c, :]).then_inc(S["qk_sq_hi"], 1)

            def head_rms(t, c):
                act.wait_ge(S["qk_ms"], 2 * t + c + 1)
                nc.scalar.activation(scratch[:, 4 + c, :], PS[:, 6 + c, :], ACT.Ln, bias=eps_col[:, 0:1])\
                  .then_inc(S["qk_ln"], 1)
                act.wait_ge(S["qk_ln"], 2 * t + c + 1)
                nc.scalar.activation(scratch[:, 4 + c, :], scratch[:, 4 + c, :], ACT.Exp, scale=-0.5)\
                  .then_inc(S["qk_inv"], 1)

            def round_values(t):
                act.wait_ge(S["sv_turned"], t + 1)
                copy(sb_v[0][:, t % 2, :, :], PS[:, 6, :].rearrange("p (i n) -> p i n", i=QT))\
                    .then_inc(S["sv_hi"], 1)

            def round_out(h):
                r = HD * (h % 2)
                act.wait_ge(S["sb_pv"], h + 1)
                copy(so_hi[r:r + HD, h // 2, :], PS[r:r + HD, 3, :]).then_inc(S["so_hi_done"], 1)

            ahead(U_QKV)
            root_mean_square(S_FFN3)
            ahead(U_QKV + 1)
            act.preload_act_table_set("natural_log_exp_and_others")
            head_square(0, 0)
            head_square(0, 1)
            ahead(U_QKV + 2)
            head_rms(0, 0)
            head_rms(0, 1)
            for h in range(SB_HEADS):
                t, odd = divmod(h, 2)
                act.wait_ge(S["z_done"], h + 1)
                if h:
                    act.wait_ge(S["w_split"], h)
                nc.scalar.activation(sb_e[:, :], ps_flat[:, 0:SBW], ACT.Abs).then_inc(S["abs_done"], 1)
                act.wait_ge(S["abs_done"], h + 1)
                nc.scalar.activation(sb_e[:, :], sb_e[:, :], ACT.Exp, scale=-1.0).then_inc(S["e_done"], 1)
                act.wait_ge(S["e_done"], h + 1)
                nc.scalar.activation(sb_e[:, :], sb_e[:, :], ACT.Ln, bias=one_col[:, 0:1]).then_inc(S["l_done"], 1)
                if not odd:
                    round_values(t)
                    if t + 1 < pairs:
                        ahead(U_QKV + 3 * (t + 1))
                        ahead(U_QKV + 3 * (t + 1) + 1)
                        head_square(t + 1, 0)
                    else:
                        ahead(U_SBO)
                        ahead(U_SBO + 1)
                elif t + 1 < pairs:
                    head_square(t + 1, 1)
                    ahead(U_QKV + 3 * (t + 1) + 2)
                if h:
                    round_out(h - 1)
                if odd and t + 1 < pairs:
                    head_rms(t + 1, 1)
                act.wait_ge(S["cum_done"], h + 1)
                nc.scalar.activation(sb_e[:, :], ps_flat[:, 0:SBW], ACT.Exp).then_inc(S["w_done"], 1)
                if not odd and t + 1 < pairs:
                    head_rms(t + 1, 0)
            round_out(SB_HEADS - 1)
            for k in range(DT):
                if k + 2 < DT:
                    ahead(U_SBO + k + 2)
                tail(k, k % 2, MIX_RES[1], T_MIX2, S_MIX2)

        round_weights(0, 0, 0)
        for k in range(DT):
            act.wait_ge(x_landed[k], 16)
            if k == 0:
                act.wait_ge(S["gains_in"], 16)
            round_input(k, T_START)
            if k == 5:
                round_weights(1, 1, 0)
        for k in range(DT):
            first_square(k)
        act.wait_ge(S["cols_ready"], 2)
        ffn_up(0)
        residual(FFN_BASE[0] + UP_UNITS, len(DOWN), FFN_RES[0], T_FFN1, S_FFN1)
        projection_1()
        attention_1()
        merge()
        residual(U_OUT, 1, MIX_RES[0], T_MIX1, S_MIX1)
        ffn_up(1)
        residual(FFN_BASE[1] + UP_UNITS, len(DOWN), FFN_RES[1], T_FINAL, S_FINAL)
        ffn_up(2)
        residual(FFN_BASE[2] + UP_UNITS, len(DOWN), FFN_RES[2], T_FFN3, S_FFN3)
        mixer_2()
        ffn_up(3)
        for u in range(FFN_BASE[3] + UP_UNITS, UNITS):
            ahead(u)

    @block.vector
    def _(dve):
        def multiply(dst, p, q):
            return nc.vector.tensor_tensor(dst, p, q, ALU.mult)

        def scale_two(dst, p, scalar, q):
            return nc.vector.scalar_tensor_tensor(dst, p, scalar, q, ALU.mult, ALU.mult)

        def reciprocal_rms(stat):
            dve.wait_ge(S["rms_done"], stat + 1)
            nc.vector.reciprocal(rstd[:, :], scratch[:, 6, :]).then_inc(S["rstd_ready"], 1)
            dve.wait_ge(S["rstd_ready"], stat + 1)

        def zero_ssq(stat):
            nc.vector.memset(ssq[:, :], 0.0).then_inc(S["ssq_zeroed"], 1)
            dve.wait_ge(S["ssq_zeroed"], stat + 1)

        def tail(k, b, t, stat):
            add_square(k, scratch[:, 4 + b, :], stat)
            split_input(k, t)

        def add_square(k, squares, stat):
            dve.wait_ge(S["sq_done"], k + (DT * stat + 1))
            if not (isinstance(k, int) and k + stat == 0):
                dve.wait_ge(S["ssq_done"], k + DT * stat)
            nc.vector.tensor_tensor(ssq[:, :], ssq[:, :], squares, ALU.add).then_inc(S["ssq_done"], 1)
            if stat == S_FINAL:
                dve.wait_ge(S["sq2_done"], k + 1)
                nc.vector.tensor_tensor(scratch[:, 0, :], scratch[:, 0, :], scratch[:, 1, :], ALU.add)\
                    .then_inc(S["ssq2_done"], 1)

        def split_input(k, t):
            dve.wait_ge(S["xn_hi_done"], k + (DT * t + 1))
            nc.vector.scalar_tensor_tensor(xn_lo[:, k, :], X[:, k, :], gains[:, t, bass.ds(k, 1)],
                                           xn_hi[:, k, :].bitcast(F32), ALU.mult, ALU.subtract)\
                .then_inc(S["xn_lo_done"], 1)

        def ffn_up(n):
            def tile(F, j):
                u, f = 2 * F + FFN_BASE[n], F + FT * n
                dve.wait_ge(S["unit_done"], u + 1)
                multiply(scratch[:, j, :], PS[:, 2 * j, :], rstd[:, :]).then_inc(S["gate_scaled"], 1)
                dve.wait_ge(S["unit_done"], u + 2)
                multiply(scratch[:, 2 + j, :], PS[:, 2 * j + 1, :], rstd[:, :]).then_inc(S["up_scaled"], 1)
                dve.wait_ge(S["silu_done"], f + 1)
                dve.wait_ge(S["up_scaled"], f + 1)
                multiply(scratch[:, 2 + j, :], scratch[:, 2 + j, :], scratch[:, j, :]).then_inc(S["h_made"], 1)
                dve.wait_ge(S["h_hi_done"], f + 1)
                nc.vector.tensor_tensor(h_lo[:, F, :], scratch[:, 2 + j, :], h_hi[:, F, :].bitcast(F32),
                                        ALU.subtract).then_inc(S["h_lo_done"], 1)

            if n == 2:
                final_norms()
            else:
                reciprocal_rms(FFN_STAT[n])
            for j in range(2):
                tile(j, j)
            if n == 2:
                for k in range(DT):
                    scale_two(X[:, k, :], X[:, k, :], gains[:, G_FINAL, k:k + 1], scratch[:, 6, :])\
                        .then_inc(S["x_normed"], 1)
                dve.wait_ge(S["x_normed"], DT)
            with dve.Fori(1, FT // 2) as it:
                for j in range(2):
                    tile(2 * it + j, j)

        def final_norms():
            dve.wait_ge(S["rms_done"], S_FINAL + 1)
            nc.vector.reciprocal(scratch[:, 6, :], scratch[:, 6, :]).then_inc(S["r1_made"], 1)
            dve.wait_ge(S["r1_made"], 1)
            dve.wait_ge(S["ms2_done"], 1)
            multiply(scratch[:, 4, :], PS[:, 5, :], scratch[:, 6, :]).then_inc(S["r1_made"], 1)
            dve.wait_ge(S["r1_made"], 2)
            multiply(scratch[:, 4, :], scratch[:, 4, :], scratch[:, 6, :]).then_inc(S["m2_scaled"], 1)
            dve.wait_ge(S["rms2_done"], 1)
            nc.vector.reciprocal(scratch[:, 5, :], scratch[:, 5, :]).then_inc(S["r2_made"], 1)
            dve.wait_ge(S["r2_made"], 1)
            multiply(rstd[:, :], scratch[:, 5, :], scratch[:, 6, :]).then_inc(S["rstd_ready"], 1)
            dve.wait_ge(S["rstd_ready"], S_FINAL + 1)

        def residual(u0, per, factor, r, t, stat):
            if stat is not None:
                zero_ssq(stat)
            if stat == S_FINAL:
                nc.vector.memset(scratch[:, 0, :], 0.0).then_inc(S["ssq2_zeroed"], 1)
                dve.wait_ge(S["ssq2_zeroed"], 1)
            with dve.Fori(0, 2) as it:
                for j in range(4):
                    update(4 * it + j, j, 4 * per * it + (u0 + per * (j + 1)), factor, r, t, stat, j % 2)

        def update(k, bank, units, factor, r, t, stat, b):
            dve.wait_ge(S["unit_done"], units)
            nc.vector.scalar_tensor_tensor(X[:, k, :], PS[:, bank, :], factor, X[:, k, :],
                                           ALU.mult, ALU.add).then_inc(S["x_updated"], 1)
            if stat is not None:
                dve.wait_ge(S["x_updated"], k + (DT * r + 1))
                tail(k, b, t, stat)

        def evacuate(dst, bank, factor):
            if factor == 1.0:
                return multiply(dst, PS[:, bank, :], rstd[:, :])
            return scale_two(dst, PS[:, bank, :], factor, rstd[:, :])

        def evacuate_1(n):
            what, t = PROJ[n]
            bank = n % 4 if n < PROJ_ALONE else 2 + (n - PROJ_ALONE) % 2
            factor = HD ** -0.5 if what in QUERY else 1.0
            dve.wait_ge(S["unit_done"], U_PROJ + n + 1)
            if what == KI:
                r = slice(HD, HD + HEADS)
                scale_two(scratch[r, 2, :], PS[r, bank, :], HEADS ** -0.5, rstd[r, :]).then_inc(S["wi_made"], 1)
            if n in ROPE:
                k = ROPE.index(n)
                rows = rope_rows(n)
                evacuate(scratch[:, 5, :], bank, factor).then_inc(S["rope_scaled"], 1)
                dve.wait_ge(S["rope_scaled"], k + 1)
                multiply(rope_out(n), scratch[rows, 5, :], rope[rows, 0, :])
            elif n in VALUES:
                v = VALUES.index(n)
                if v >= 2:
                    dve.wait_ge(S["v_turned"], 4 if v == 4 else v - 1)
                evacuate(scratch[:, VALUE_BUFFER[v], :], bank, factor).then_inc(S["v_made"], 1)
            else:
                evacuate((qa if what == QA else ka)[:, t, :], bank, factor).then_inc(S["plain_made"], 1)

        def rope_rows(n):
            return slice(0, HD if PROJ[n][0] == KI else P)

        def rope_out(n):
            what, t = PROJ[n]
            return {KI: ki[0:HD, :], QI: qi[:, t, :], KB: kb[:, :], QB: qb[:, t, :]}[what]

        def finish_rope(n):
            if n not in ROPE:
                return
            k = ROPE.index(n)
            rows = rope_rows(n)
            dve.wait_ge(S["swap_done"], k + 1)
            multiply(scratch[rows, 6, :], PS[rows, 7, :], rope[rows, 1, :]).then_inc(S["rope_sined"], 1)
            dve.wait_ge(S["rope_sined"], k + 1)
            nc.vector.tensor_tensor(rope_out(n), rope_out(n), scratch[rows, 6, :], ALU.add)\
                .then_inc(S["rope_added"], 1)

        def projection_1():
            reciprocal_rms(S_FFN1)
            nc.vector.memset(mask[0][:, :], 0.0).then_inc(S["mask_ready"], 1)
            dve.wait_ge(S["bias_in"], 16)
            nc.vector.memset(bias[0:CHUNK, :, 0:CHUNK], FAR).then_inc(S["bias_ready"], 1)
            dve.wait_ge(S["mask_ready"], 1)
            nc.vector.memset(mask[0][0:CHUNK, CHUNK:P], FAR).then_inc(S["mask_ready"], 1)
            dve.wait_ge(S["rope_in"], 16)
            for n in range(PROJ_ALONE):
                if n - 1 in ROPE and n in ROPE:
                    finish_rope(n - 1)
                    evacuate_1(n)
                else:
                    evacuate_1(n)
                    finish_rope(n - 1)
                if n == 2:
                    dve.wait_ge(S["wt_turned"], 1)
                    nc.vector.tensor_copy(w_tok, PS[:, 4, 0:32]).then_inc(S["wt_copied"], 1)
                for m in index_steps(n):
                    add_index(m)
                if TOP_FROM <= n < PROJ_ALONE - 1:
                    for k in range(TOP_EACH * (n - TOP_FROM), TOP_EACH * (n - TOP_FROM + 1)):
                        select(k)

        def add_index(m):
            i, h = INDEX[m]
            W = P * (i + 1)
            relu = scratch[:, (1, 4)[m % 2], 0:W]
            weight = w_tok[:, 8 * i + h:8 * i + h + 1]
            dve.wait_ge(S["relu_done"], m + 1)
            if m == 0:
                dve.wait_ge(S["wt_copied"], 1)
            if h == 0:
                nc.vector.tensor_scalar(mask[i][:, :], relu, weight, None, ALU.mult).then_inc(S["idx_added"], 1)
            else:
                dve.wait_ge(S["idx_added"], m)
                nc.vector.scalar_tensor_tensor(mask[i][:, :], relu, weight, mask[i][:, :],
                                               ALU.mult, ALU.add).then_inc(S["idx_added"], 1)
            if h == HEADS - 1:
                dve.wait_ge(S["idx_added"], m + 1)
                nc.vector.memset(mask[i][0:CHUNK, W - CHUNK:W], OUTSIDE).then_inc(S["score_ready"], 1)

        def select(k):
            i, eight = 1 + k // ROUNDS, top8[:, 8 * (k % 2):8 * (k % 2) + 8]
            if k % ROUNDS == 0:
                dve.wait_ge(S["score_ready"], i)
            if k:
                dve.wait_ge(S["top_taken"], k)
            nc.vector.max(eight, mask[i][:, :]).then_inc(S["top_found"], 1)
            dve.wait_ge(S["top_found"], k + 1)
            nc.vector.match_replace(mask[i][:, :], eight, mask[i][:, :], TAKEN).then_inc(S["top_taken"], 1)
            if k % ROUNDS == ROUNDS - 1:
                dve.wait_ge(S["top_taken"], k + 1)
                nc.vector.tensor_scalar(mask[i][:, :], mask[i][:, :], TAKEN_BELOW, FAR, ALU.is_gt, ALU.mult)\
                    .then_inc(S["mask_ready"], 1)

        def attention_1():
            taken = TOP_EACH * (PROJ_ALONE - 1 - TOP_FROM)
            for m in range(LAST_STEP + 2):
                if m < len(STEPS):
                    br, i, h = STEPS[m]
                    W = P * (i + 1)
                    dve.wait_ge(S["s_done"], m + 1)
                    if m == 0:
                        dve.wait_ge(S["bias_ready"], 1)
                    if br == 1 and h == 0:
                        dve.wait_ge(S["mask_ready"], 2 + i)
                    if m >= 1:
                        dve.wait_ge(S["p_made"], m)
                    add = bias[:, h, W - 1::-1] if br == 0 else mask[i][:, :]
                    nc.vector.tensor_tensor_reduce(scratch[:, 1, 0:W], PS[:, 4 + m % 2, 0:W], add,
                                                   -1.0, -FAR, ALU.add, ALU.min,
                                                   row_neg_max[:, m:m + 1]).then_inc(S["s_biased"], 1)
                if m - 1 in ENDS:
                    n = ENDS.index(m - 1)
                    if n < len(PROJ) - PROJ_ALONE:
                        evacuate_1(PROJ_ALONE + n)
                    else:
                        j = n + PROJ_ALONE - len(PROJ)
                        dve.wait_ge(S["unit_done"], unit_between(n) + 1)
                        evacuate(gate(j), 2 + n % 2, 1.0).then_inc(S["gate_in"], 1)
                if m - 3 in ENDS and ENDS.index(m - 3) < len(PROJ) - PROJ_ALONE:
                    finish_rope(PROJ_ALONE + ENDS.index(m - 3))
                if m % HEADS == 1 and m > HEADS:
                    g = m // HEADS - 1
                    dve.wait_ge(S["p_made"], HEADS * (g + 1))
                    nc.vector.reciprocal(row_inv, row_sum[:, HEADS * g:HEADS * (g + 1)]).then_inc(S["inv_made"], 1)
                    dve.wait_ge(S["inv_made"], g + 1)
                    dve.wait_ge(S["pv_done"], HEADS * (g + 1))
                    if g:
                        dve.wait_ge(S["o_turned"], g)
                    multiply(ssq[:, :].rearrange("p (h d) -> p h d", h=HEADS),
                             PS[:, g % 2, :].rearrange("p (h d) -> p h d", h=HEADS),
                             row_inv.unsqueeze(2).broadcast_to([P, HEADS, HD])).then_inc(S["o_normed"], 1)
                if m % HEADS == 4 and m > HEADS:
                    g = m // HEADS - 1
                    br, i = g // QT, g % QT
                    dve.wait_ge(S["o_hi_done"], g + 1)
                    nc.vector.tensor_tensor(o_lo[br][:, :, P * i:P * (i + 1)],
                                            PS[:, g % 2, :].rearrange("p (c n) -> p c n", c=4),
                                            o_hi[br][:, :, P * i:P * (i + 1)].bitcast(F32), ALU.subtract)\
                        .then_inc(S["o_lo_done"], 1)
                if taken < ROUNDS * (QT - 1):
                    select(taken)
                    taken += 1

        def merge():
            for n in range(DT):
                b = 4 * (n % 2)
                dve.wait_ge(S["unit_done"], U_GATE + 2 * DT + n + 1)
                for g in range(2):
                    dve.wait_ge(S["gate_sig"], 2 * n + g + 1)
                    multiply(scratch[:, 3 + g, :], PS[:, b + g, :], gate(2 * n + g)).then_inc(S["branch_gated"], 1)
                dve.wait_ge(S["branch_gated"], 2 * n + 2)
                nc.vector.tensor_tensor(scratch[:, 5 + n % 2, :], scratch[:, 3, :], scratch[:, 4, :], ALU.add)\
                    .then_inc(S["merged"], 1)
                dve.wait_ge(S["m_hi_done"], n + 1)
                nc.vector.tensor_tensor(m_lo[:, n, :], scratch[:, 5 + n % 2, :], m_hi[:, n, :].bitcast(F32),
                                        ALU.subtract).then_inc(S["m_lo_done"], 1)

        def mixer_2():
            pairs = SB_HEADS // 2

            def make(t, c):
                n = 3 * t + c
                dve.wait_ge(S["unit_done"], U_QKV + n + 1)
                if c == 2:
                    if t:
                        dve.wait_ge(S["sv_turned"], t)
                    evacuate(scratch[:, 6, :], 4 + n % 2, 1.0).then_inc(S["sv_made"], 1)
                else:
                    evacuate(scratch[:, c, :], 4 + n % 2, 1.0).then_inc(S["qk_made"], 1)

            def split_squares(t, c):
                dve.wait_ge(S["qk_sq_hi"], 2 * t + c + 1)
                nc.vector.tensor_tensor(qk_sq[c][1][:, :], scratch[:, 4 + c, :], qk_sq[c][0][:, :].bitcast(F32),
                                        ALU.subtract).then_inc(S["qk_sq_split"], 1)

            def head_norm(t, c):
                dve.wait_ge(S["qk_inv"], 2 * t + c + 1)
                hi, lo = (part[:, t % 2, :] for part in (sb_q, sb_k)[c])
                full = scratch[:, c, :]
                scale_two(full, full, head_gain[:, 2 + c:3 + c], scratch[:, 4 + c, :])\
                    .then_inc(S["qk_normed"], 1)
                dve.wait_ge(S["qk_normed"], 2 * t + c + 1)
                nc.vector.tensor_copy(hi, full).then_inc(S["qk_hi"], 1)
                dve.wait_ge(S["qk_hi"], 2 * t + c + 1)
                nc.vector.tensor_tensor(lo, full, hi.bitcast(F32), ALU.subtract).then_inc(S["qk_split"], 1)

            def split_values(t):
                dve.wait_ge(S["sv_hi"], t + 1)
                hi, lo = (part[:, t % 2, :, :] for part in sb_v)
                nc.vector.tensor_tensor(lo, PS[:, 6, :].rearrange("p (i n) -> p i n", i=QT), hi.bitcast(F32),
                                        ALU.subtract).then_inc(S["sv_split"], 1)

            def split_out(h):
                r = HD * (h % 2)
                dve.wait_ge(S["so_hi_done"], h + 1)
                nc.vector.tensor_tensor(so_lo[r:r + HD, h // 2, :], PS[r:r + HD, 3, :],
                                        so_hi[r:r + HD, h // 2, :].bitcast(F32), ALU.subtract)\
                    .then_inc(S["so_lo_done"], 1)

            reciprocal_rms(S_FFN3)
            dve.wait_ge(S["cols_ready"], 3)
            make(0, 0)
            make(0, 1)
            split_squares(0, 0)
            split_squares(0, 1)
            head_norm(0, 0)
            head_norm(0, 1)
            make(0, 2)
            zero_ssq(S_MIX2)
            for h in range(SB_HEADS):
                t, odd = divmod(h, 2)
                if odd and t + 1 < pairs:
                    make(t + 1, 1)
                dve.wait_ge(S["l_done"], h + 1)
                nc.vector.scalar_tensor_tensor(sb_e[:, :], ps_flat[:, 0:SBW], 0.0, sb_e[:, :], ALU.max, ALU.add)\
                    .then_inc(S["sp_done"], 1)
                if odd and t + 1 < pairs:
                    split_squares(t + 1, 1)
                dve.wait_ge(S["sp_done"], h + 1)
                if h:
                    dve.wait_ge(S["cum_done"], h)
                nc.vector.tensor_copy(sp[0][:, :], sb_e[:, :]).then_inc(S["sp_hi_done"], 1)
                dve.wait_ge(S["sp_hi_done"], h + 1)
                nc.vector.tensor_tensor(sp[1][:, :], sb_e[:, :], sp[0][:, :].bitcast(F32), ALU.subtract)\
                    .then_inc(S["sp_split"], 1)
                if not odd:
                    split_values(t)
                if not odd and t + 1 < pairs:
                    make(t + 1, 0)
                    split_squares(t + 1, 0)
                if h:
                    split_out(h - 1)
                if odd and t + 1 < pairs:
                    head_norm(t + 1, 1)
                dve.wait_ge(S["w_done"], h + 1)
                if h:
                    dve.wait_ge(S["sb_pv"], h)
                nc.vector.tensor_copy(sb_w[0][:, :], sb_e[:, :]).then_inc(S["w_hi_done"], 1)
                dve.wait_ge(S["w_hi_done"], h + 1)
                nc.vector.tensor_tensor(sb_w[1][:, :], sb_e[:, :], sb_w[0][:, :].bitcast(F32), ALU.subtract)\
                    .then_inc(S["w_split"], 1)
                if t + 1 < pairs:
                    if odd:
                        make(t + 1, 2)
                    else:
                        head_norm(t + 1, 0)
            split_out(SB_HEADS - 1)
            for k in range(DT):
                update(k, (k + 4) % 8, U_SBO + k + 1, 1.0, MIX_RES[1], T_MIX2, S_MIX2, k % 2)

        nc.vector.memset(eps_col[:, :], EPS).then_inc(S["cols_ready"], 1)
        nc.vector.memset(one_col[:, :], 1.0).then_inc(S["cols_ready"], 1)
        zero_ssq(S_START)
        dve.wait_ge(S["gains_in"], 16)
        for k in range(DT):
            split_input(k, T_START)
        for k in range(DT):
            add_square(k, first_squares[:, k, :], S_START)
        dve.wait_ge(S["to_round_in"], 16)
        nc.vector.tensor_copy(const_r[:, :, :], to_round[:, :, :])
        dve.wait_ge(S["head_gains_in"], 16)
        nc.vector.tensor_scalar(head_gain[:, 2:3], head_gain[:, 0:1], HD ** -0.5, None, ALU.mult)
        multiply(gains[:, T_FINAL, :], gains[:, T_FINAL, :], gains[:, G_FINAL, :])
        nc.vector.tensor_copy(head_gain[:, 3:4], head_gain[:, 1:2]).then_inc(S["cols_ready"], 1)
        ffn_up(0)
        residual(FFN_BASE[0] + UP_UNITS, len(DOWN), 0.5, FFN_RES[0], T_FFN1, S_FFN1)
        projection_1()
        attention_1()
        merge()
        residual(U_OUT, 1, 1.0, MIX_RES[0], T_MIX1, S_MIX1)
        ffn_up(1)
        residual(FFN_BASE[1] + UP_UNITS, len(DOWN), 0.5, FFN_RES[1], T_FINAL, S_FINAL)
        ffn_up(2)
        residual(FFN_BASE[2] + UP_UNITS, len(DOWN), 0.5, FFN_RES[2], T_FFN3, S_FFN3)
        mixer_2()
        ffn_up(3)
        residual(FFN_BASE[3] + UP_UNITS, len(DOWN), 0.5, FFN_RES[3], None, None)


def mean_bank(stat):
    return 7 if stat == S_FFN3 else 4


def index_steps(n):
    first = INDEX_EACH * (n - INDEX_FROM)
    return range(max(first, 0), max(min(first + INDEX_EACH, len(INDEX)), 0))


def _units(w, width=P):
    k, n = w.shape
    return w.reshape(k // P, P, n // P, P).transpose(2, 1, 0, 3)


def _ffn_units(w_in, w_out):
    up = _units(w_in).reshape(2, FT, P, UK, P).transpose(1, 0, 2, 3, 4).reshape(UP_UNITS, P, UK, P)
    down = np.pad(_units(w_out), ((0, 0), (0, 0), (0, len(DOWN) * UK - FT), (0, 0)))
    down = down.reshape(DT, P, len(DOWN), UK, P).transpose(0, 2, 1, 3, 4).reshape(DOWN_UNITS, P, UK, P)
    return [up, down]


def _mixer_units(w_in, w_a, w_b, w_out):
    width = HEADS * HD
    cut = np.cumsum([width, width, width, width, 2 * HD, 2 * HD, width, HD, HEADS, D])
    qa, ka, va, qb, kb, vb, qi, ki, wi, ga, gb = np.split(w_in, cut, axis=1)
    qb = qb.reshape(D, 2, 4, HD).transpose(0, 2, 1, 3).reshape(D, width)
    ki = np.pad(np.concatenate([ki, wi], axis=1), ((0, 0), (0, P - HD - HEADS)))
    proj = [_units(np.ascontiguousarray(w)) for w in (ki, qi, qa, ka, va, kb, vb, qb)]
    both = np.concatenate([_units(w_a), _units(w_b)], axis=2)
    gate = np.stack([_units(np.ascontiguousarray(ga)), _units(np.ascontiguousarray(gb))], axis=1)
    return proj + [gate.reshape(2 * DT, P, UK, P), both, _units(w_out)]


def _constants():
    rows, cols = np.arange(P)[:, None], np.arange(P)[None, :]
    head = (rows // HD == cols // HD)
    rot = HD // 4
    d = np.arange(P) % HD
    partner = np.where(d < rot // 2, np.arange(P) + rot // 2, np.arange(P) - rot // 2)
    swap = (rows == partner[None, :]) & (d < rot)[None, :]
    upto = rows >= cols
    consts = np.stack([rows == cols, np.full((P, P), 1.0 / D), swap, head / HD, -1.0 * upto,
                       np.full((P, P), -1.0)], axis=1).astype(np.float32)
    freq = np.power(np.float32(500000.0), -np.arange(0, rot, 2, dtype=np.float32) / np.float32(rot))
    ang = np.arange(TOK, dtype=np.float32)[None, :] * freq.astype(np.float32)[:, None]
    cos, sin = np.ones((P, TOK), np.float32), np.zeros((P, TOK), np.float32)
    for p in range(P):
        if d[p] < rot:
            cos[p] = np.cos(ang[d[p] % (rot // 2)])
            sin[p] = np.sin(ang[d[p] % (rot // 2)]) * (-1.0 if d[p] < rot // 2 else 1.0)
    return consts, np.stack([rows == cols, FAR * upto], axis=1), np.stack([cos, sin], axis=1)


def kernel(**inputs):
    import ml_dtypes
    import concourse.bacc as bacc
    from concourse.bass_utils import run_bass_kernel_spmd

    i = {name: np.asarray(value) for name, value in inputs.items()}
    streams = _ffn_units(i["ffn1_w_in"][0], i["ffn1_w_out"][0])
    streams += _mixer_units(i["w_in"][0], i["w_branch_a"][0], i["w_branch_b"][0], i["w_out"][0])
    streams += _ffn_units(i["ffn2_w_in"][0], i["ffn2_w_out"][0])
    streams += _ffn_units(i["l0_ff1_w_in_2"], i["l0_ff1_w_out_2"])
    qkv = _units(i["l0_sb_w_qkv_2"]).reshape(3, DT, P, UK, P).transpose(1, 0, 2, 3, 4)
    streams += [qkv.reshape(QKV_UNITS, P, UK, P), _units(i["l0_sb_w_o_2"])]
    streams += _ffn_units(i["l0_ff2_w_in_2"], i["l0_ff2_w_out_2"])
    gain = np.stack([i["n1_g"][0], i["n2_g"][0], i["n3_g"][0], i["l0_ff1_norm_2"], i["l0_mix_norm_2"],
                     i["l0_ff2_norm_2"], i["nf_g"]])
    rel = i["rel_bias"][0]
    rel = np.pad(rel, ((0, 0), (0, TOK + P - rel.shape[1])), mode="edge")
    consts, consts_b, ropes = _constants()
    q_gain, k_gain = i["l0_sb_q_norm_2"], i["l0_sb_k_norm_2"]
    arrays = {
        "weights": np.concatenate(streams, axis=0),
        "consts": consts,
        "consts_b": consts_b.astype(ml_dtypes.bfloat16),
        "ropes": ropes,
        "rel": np.ascontiguousarray(rel),
        "gain_cols": np.ascontiguousarray(gain.reshape(7, DT, P).transpose(2, 0, 1)),
        "head_gains": np.stack([np.concatenate([q_gain, q_gain]), np.concatenate([k_gain, k_gain])], axis=1),
        "x_t": np.ascontiguousarray(i["x"][0].T.reshape(DT, P, TOK).transpose(1, 0, 2)),
    }
    nc = bacc.Bacc("TRN2", target_bir_lowering=False, num_devices=1)
    args = [nc.dram_tensor(name, v.shape, mybir.dt.from_np(v.dtype), kind="ExternalInput").ap()
            for name, v in arrays.items()]
    args.append(nc.dram_tensor("out_t", (P, DT, TOK), F32, kind="ExternalOutput").ap())
    program(nc, *args)
    r = run_bass_kernel_spmd(nc, [arrays], core_ids=[0])
    got = np.asarray(r.results[0]["out_t"])
    return np.ascontiguousarray(got.transpose(2, 1, 0).reshape(1, TOK, D))
```
